# Optimizing a Trainium2 kernel written in Bass

```python
import math
import jax, jax.numpy as jnp
from jax import lax
import numpy as np

D_MODEL = 1024
BATCH = 1
SEQ = 256
DEPTH = 1

N_MIXERS = 2
RMS_EPS = 1e-6
GN_EPS = 1e-6
NEG_INF = -1e30

NSA_HEADS = 16
NSA_HEAD_DIM = 64
NSA_KV_GROUPS = 4
NSA_Q_PER_GROUP = NSA_HEADS // NSA_KV_GROUPS
NSA_WIDTH = NSA_HEADS * NSA_HEAD_DIM
NSA_KV_WIDTH = NSA_KV_GROUPS * NSA_HEAD_DIM
CMP_BLOCK = 32
CMP_STRIDE = 16
CMP_HIDDEN = 256
SLC_BLOCK = 64
SLC_TOPN = 16
SLC_Q_BLOCK = 32
WIN_SIZE = 512
WIN_Q_BLOCK = 128
FORCED_SCORE = 1e3
NSA_PROJ = NSA_WIDTH + 6 * NSA_KV_WIDTH + 3 * NSA_HEADS + 3 * NSA_WIDTH

REL_BUCKETS = 32
REL_MAX_DIST = 128

RET_HEADS = 4
RET_QK_DIM = 256
RET_V_DIM = 512
RET_QK_WIDTH = RET_HEADS * RET_QK_DIM
RET_WIDTH = RET_HEADS * RET_V_DIM
RET_CHUNK = 128
ROPE_BASE = 10000.0
RET_PROJ = 2 * RET_QK_WIDTH + 2 * RET_WIDTH


def rms_norm(x, gain):
    xf = x.astype(jnp.float32)
    y = xf * lax.rsqrt(jnp.mean(xf * xf, axis=-1, keepdims=True) + RMS_EPS)
    return (y * gain.astype(jnp.float32)).astype(x.dtype)

def split_cols(a, sizes):
    return jnp.split(a, list(np.cumsum(sizes)[:-1]), axis=-1)

def masked_softmax(logits, mask):
    p = jax.nn.softmax(jnp.where(mask, logits, NEG_INF), axis=-1)
    return jnp.where(mask, p, 0.0)

def t5_bucket(dist):
    n = jnp.maximum(dist, 0)
    max_exact = REL_BUCKETS // 2
    nf = jnp.maximum(n, 1).astype(jnp.float32)
    large = max_exact + (jnp.log(nf / max_exact) / math.log(REL_MAX_DIST / max_exact)
                         * (REL_BUCKETS - max_exact)).astype(jnp.int32)
    large = jnp.minimum(large, REL_BUCKETS - 1)
    return jnp.where(n < max_exact, n, large)

def compress_kv(kv, pos, w1, w2):
    B, S, G, dh = kv.shape
    n_cmp = (S - CMP_BLOCK) // CMP_STRIDE + 1
    idx = jnp.arange(n_cmp)[:, None] * CMP_STRIDE + jnp.arange(CMP_BLOCK)[None, :]
    blocks = kv[:, idx] + pos[None, None, :, None, :].astype(kv.dtype)
    flat = blocks.transpose(0, 1, 3, 2, 4).reshape(B, n_cmp, G, CMP_BLOCK * dh)
    return jax.nn.silu(flat @ w1) @ w2

def nsa_compressed(q, kc, vc, table):
    B, S, H, dh = q.shape
    n_cmp = kc.shape[1]
    qg = q.reshape(B, S, NSA_KV_GROUPS, NSA_Q_PER_GROUP, dh)
    logits = jnp.einsum('bsgrd,bcgd->bgrsc', qg, kc).astype(jnp.float32) * (dh ** -0.5)
    t = jnp.arange(S)
    end = jnp.arange(n_cmp) * CMP_STRIDE + CMP_BLOCK - 1
    dist = t[:, None] - end[None, :]
    bias = table[t5_bucket(dist)].astype(jnp.float32)
    bias = bias.reshape(S, n_cmp, NSA_KV_GROUPS, NSA_Q_PER_GROUP).transpose(2, 3, 0, 1)
    p = masked_softmax(logits + bias, dist >= 0)
    o = jnp.einsum('bgrsc,bcgd->bsgrd', p.astype(vc.dtype), vc).reshape(B, S, H, dh)
    return o, p

def select_blocks(p_cmp, S):
    n_cmp = p_cmp.shape[-1]
    n_sel = S // SLC_BLOCK
    cs = jnp.arange(n_cmp) * CMP_STRIDE
    j = jnp.arange(n_sel)
    overlap = ((cs[:, None] < (j[None, :] + 1) * SLC_BLOCK)
               & (cs[:, None] + CMP_BLOCK > j[None, :] * SLC_BLOCK)).astype(jnp.float32)
    imp = jnp.einsum('bgrsc,cj->bgsj', p_cmp, overlap)
    t = jnp.arange(S)
    cur = t // SLC_BLOCK
    valid = j[None, :] * SLC_BLOCK <= t[:, None]
    forced = (j[None, :] == 0) | (j[None, :] == cur[:, None]) | (j[None, :] == cur[:, None] - 1)
    score = jnp.where(valid, imp + jnp.where(forced, FORCED_SCORE, 0.0), NEG_INF)
    _, sel = lax.top_k(score, min(SLC_TOPN, n_sel))
    return sel

def nsa_selected(q, k, v, sel, table):
    B, S, H, dh = q.shape
    G, R = NSA_KV_GROUPS, NSA_Q_PER_GROUP
    n_sel = S // SLC_BLOCK
    n_top = sel.shape[-1]
    n_keys = n_top * SLC_BLOCK
    kb = k.reshape(B, n_sel, SLC_BLOCK, G, dh).transpose(0, 3, 1, 2, 4)
    vb = v.reshape(B, n_sel, SLC_BLOCK, G, dh).transpose(0, 3, 1, 2, 4)
    nq = S // SLC_Q_BLOCK
    q_blk = q.reshape(B, nq, SLC_Q_BLOCK, G, R, dh).transpose(1, 0, 2, 3, 4, 5)
    sel_blk = sel.reshape(B, G, nq, SLC_Q_BLOCK, n_top).transpose(2, 0, 1, 3, 4)
    bi = jnp.arange(B)[:, None, None, None]
    gi = jnp.arange(G)[None, :, None, None]
    tbl = table.reshape(REL_BUCKETS, G, R)

    def one(args):
        qb, sb, blk = args
        t = blk * SLC_Q_BLOCK + jnp.arange(SLC_Q_BLOCK)
        kg = kb[bi, gi, sb].reshape(B, G, SLC_Q_BLOCK, n_keys, dh)
        vg = vb[bi, gi, sb].reshape(B, G, SLC_Q_BLOCK, n_keys, dh)
        pos = (sb[..., None] * SLC_BLOCK + jnp.arange(SLC_BLOCK)).reshape(B, G, SLC_Q_BLOCK, n_keys)
        dist = t[None, None, :, None] - pos
        bias = tbl[t5_bucket(dist), gi].astype(jnp.float32).transpose(0, 1, 4, 2, 3)
        logits = jnp.einsum('bqgrd,bgqkd->bgrqk', qb, kg).astype(jnp.float32) * (dh ** -0.5)
        p = masked_softmax(logits + bias, (dist >= 0)[:, :, None])
        return jnp.einsum('bgrqk,bgqkd->bqgrd', p.astype(vg.dtype), vg)

    out = lax.map(one, (q_blk, sel_blk, jnp.arange(nq)))
    return out.transpose(1, 0, 2, 3, 4, 5).reshape(B, S, H, dh)

def nsa_window(q, k, v, table):
    B, S, H, dh = q.shape
    G, R = NSA_KV_GROUPS, NSA_Q_PER_GROUP
    nq = S // WIN_Q_BLOCK
    span = WIN_SIZE + WIN_Q_BLOCK
    kp = jnp.pad(k, ((0, 0), (WIN_SIZE, 0), (0, 0), (0, 0)))
    vp = jnp.pad(v, ((0, 0), (WIN_SIZE, 0), (0, 0), (0, 0)))
    q_blk = q.reshape(B, nq, WIN_Q_BLOCK, G, R, dh).transpose(1, 0, 2, 3, 4, 5)

    def one(args):
        qb, blk = args
        start = blk * WIN_Q_BLOCK
        kw = lax.dynamic_slice_in_dim(kp, start, span, axis=1)
        vw = lax.dynamic_slice_in_dim(vp, start, span, axis=1)
        t = start + jnp.arange(WIN_Q_BLOCK)
        pos = start - WIN_SIZE + jnp.arange(span)
        dist = t[:, None] - pos[None, :]
        mask = (dist >= 0) & (dist < WIN_SIZE) & (pos[None, :] >= 0)
        bias = table[t5_bucket(dist)].astype(jnp.float32)
        bias = bias.reshape(WIN_Q_BLOCK, span, G, R).transpose(2, 3, 0, 1)
        logits = jnp.einsum('bqgrd,bkgd->bgrqk', qb, kw).astype(jnp.float32) * (dh ** -0.5)
        p = masked_softmax(logits + bias, mask)
        return jnp.einsum('bgrqk,bkgd->bqgrd', p.astype(vw.dtype), vw)

    out = lax.map(one, (q_blk, jnp.arange(nq)))
    return out.transpose(1, 0, 2, 3, 4, 5).reshape(B, S, H, dh)

def nsa_mixer(h, w_in, w_out, k_pos, k_w1, k_w2, v_pos, v_w1, v_w2, table):
    B, S, _ = h.shape
    H, dh, G = NSA_HEADS, NSA_HEAD_DIM, NSA_KV_GROUPS
    q, kv, g, z = split_cols(h @ w_in, [NSA_WIDTH, 6 * NSA_KV_WIDTH, 3 * H, 3 * NSA_WIDTH])
    q = q.reshape(B, S, H, dh)
    k_c, v_c, k_s, v_s, k_w, v_w = [a.reshape(B, S, G, dh) for a in jnp.split(kv, 6, axis=-1)]
    gates = jax.nn.sigmoid(g).reshape(B, S, 3, H, 1)
    zs = jax.nn.silu(z).reshape(B, S, 3, H, dh)
    kc = compress_kv(k_c, k_pos, k_w1, k_w2)
    vc = compress_kv(v_c, v_pos, v_w1, v_w2)
    o_cmp, p_cmp = nsa_compressed(q, kc, vc, table)
    sel = select_blocks(p_cmp, S)
    o_slc = nsa_selected(q, k_s, v_s, sel, table)
    o_win = nsa_window(q, k_w, v_w, table)
    o = jnp.stack([o_cmp, o_slc, o_win], axis=2)
    y = jnp.sum(gates * o * zs, axis=2).reshape(B, S, NSA_WIDTH)
    return y @ w_out

def rotary(x):
    S, d = x.shape[1], x.shape[-1]
    inv = 1.0 / (ROPE_BASE ** jnp.linspace(0.0, 1.0, d // 2, dtype=jnp.float32))
    ang = jnp.arange(S, dtype=jnp.float32)[:, None] * inv[None, :]
    cos = jnp.cos(ang)[None, :, None, :].astype(x.dtype)
    sin = jnp.sin(ang)[None, :, None, :].astype(x.dtype)
    x1, x2 = x[..., :d // 2], x[..., d // 2:]
    return jnp.concatenate([x1 * cos - x2 * sin, x1 * sin + x2 * cos], axis=-1)

def chunkwise_retention(q, k, v):
    B, S, H, dk = q.shape
    dv = v.shape[-1]
    C = RET_CHUNK
    nc = S // C
    dt = q.dtype
    log_g = jnp.log(1.0 - 2.0 ** (-5.0 - jnp.arange(H, dtype=jnp.float32)))
    i = jnp.arange(C, dtype=jnp.float32)
    diff = i[:, None] - i[None, :]
    inner = jnp.where(diff >= 0, jnp.exp(diff[None] * log_g[:, None, None]), 0.0).astype(dt)
    xi = jnp.exp((i + 1.0)[None, :] * log_g[:, None]).astype(dt)
    zeta = jnp.exp((C - 1.0 - i)[None, :] * log_g[:, None]).astype(dt)
    chunk_decay = jnp.exp(C * log_g).astype(dt)
    qc = q.reshape(B, nc, C, H, dk).transpose(1, 0, 3, 2, 4)
    kc = k.reshape(B, nc, C, H, dk).transpose(1, 0, 3, 2, 4)
    vc = v.reshape(B, nc, C, H, dv).transpose(1, 0, 3, 2, 4)

    def step(state, inp):
        qi, ki, vi = inp
        attn = jnp.einsum('bhid,bhjd->bhij', qi, ki) * inner[None]
        o = (jnp.einsum('bhij,bhjv->bhiv', attn, vi)
             + jnp.einsum('bhid,bhdv->bhiv', qi, state) * xi[None, :, :, None])
        state = (state * chunk_decay[None, :, None, None]
                 + jnp.einsum('bhjd,bhjv->bhdv', ki * zeta[None, :, :, None], vi))
        return state, o

    state0 = jnp.zeros((B, H, dk, dv), dt)
    _, o = lax.scan(step, state0, (qc, kc, vc))
    return o.transpose(1, 0, 3, 2, 4).reshape(B, S, H, dv)

def retention_mixer(h, w_in, w_out, gn_gain):
    B, S, _ = h.shape
    q, k, v, z = split_cols(h @ w_in, [RET_QK_WIDTH, RET_QK_WIDTH, RET_WIDTH, RET_WIDTH])
    q = rotary(q.reshape(B, S, RET_HEADS, RET_QK_DIM))
    k = rotary(k.reshape(B, S, RET_HEADS, RET_QK_DIM)) * (RET_QK_DIM ** -0.5)
    v = v.reshape(B, S, RET_HEADS, RET_V_DIM)
    o = chunkwise_retention(q, k, v).astype(jnp.float32)
    mu = jnp.mean(o, axis=-1, keepdims=True)
    var = jnp.mean(jnp.square(o - mu), axis=-1, keepdims=True)
    o = (o - mu) * lax.rsqrt(var + GN_EPS) * gn_gain.reshape(RET_HEADS, RET_V_DIM).astype(jnp.float32)
    o = o.astype(h.dtype).reshape(B, S, RET_WIDTH)
    return (o * jax.nn.silu(z)) @ w_out

def first_inputs(seed: int = 0) -> dict:
    key = jax.random.key(seed)
    ks = jax.random.split(key, 16)
    n_nsa = (DEPTH + N_MIXERS - 1) // N_MIXERS
    n_ret = DEPTH // N_MIXERS

    def nrm(k, shape, scale):
        return jax.random.normal(k, shape, jnp.float32) * scale

    return {
        "x": nrm(ks[0], (BATCH, SEQ, D_MODEL), 1.0),
        "pre_norm_gain": 1.0 + nrm(ks[1], (DEPTH, D_MODEL), 0.1),
        "post_norm_gain": 1.0 + nrm(ks[2], (DEPTH, D_MODEL), 0.1),
        "rel_bias_table": nrm(ks[3], (REL_BUCKETS, NSA_HEADS), 0.5),
        "nsa_w_in": nrm(ks[4], (n_nsa, D_MODEL, NSA_PROJ), D_MODEL ** -0.5),
        "nsa_w_out": nrm(ks[5], (n_nsa, NSA_WIDTH, D_MODEL), NSA_WIDTH ** -0.5),
        "nsa_cmp_k_pos": nrm(ks[6], (n_nsa, CMP_BLOCK, NSA_HEAD_DIM), 0.5),
        "nsa_cmp_k_w1": nrm(ks[7], (n_nsa, CMP_BLOCK * NSA_HEAD_DIM, CMP_HIDDEN), (CMP_BLOCK * NSA_HEAD_DIM) ** -0.5),
        "nsa_cmp_k_w2": nrm(ks[8], (n_nsa, CMP_HIDDEN, NSA_HEAD_DIM), CMP_HIDDEN ** -0.5),
        "nsa_cmp_v_pos": nrm(ks[9], (n_nsa, CMP_BLOCK, NSA_HEAD_DIM), 0.5),
        "nsa_cmp_v_w1": nrm(ks[10], (n_nsa, CMP_BLOCK * NSA_HEAD_DIM, CMP_HIDDEN), (CMP_BLOCK * NSA_HEAD_DIM) ** -0.5),
        "nsa_cmp_v_w2": nrm(ks[11], (n_nsa, CMP_HIDDEN, NSA_HEAD_DIM), CMP_HIDDEN ** -0.5),
        "ret_w_in": nrm(ks[12], (n_ret, D_MODEL, RET_PROJ), D_MODEL ** -0.5),
        "ret_w_out": nrm(ks[13], (n_ret, RET_WIDTH, D_MODEL), RET_WIDTH ** -0.5),
        "ret_gn_gain": 1.0 + nrm(ks[14], (n_ret, RET_WIDTH), 0.1),
    }

def first_block(x, pre_norm_gain, post_norm_gain, rel_bias_table, nsa_w_in, nsa_w_out,
              nsa_cmp_k_pos, nsa_cmp_k_w1, nsa_cmp_k_w2, nsa_cmp_v_pos, nsa_cmp_v_w1, nsa_cmp_v_w2,
              ret_w_in, ret_w_out, ret_gn_gain):
    h = x
    for layer in range(DEPTH):
        slot = layer // N_MIXERS
        u = rms_norm(h, pre_norm_gain[layer])
        if layer % N_MIXERS == 0:
            y = nsa_mixer(u, nsa_w_in[slot], nsa_w_out[slot],
                          nsa_cmp_k_pos[slot], nsa_cmp_k_w1[slot], nsa_cmp_k_w2[slot],
                          nsa_cmp_v_pos[slot], nsa_cmp_v_w1[slot], nsa_cmp_v_w2[slot],
                          rel_bias_table)
        else:
            y = retention_mixer(u, ret_w_in[slot], ret_w_out[slot], ret_gn_gain[slot])
        h = h + rms_norm(y, post_norm_gain[layer])
    return h


DEPTH_2 = 2

D_MIX = D_MODEL
SB_WIDTH = D_MIX // 2
CONV_WIDTH = D_MIX - SB_WIDTH
SB_HEAD_DIM = 64
SB_HEADS = SB_WIDTH // SB_HEAD_DIM
CONV_K = 3
Q_BLOCK = 128
D_FF = 7 * D_MODEL // 2
N_EXPERTS = 8
TOP_K = 2
D_PLE = 256
N_DENSE = (DEPTH_2 + 1) // 2
N_MOE = DEPTH_2 // 2
D_IN_PROJ = 3 * SB_WIDTH + 3 * CONV_WIDTH
EPS = 1e-6


def rmsnorm(x, g):
    xf = x.astype(jnp.float32)
    y = xf * lax.rsqrt(jnp.mean(xf * xf, axis=-1, keepdims=True) + EPS)
    return (y * g.astype(jnp.float32)).astype(x.dtype)

def stick_breaking_attention(q, k, v):
    bsz, nh, s_len, dh = q.shape
    dtype = q.dtype
    qf = q.astype(jnp.float32)
    kf = k.astype(jnp.float32)
    vf = v.astype(jnp.float32)
    scale = 1.0 / np.sqrt(dh).astype(np.float32)
    n_blocks = s_len // Q_BLOCK
    q_blocks = qf.reshape(bsz, nh, n_blocks, Q_BLOCK, dh).transpose(2, 0, 1, 3, 4)
    key_pos = jnp.arange(s_len)

    def one_block(args):
        q_blk, blk_idx = args
        z = jnp.einsum('bhqd,bhkd->bhqk', q_blk, kf) * scale
        q_pos = blk_idx * Q_BLOCK + jnp.arange(Q_BLOCK)
        causal = key_pos[None, :] < q_pos[:, None]
        log_beta = jax.nn.log_sigmoid(z)
        log_one_minus = jnp.where(causal, jax.nn.log_sigmoid(-z), 0.0)
        later = lax.cumsum(log_one_minus, axis=3, reverse=True) - log_one_minus
        weights = jnp.where(causal, jnp.exp(log_beta + later), 0.0)
        return jnp.einsum('bhqk,bhkd->bhqd', weights, vf)

    out = lax.map(one_block, (q_blocks, jnp.arange(n_blocks)))
    out = out.transpose(1, 2, 0, 3, 4).reshape(bsz, nh, s_len, dh)
    return out.astype(dtype)

def causal_depthwise_conv(u, w, bias):
    ch = u.shape[-1]
    rhs = w.reshape(CONV_K, 1, ch).astype(u.dtype)
    out = lax.conv_general_dilated(
        u, rhs, window_strides=(1,), padding=[(CONV_K - 1, 0)],
        dimension_numbers=('NWC', 'WIO', 'NWC'), feature_group_count=ch)
    return out + bias.astype(u.dtype)

def swiglu(x, w1, w3, w2):
    return (jax.nn.silu(x @ w1) * (x @ w3)) @ w2

def moe_swiglu(x, router_w, w1, w3, w2):
    bsz, s_len, d = x.shape
    xt = x.reshape(bsz * s_len, d)
    logits = (xt @ router_w).astype(jnp.float32)
    top_vals, top_idx = lax.top_k(logits, TOP_K)
    gates = jax.nn.softmax(top_vals, axis=-1)
    combine = jnp.sum(jax.nn.one_hot(top_idx, N_EXPERTS, dtype=jnp.float32)
                      * gates[..., None], axis=1).astype(x.dtype)
    out = jnp.zeros_like(xt)
    for e in range(N_EXPERTS):
        out = out + combine[:, e:e + 1] * swiglu(xt, w1[e], w3[e], w2[e])
    return out.reshape(bsz, s_len, d)

def second_inputs(seed: int = 0) -> dict:
    key = jax.random.key(seed)
    ks = jax.random.split(key, 24)

    def nrm(k, shape, scale):
        return jax.random.normal(k, shape, jnp.float32) * scale

    def gain(k, shape):
        return 1.0 + 0.02 * jax.random.normal(k, shape, jnp.float32)

    return {
        "x": nrm(ks[0], (BATCH, SEQ, D_MODEL), 1.0),
        "p": nrm(ks[1], (DEPTH_2, BATCH, SEQ, D_PLE), 1.0),
        "mix_norm_g": gain(ks[2], (DEPTH_2, D_MODEL)),
        "w_in": nrm(ks[3], (DEPTH_2, D_MODEL, D_IN_PROJ), D_MODEL ** -0.5),
        "q_norm_g": gain(ks[4], (DEPTH_2, SB_HEAD_DIM)),
        "k_norm_g": gain(ks[5], (DEPTH_2, SB_HEAD_DIM)),
        "conv_w": nrm(ks[6], (DEPTH_2, CONV_K, CONV_WIDTH), CONV_K ** -0.5),
        "conv_b": nrm(ks[7], (DEPTH_2, CONV_WIDTH), 0.02),
        "attn_out_g": gain(ks[8], (DEPTH_2, SB_WIDTH)),
        "conv_out_g": gain(ks[9], (DEPTH_2, CONV_WIDTH)),
        "w_o": nrm(ks[10], (DEPTH_2, D_MIX, D_MODEL), D_MIX ** -0.5),
        "ffn_norm_g": gain(ks[11], (DEPTH_2, D_MODEL)),
        "dense_w1": nrm(ks[12], (N_DENSE, D_MODEL, D_FF), D_MODEL ** -0.5),
        "dense_w3": nrm(ks[13], (N_DENSE, D_MODEL, D_FF), D_MODEL ** -0.5),
        "dense_w2": nrm(ks[14], (N_DENSE, D_FF, D_MODEL), D_FF ** -0.5),
        "router_w": nrm(ks[15], (N_MOE, D_MODEL, N_EXPERTS), D_MODEL ** -0.5),
        "moe_w1": nrm(ks[16], (N_MOE, N_EXPERTS, D_MODEL, D_FF), D_MODEL ** -0.5),
        "moe_w3": nrm(ks[17], (N_MOE, N_EXPERTS, D_MODEL, D_FF), D_MODEL ** -0.5),
        "moe_w2": nrm(ks[18], (N_MOE, N_EXPERTS, D_FF, D_MODEL), D_FF ** -0.5),
        "ple_norm_g": gain(ks[19], (DEPTH_2, D_MODEL)),
        "ple_gate_w": nrm(ks[20], (DEPTH_2, D_MODEL, D_MODEL), D_MODEL ** -0.5),
        "ple_proj_w": nrm(ks[21], (DEPTH_2, D_PLE, D_MODEL), D_PLE ** -0.5),
    }

def second_block(x, p, mix_norm_g, w_in, q_norm_g, k_norm_g, conv_w, conv_b,
              attn_out_g, conv_out_g, w_o, ffn_norm_g, dense_w1, dense_w3, dense_w2,
              router_w, moe_w1, moe_w3, moe_w2, ple_norm_g, ple_gate_w, ple_proj_w):
    bsz, s_len, _ = x.shape
    h = x
    for i in range(DEPTH_2):
        a = rmsnorm(h, mix_norm_g[i])
        proj = a @ w_in[i]
        q, k, v = (proj[..., 0:SB_WIDTH],
                   proj[..., SB_WIDTH:2 * SB_WIDTH],
                   proj[..., 2 * SB_WIDTH:3 * SB_WIDTH])
        off = 3 * SB_WIDTH
        u, c_gate, b_gate = (proj[..., off:off + CONV_WIDTH],
                             proj[..., off + CONV_WIDTH:off + 2 * CONV_WIDTH],
                             proj[..., off + 2 * CONV_WIDTH:off + 3 * CONV_WIDTH])

        def heads(t):
            return t.reshape(bsz, s_len, SB_HEADS, SB_HEAD_DIM).transpose(0, 2, 1, 3)
        qh = rmsnorm(heads(q), q_norm_g[i])
        kh = rmsnorm(heads(k), k_norm_g[i])
        vh = heads(v)
        attn = stick_breaking_attention(qh, kh, vh)
        attn = attn.transpose(0, 2, 1, 3).reshape(bsz, s_len, SB_WIDTH)

        conv = b_gate * causal_depthwise_conv(c_gate * u, conv_w[i], conv_b[i])

        mixed = jnp.concatenate([rmsnorm(attn, attn_out_g[i]),
                                 rmsnorm(conv, conv_out_g[i])], axis=-1)
        h = h + mixed @ w_o[i]

        f = rmsnorm(h, ffn_norm_g[i])
        if i % 2 == 0:
            j = i // 2
            h = h + swiglu(f, dense_w1[j], dense_w3[j], dense_w2[j])
        else:
            j = i // 2
            h = h + moe_swiglu(f, router_w[j], moe_w1[j], moe_w3[j], moe_w2[j])

        gate = jax.nn.sigmoid(rmsnorm(h, ple_norm_g[i]) @ ple_gate_w[i])
        h = h + gate * (p[i] @ ple_proj_w[i])
    return h


def setup_inputs(seed=0):
    out = dict(first_inputs(seed))
    for name, value in second_inputs(seed + 1).items():
        if name != "x":
            out[name + "_2"] = value
    return out


def reference(
    x, pre_norm_gain, post_norm_gain, rel_bias_table, nsa_w_in, nsa_w_out, nsa_cmp_k_pos,
    nsa_cmp_k_w1, nsa_cmp_k_w2, nsa_cmp_v_pos, nsa_cmp_v_w1, nsa_cmp_v_w2, ret_w_in, ret_w_out,
    ret_gn_gain, p_2, mix_norm_g_2, w_in_2, q_norm_g_2, k_norm_g_2, conv_w_2, conv_b_2,
    attn_out_g_2, conv_out_g_2, w_o_2, ffn_norm_g_2, dense_w1_2, dense_w3_2, dense_w2_2,
    router_w_2, moe_w1_2, moe_w3_2, moe_w2_2, ple_norm_g_2, ple_gate_w_2, ple_proj_w_2,
):
    x = first_block(
        x, pre_norm_gain, post_norm_gain, rel_bias_table, nsa_w_in, nsa_w_out, nsa_cmp_k_pos,
        nsa_cmp_k_w1, nsa_cmp_k_w2, nsa_cmp_v_pos, nsa_cmp_v_w1, nsa_cmp_v_w2, ret_w_in,
        ret_w_out, ret_gn_gain,
    )
    return second_block(
        x, p_2, mix_norm_g_2, w_in_2, q_norm_g_2, k_norm_g_2, conv_w_2, conv_b_2, attn_out_g_2,
        conv_out_g_2, w_o_2, ffn_norm_g_2, dense_w1_2, dense_w3_2, dense_w2_2, router_w_2,
        moe_w1_2, moe_w3_2, moe_w2_2, ple_norm_g_2, ple_gate_w_2, ple_proj_w_2,
    )


_drawn_inputs = setup_inputs


def setup_inputs(seed=0):
    import zlib

    import numpy as np

    out = dict(_drawn_inputs(seed))
    spreads = {}
    factors = {'q_norm_g_2': 5.585,
     'k_norm_g_2': 4.736,
     'conv_b_2': 3.216,
     'attn_out_g_2': 2.892,
     'ple_norm_g_2': 81.075,
     'conv_out_g_2': 3.533,
     'ffn_norm_g_2': 4.069}
    for name, (base, spread) in spreads.items():
        noise = np.random.default_rng([zlib.crc32(name.encode()), seed]).standard_normal(out[name].shape)
        drawn = base * np.exp(spread * noise) if base else spread * noise
        out[name] = __import__('jax').numpy.asarray(drawn.astype(out[name].dtype))
    for name, factor in factors.items():
        out[name] = (out[name] * factor).astype(out[name].dtype)
    return out
```

```python
from contextlib import ExitStack

import numpy as np

import concourse.bass as bass
from concourse import mybir

F32 = mybir.dt.float32
F32R = mybir.dt.float32r
I32 = mybir.dt.int32
ALU = mybir.AluOpType
ACT = mybir.ActivationFunctionType
AX = mybir.AxisListType.X

P = 128
S = 256
NT = S // P
D = 1024
KD = D // P
NB = 512
KU = 4

NH, DH, NG = 16, 64, 4
RG = NH // NG
KV0, G0, Z0 = NH * DH, NH * DH + 6 * NG * DH, NH * DH + 6 * NG * DH + 3 * NH
CB, CS = 32, 16
NC_ = (S - CB) // CS + 1
HC = 256
NBUCK, MAXD = 32, 128
SC = DH ** -0.5
MASKED = -1e30 / SC
LREV = 384

SH = 8
FF = 3584
NFB = FF // NB
NE = 8
EPS = 1e-6

RAW = 6
SPL = 3
AHEAD = SPL - 1
UNITS_ROUND = 2 * NFB * 2 + FF // (KU * P) * 2
BLOCKS_ROUND = 2 * NFB


def weight_units(w):
    def block(m, c0, n=NB, kt=KD):
        return [(m, k, min(KU, kt - k), c0, n) for k in range(0, kt, KU)]

    def ffn(w1, w3, w2):
        out = []
        for b in range(NFB):
            out += block(w1, b * NB) + block(w3, b * NB)
        for k in range(0, FF // P, KU):
            out += [(w2, k, KU, 0, NB), (w2, k, KU, NB, NB)]
        return out

    nsa = block(w["nsa_in"], KV0)
    nsa += block(w["nsa_in"], 0) + block(w["nsa_in"], NB)
    nsa += block(w["nsa_in"], KV0 + NB) + block(w["nsa_in"], KV0 + 2 * NB)
    nsa += [(w["nsa_in"], 0, KD, G0, 3 * NH)]
    nsa += [(w["cmp_k1"], 0, 8, 0, HC), (w["cmp_k1"], 8, 8, 0, HC)]
    nsa += [(w["cmp_v1"], 0, 8, 0, HC), (w["cmp_v1"], 8, 8, 0, HC)]
    for b in range(6):
        nsa += block(w["nsa_in"], Z0 + b * NB)
    nsa += block(w["nsa_out"], 0) + block(w["nsa_out"], NB)

    def mix(i):
        out = []
        for b in range(6):
            out += block(w[f"in{i}"], b * NB)
        return out + block(w[f"o{i}"], 0) + block(w[f"o{i}"], NB)

    def ple(i):
        return (block(w[f"pg{i}"], 0) + block(w[f"pg{i}"], NB)
                + block(w[f"pp{i}"], 0, kt=2) + block(w[f"pp{i}"], NB, kt=2))

    before = nsa + mix(0) + ffn(w["d1"], w["d3"], w["d2"]) + ple(0) + mix(1)
    return before, ffn(w["m1"], w["m3"], w["m2"]), ple(1)


def first_unit_of():
    at, out = 0, {}
    for name, n in (("kv_c", 2), ("q", 4), ("kv_s", 2), ("kv_w", 2), ("gate", 1), ("cmp", 4), ("z", 12),
                    ("nsa_out", 4), ("in0", 12), ("o0", 4), ("ffn0", UNITS_ROUND), ("ple0", 6), ("in1", 12),
                    ("o1", 4), ("ffn1", UNITS_ROUND)):
        out[name] = at
        at += n
    out["ple1"] = out["ffn1"]
    return out


def build(nc, t, out):
    U = first_unit_of()
    B = {}
    nblk = 0
    for name, n in (("kv_c", 1), ("q", 2), ("kv_s", 1), ("kv_w", 1), ("gate", 1), ("cmp", 2), ("z", 6),
                    ("nsa_out", 2), ("in0", 6), ("oT0", 1), ("o0", 2), ("ffn0", BLOCKS_ROUND), ("ple0", 4),
                    ("in1", 6), ("oT1", 1), ("o1", 2), ("ffn1", BLOCKS_ROUND)):
        B[name] = nblk
        nblk += n
    z_blocks = range(B["z"], B["z"] + 6)
    B["ple1"] = B["ffn1"]
    block_end = {}
    for name, n, units in (("kv_c", 1, 2), ("q", 2, 2), ("kv_s", 1, 2), ("kv_w", 1, 2), ("gate", 1, 1),
                           ("cmp", 2, 2), ("z", 6, 2), ("nsa_out", 2, 2), ("in0", 6, 2), ("o0", 2, 2),
                           ("ffn0", BLOCKS_ROUND, 2), ("in1", 6, 2), ("o1", 2, 2), ("ffn1", BLOCKS_ROUND, 2)):
        for j in range(n):
            block_end[B[name] + j] = U[name] + (j + 1) * units
    ple_end = [2, 4, 5, 6]
    for j in range(4):
        block_end[B["ple0"] + j] = U["ple0"] + ple_end[j]

    weights = {
        "nsa_in": t["nsa_w_in"][0], "nsa_out": t["nsa_w_out"][0],
        "cmp_k1": t["nsa_cmp_k_w1"][0], "cmp_v1": t["nsa_cmp_v_w1"][0],
        "d1": t["dense_w1_2"][0], "d3": t["dense_w3_2"][0], "d2": t["dense_w2_2"][0],
        "m1": t["moe_w1_2"][0], "m3": t["moe_w3_2"][0], "m2": t["moe_w2_2"][0],
    }
    for i in range(2):
        weights |= {f"in{i}": t["w_in_2"][i], f"o{i}": t["w_o_2"][i],
                    f"pg{i}": t["ple_gate_w_2"][i], f"pp{i}": t["ple_proj_w_2"][i]}
    before, per_round, after = weight_units(weights)
    assert len(before) == U["ffn1"] and len(per_round) == UNITS_ROUND

    with ExitStack() as ctx:
        def sb(name, shape, dt=F32, scope=ctx):
            return scope.enter_context(nc.sbuf_tensor(name, shape, dt))

        raw = sb("raw", [P, RAW, KU * NB])
        whi = sb("whi", [P, SPL, KU * NB], F32R)
        wlo = sb("wlo", [P, SPL, KU * NB], F32R)
        h = sb("h", [P, NT, D])
        tok = sb("tok", [P, NT, D])
        xh = sb("xh", [P, KD, S], F32R)
        xl = sb("xl", [P, KD, S], F32R)
        con = sb("con", [P, 8 * P + 64 + 8])
        ident, ntri, nones, negm, keep, stri, ones, iota = (con[:, i * P:(i + 1) * P] for i in range(8))
        tril8 = con[:, 8 * P:8 * P + 64]
        bdiag = con[:, 8 * P + 64:8 * P + 72]
        gains = sb("gains", [P, 7, KD])
        ogain = sb("ogain", [P, 2, KD])
        qkg = sb("qkg", [P, 2, 2])
        convw = sb("convw", [P, 2, 4, 4])
        rw = sb("rw", [P, KD, NE])
        rwh = sb("rwh", [P, KD, NE], F32R)
        rwl = sb("rwl", [P, KD, NE], F32R)
        st = sb("st", [P, 64])
        epst = sb("epst", [P, 1])
        nround = sb("nround", [1, 1], I32)

        with ExitStack() as nsa:
            tabx = sb("tabx", [NBUCK + 1, NH], scope=nsa)
            with ExitStack() as a:
                kc2 = sb("kc2", [P, NT, 2 * NG, 2, DH], scope=a)
                XW = 2 * (CB // 2) * NG * NC_
                XT = XW + P - NG * NC_
                xw = sb("xw", [P, XT], scope=a)
            bias = sb("bias", [P, NH, S], scope=nsa)
            cbias = sb("cbias", [P, NT, NH, NC_], scope=nsa)
            qT = sb("qT", [P, NH // 2, S], scope=nsa)
            kT = sb("kT", [P, 2, NG, S], scope=nsa)
            vs = sb("vs", [P, 2, NT, NG * DH], scope=nsa)
            pos2 = sb("pos2", [P, 2, CB // 2], scope=nsa)
            w2k = sb("w2k", [P, 2, 2, DH], scope=nsa)
            w2v = sb("w2v", [P, 2, DH], scope=nsa)
            kcT = sb("kcT", [P, NG * NC_], scope=nsa)
            gate = sb("gate", [P, NT, 3 * NH], scope=nsa)
            cst = sb("cst", [P, 3, NT * NH], scope=nsa)
            grow = sb("grow", [P, NT, NH], scope=nsa)
            ast_ = sb("ast", [P, 16, 3, RG], scope=nsa)
            with ExitStack() as early:
                with ExitStack() as a:
                    oh = sb("oh", [NBUCK + 1, 512 + LREV], scope=a)
                    revb = sb("revb", [NH, LREV], scope=a)
                    kd = sb("kd", [P, 2, NT, NG, 2, DH], scope=a)
                    xwh = sb("xwh", [P, XT], F32R, scope=a)
                    xwl = sb("xwl", [P, XT], F32R, scope=a)
                with ExitStack() as a:
                    hc = sb("hc", [NG * NC_, 2, HC], scope=a)
                    hcT = sb("hcT", [P, 2, 2, NG * NC_], scope=a)
                    hcR = sb("hcR", [P, 2, 2, 8 * NC_], scope=a)
                    vcb = sb("vcb", [8 * NC_, 2, 8, DH], scope=a)
                    lcT = sb("lcT", [8 * NC_, 2 * NT, P], scope=a)
                    lc = sb("lc", [P, NT, NH, NC_], scope=a)
            y = tok
            with ExitStack() as late:
                ob = sb("ob", [P, NT, D], scope=late)
                zt = sb("zt", [P, NT, NB], scope=late)
                sg = sb("sg", [P, 2, RG, S], scope=late)
                pT = sb("pT", [P, 2, RG, NT, P], scope=late)
                postg = sb("postg", [P, D], scope=late)

        with ExitStack() as mx:
            qk = sb("qk", [P, 2, NT, NB], scope=mx)
            sq = sb("sq", [P, NT, NB], scope=mx)
            qk_ss = sb("qk_ss", [P, 2, NT, SH], scope=mx)
            v2 = sb("v2", [P, NT, NB], scope=mx)
            qkT = sb("qkT", [P, 2, 4, S], scope=mx)
            uT = sb("uT", [P, 4, S], scope=mx)
            cu = sb("cu", [P, 4, S + 2], scope=mx)
            cv = sb("cv", [P, 4, S], scope=mx)
            mixT = sb("mixT", [P, 8, S], scope=mx)
            mixs = sb("mixs", [P, 8, S], scope=mx)
            rn = sb("rn", [P, 2, S], scope=mx)
            spa = sb("spa", [P, 4, 3 * P], scope=mx)
            spb = sb("spb", [P, 4, 3 * P], scope=mx)
            wT = sb("wT", [P, 4, 3 * P], scope=mx)

        with ExitStack() as ff:
            gt = sb("gt", [P, NT, NB], scope=ff)
            ht = sb("ht", [P, NT, NB], scope=ff)
            pt_in = sb("pt_in", [P, NT, 2 * P], scope=ff)
            with ExitStack() as a:
                hTh = sb("hTh", [P, FF // P, S], F32R, scope=a)
                hTl = sb("hTl", [P, FF // P, S], F32R, scope=a)
            with ExitStack() as a:
                mTh = sb("mTh", [P, FF // P, P], F32R, scope=a)
                mTl = sb("mTl", [P, FF // P, P], F32R, scope=a)
                xnh = sb("xnh", [P, NT, D], F32R, scope=a)
                xnl = sb("xnl", [P, NT, D], F32R, scope=a)
                xgh = sb("xgh", [P, KD, P], F32R, scope=a)
                xgl = sb("xgl", [P, KD, P], F32R, scope=a)
                yh = sb("yh", [P, D], F32R, scope=a)
                yl = sb("yl", [P, D], F32R, scope=a)
                pick = sb("pick", [P, NT, P], F32R, scope=a)
                pickT = sb("pickT", [P, NT, P], F32R, scope=a)
                lg = sb("lg", [P, NT, NE], scope=a)
                cmpa = sb("cmpa", [P, NT, NE, NE], scope=a)
                cmpb = sb("cmpb", [P, NT, NE, NE], scope=a)
                sel = sb("sel", [P, NT, NE], scope=a)
                gw = sb("gw", [P, NT, NE], scope=a)
                slot = sb("slot", [P, NT, 2 * NE + 1], scope=a)
                cnt = sb("cnt", [P, NE + 4], scope=a)
            with ExitStack() as a:
                ptTh = sb("ptTh", [P, 2, S], F32R, scope=a)
                ptTl = sb("ptTl", [P, 2, S], F32R, scope=a)
                pg = sb("pg", [P, 2, NT, NB], scope=a)
                pm = sb("pm", [P, NT, NB], scope=a)

        ps = ctx.enter_context(nc.psum_tensor("ps", [P, 8, NB], F32))
        bias_dram = nc.dram_tensor("bias_scratch", [NH, P, LREV], F32, kind="Internal").ap()

        per = {}

        def sem(name, each_round=0):
            per[name] = each_round
            return ctx.enter_context(nc.semaphore(name))

        unit_loaded = [sem(f"unit_loaded{s}", 16 * UNITS_ROUND // RAW) for s in range(RAW)]
        high_done, low_done, unit_used = (sem(n, UNITS_ROUND) for n in ("high_done", "low_done", "unit_used"))
        banks_free = [sem(f"banks_free{i}", BLOCKS_ROUND // 2) for i in range(2)]
        hidden_turned, hidden_high, hidden_low = (
            sem(n, NFB) for n in ("hidden_turned", "hidden_high", "hidden_low"))
        act_step, dve_step = sem("act_step"), sem("dve_step")
        pick_done = sem("pick_done", 1)
        pick_turned = sem("pick_turned", 1)
        pick_copied = sem("pick_copied", 1)
        gathered = sem("gathered", 1)
        gather_high = sem("gather_high", 1)
        gather_low = sem("gather_low", 1)
        y_high = sem("y_high", 1)
        y_low = sem("y_low", 1)
        scatter_done = sem("scatter_done", 1)
        round_done = sem("round_done", 1)
        rounds_known = sem("rounds_known")
        h_half = sem("h_half")
        stored = sem("stored")
        h_turned = sem("h_turned")
        gains_loaded = sem("gains_loaded")
        tab_product = sem("tab_product")
        x_loaded = sem("x_loaded")
        eps_set = sem("eps_set")
        windows_done = sem("windows_done")
        q_turned = sem("q_turned")
        k_turned = sem("k_turned")
        cmp_logits = sem("cmp_logits")
        logits_done = sem("logits_done")
        z_used = sem("z_used")
        y_turned = sem("y_turned")
        qk_squares = sem("qk_squares")
        z_scores = sem("z_scores")
        sp_done = sem("sp_done")
        stick_done = sem("stick_done")
        pv_done = sem("pv_done")
        mix_sums = sem("mix_sums")
        mix_normed = sem("mix_normed")
        p_turned = sem("p_turned")
        post_added = sem("post_added")
        dense_added = sem("dense_added")
        router_loaded = sem("router_loaded")
        logit_shift = sem("logit_shift")
        root_done = sem("root_done")
        xh_done = sem("xh_done")
        cbias_done = sem("cbias_done")
        kc_turned = sem("kc_turned")
        cmp_loaded = sem("cmp_loaded")
        window_high = sem("window_high")
        hc_turned = sem("hc_turned")
        rev_stored = sem("rev_stored")
        kcvc_product = sem("kcvc_product")
        cmp_scores = sem("cmp_scores")
        cmp_exp = sem("cmp_exp")
        lc_turned = sem("lc_turned")
        cmp_out = sem("cmp_out")
        o_evac = sem("o_evac")
        bias_loaded = sem("bias_loaded")
        scores_done = sem("scores_done")
        p_turned_all = sem("p_turned_all")
        pv_step = sem("pv_step")
        exp_done = sem("exp_done")
        z_done = sem("z_done")
        yh_done = sem("yh_done")
        post_root = sem("post_root")
        postg_loaded = sem("postg_loaded")
        qk_root = sem("qk_root")
        qk_turned = sem("qk_turned")
        mix_loaded = sem("mix_loaded")
        ln_done = sem("ln_done")
        mix_root = sem("mix_root")
        mixh_done = sem("mixh_done")
        ph_done = sem("ph_done")
        router_high = sem("router_high")
        xn_high = sem("xn_high")
        router_logits = sem("router_logits")
        sel_done = sem("sel_done")
        gate_exp = sem("gate_exp")
        slots_counted = sem("slots_counted")
        h_normed = sem("h_normed")
        con_loaded = sem("con_loaded")
        oh_loaded = sem("oh_loaded")
        table_one = sem("table_one")
        rev_ready = sem("rev_ready")
        xl_done = sem("xl_done")
        qT_done = sem("qT_done")
        window_low = sem("window_low")
        kT_done = sem("kT_done")
        hcT_done = sem("hcT_done")
        kcT_done = sem("kcT_done")
        lcT_done = sem("lcT_done")
        vcb_done = sem("vcb_done")
        pT_done = sem("pT_done")
        yl_done = sem("yl_done")
        qk_normed = sem("qk_normed")
        stick_exp = sem("stick_exp")
        qkT_done = sem("qkT_done")
        mix_squares = sem("mix_squares")
        mixl_done = sem("mixl_done")
        p_loaded = sem("p_loaded")
        pl_done = sem("pl_done")
        router_low = sem("router_low")
        xn_low = sem("xn_low")

        class Prog:

            def __init__(self):
                self.r, self.n, self.split, self.post = None, 0, 0, False

            def at(self, semaphore, n):
                k = per[semaphore.name]
                return n if self.r is None or not k else self.r * k + n

            def through(self, b):
                end = block_end[b] if not (self.post and b >= B["ple1"]) else U["ple1"] + ple_end[b - B["ple1"]]
                return self.at(unit_used, end)

            def freed(self, b):
                count = len([x for x in range(b % 2, b + 1, 2) if x not in z_blocks])
                return self.at(banks_free[b % 2], count)

        def pair(b):
            return 2 * (b % 2)

        def unit_columns(v, post):
            if v >= U["ffn1"] and not post:
                return KU * NB
            _, _, nk, _, n = after[v - U["ffn1"]] if post else before[v]
            return nk * n

        ld = nc.allow_non_contiguous_dma("small gains and constants")
        ctx.enter_context(ld)
        block_ = ctx.enter_context(nc.Block())

        @block_.sync
        def _(sp):
            g = Prog()
            sp.dma_start(h[:], t["x"][0].rearrange("(t p) d -> p t d", p=P)).then_inc(x_loaded, 16)

            def load(u, unit, e=None):
                m, k0, nk, c0, n = unit
                s = u % RAW
                if u >= RAW:
                    sp.wait_ge(low_done, g.at(low_done, u - RAW + 1))
                if e is None:
                    src = m[k0 * P:(k0 + nk) * P, c0:c0 + n].rearrange("(k p) n -> p k n", p=P)
                else:
                    src = m[bass.ds(e, 1), k0 * P:(k0 + nk) * P, c0:c0 + n].rearrange("a (k p) n -> p (a k) n", p=P)
                sp.dma_start(raw[:, s, 0:nk * n].rearrange("p (k n) -> p k n", k=nk), src)\
                    .then_inc(unit_loaded[s], 16)

            for u, unit in enumerate(before):
                load(u, unit)
            with sp.Fori(0, NE) as r:
                g.r = r
                for j, unit in enumerate(per_round):
                    load(U["ffn1"] + j, unit, r)
            g.r = None
            sp.wait_ge(rounds_known, 1)
            rounds = sp.value_load(nround[0:1, 0:1], min_val=NE, max_val=2 * NE)
            with sp.If(rounds > NE):
                with sp.Fori(NE, 2 * NE) as r:
                    g.r = r
                    for j, unit in enumerate(per_round):
                        load(U["ffn1"] + j, unit, r - NE)
            g.r = rounds
            for j, unit in enumerate(after):
                load(U["ple1"] + j, unit)
            for j in range(2):
                sp.wait_ge(h_half, 3 + j)
                c = slice(j * NB, (j + 1) * NB)
                sp.dma_start(out[0][:, c].rearrange("(t p) d -> p t d", p=P), h[:, :, c])\
                    .then_inc(stored, 16)
            sp.wait_ge(stored, 32)

        @block_.gpsimd
        def _(pool):
            def small(semaphore, dst, src):
                pool.dma_start(dst, src).then_inc(semaphore, 16)

            small(con_loaded, con[:], t["c_square"])
            small(oh_loaded, oh[:], t["c_onehot"])
            small(oh_loaded, tabx[0:NBUCK, :], t["rel_bias_table"])
            pool.memset(tabx[NBUCK:NBUCK + 1, :], 1.0).then_inc(table_one, 1)
            pool.wait_ge(table_one, 1)
            pool.memset(epst[:], EPS).then_inc(eps_set, 1)
            small(gains_loaded, gains[:, 0, :], t["pre_norm_gain"][0].rearrange("(k p) -> p k", p=P))
            for i in range(2):
                for j, n in ((1, "mix_norm_g_2"), (2, "ffn_norm_g_2"), (3, "ple_norm_g_2")):
                    small(gains_loaded, gains[:, 3 * i + j, :], t[n][i].rearrange("(k p) -> p k", p=P))
            for kv, n in ((0, "nsa_cmp_k_pos"), (1, "nsa_cmp_v_pos")):
                small(cmp_loaded, pos2[:, kv, :], t[n][0].rearrange("(m s) d -> (s d) m", s=2))
            for s in range(2):
                small(cmp_loaded, w2k[:, :, s, :], t["nsa_cmp_k_w2"][0].rearrange("(j p) d -> p j d", p=P))
            small(cmp_loaded, w2v[:], t["nsa_cmp_v_w2"][0].rearrange("(j p) d -> p j d", p=P))
            for i in range(2):
                for j, n in ((0, "attn_out_g_2"), (4, "conv_out_g_2")):
                    small(mix_loaded, ogain[:, i, j:j + 4], t[n][i].rearrange("(k p) -> p k", p=P))
                for j, n in ((0, "q_norm_g_2"), (1, "k_norm_g_2")):
                    for s in range(2):
                        small(mix_loaded, qkg[s * DH:(s + 1) * DH, i, j:j + 1],
                              t[n][i:i + 1].rearrange("a d -> d a"))
                for j in range(3):
                    small(mix_loaded, convw[:, i, :, j], t["conv_w_2"][i, j].rearrange("(k p) -> p k", p=P))
                small(mix_loaded, convw[:, i, :, 3], t["conv_b_2"][i].rearrange("(k p) -> p k", p=P))
            small(router_loaded, rw[:], t["router_w_2"][0].rearrange("(k p) e -> p k e", p=P))
            pool.wait_ge(rev_ready, 1)
            pool.dma_start(bias_dram, revb[:].unsqueeze(1).broadcast_to([NH, P, LREV])).then_inc(rev_stored, 16)
            pool.wait_ge(rev_stored, 16)
            pool.wait_ge(window_low, 1)
            pool.dma_start(bias[:], bass.AP(tensor=bias_dram.tensor, offset=P - 1,
                                            ap=[[LREV - 1, P], [P * LREV, NH], [1, S]])).then_inc(bias_loaded, 16)
            pool.wait_ge(o_evac, 1)
            small(postg_loaded, postg[:], t["post_norm_gain"][0:1].broadcast_to([P, D]))
            for i in range(2):
                pool.wait_ge(mixl_done, i + 1)
                small(p_loaded, pt_in[:], t["p_2"][i, 0].rearrange("(t p) d -> p t d", p=P))

        @block_.scalar
        def _(act):
            g = Prog()

            def step(ins):
                g.n += 1
                ins.then_inc(act_step, 1)
                act.wait_ge(act_step, g.n)

            AC = nc.scalar.activation

            def split_to(u):
                while g.split <= u:
                    v = g.split
                    n = unit_columns(v, g.post)
                    act.wait_ge(unit_loaded[v % RAW], g.at(unit_loaded[v % RAW], 16 * (v // RAW + 1)))
                    if v >= SPL:
                        act.wait_ge(unit_used, g.at(unit_used, v - SPL + 1))
                    AC(whi[:, v % SPL, 0:n], raw[:, v % RAW, 0:n], ACT.Copy).then_inc(high_done, 1)
                    g.split += 1

            def norm(k):
                for i in range(NT):
                    ins = AC(tok[:, i, :], h[:, i, :], ACT.Square, accum_out=st[:, i:i + 1])
                step(ins)
                AC(st[:, 2:4], st[:, 0:2], ACT.Sqrt, scale=1.0 / D, bias=epst[:, 0:1])\
                    .then_inc(root_done, 1)

            def turned_high(k):
                act.wait_ge(h_turned, k + 1)
                if k == 0:
                    act.wait_ge(gains_loaded, 16 * 7)
                for j in range(KD):
                    ins = AC(xh[:, j, :], ps[:, 4 + j // 2, (j % 2) * S:(j % 2 + 1) * S], ACT.Copy,
                             scale=gains[:, k, j:j + 1])
                ins.then_inc(xh_done, 1)

            def both(b):
                return ps[:, pair(b):pair(b) + 2, :]

            def flat(x):
                return x.rearrange("p a n -> p (a n)")

            def evac(b, dst, src=None, func=ACT.Copy):
                act.wait_ge(unit_used, g.through(b))
                AC(dst, both(b) if src is None else src, func).then_inc(banks_free[b % 2], 1)

            act.wait_ge(tab_product, 1)
            AC(revb[:], ps[0:NH, 0, 0:LREV], ACT.Copy).then_inc(rev_ready, 1)
            act.wait_ge(x_loaded, 16)
            act.wait_ge(eps_set, 1)
            norm(0)
            split_to(1)
            turned_high(0)
            split_to(U["q"] + 1)
            b = B["kv_c"]
            act.wait_ge(unit_used, g.through(b))
            for T in range(NT):
                for s in range(2):
                    ins = AC(kc2[:, T, :, s, :], ps[:, pair(b) + T, :].rearrange("p (g d) -> p g d", d=DH), ACT.Copy)
            ins.then_inc(banks_free[b % 2], 1)
            for i in range(2):
                split_to(U["q"] + 2 * i + 3)
                evac(B["q"] + i, tok[:, :, i * NB:(i + 1) * NB])
            act.wait_ge(windows_done, 1)
            AC(xwh[:], xw[:], ACT.Copy).then_inc(window_high, 1)
            for i in range(2):
                split_to(U["kv_s"] + 2 * i + 3)
                b = B["kv_s"] + i
                act.wait_ge(unit_used, g.through(b))
                for T in range(NT):
                    for s in range(2):
                        AC(kd[:, i, T, :, s, :], ps[:, pair(b) + T, 0:NG * DH].rearrange("p (g d) -> p g d", d=DH),
                           ACT.Copy)
                AC(vs[:, i, :, :], ps[:, pair(b):pair(b) + 2, NG * DH:NB], ACT.Copy).then_inc(banks_free[b % 2], 1)
                if i == 0:
                    act.wait_ge(q_turned, 1)
                    AC(flat(qT[:]), flat(ps[:, 4:8, :]), ACT.Copy).then_inc(qT_done, 1)
            split_to(U["gate"] + 2)
            b = B["gate"]
            evac(b, gate[:], ps[:, pair(b):pair(b) + 2, 0:3 * NH], ACT.Sigmoid)
            act.wait_ge(k_turned, 1)
            AC(kT[:].rearrange("p a g n -> p (a g n)"), flat(ps[:, 4:8, :]), ACT.Copy).then_inc(kT_done, 1)
            for kv in range(2):
                split_to(U["cmp"] + 2 * kv + 3)
                b = B["cmp"] + kv
                evac(b, hc[:, kv, :], ps[0:NG * NC_, pair(b), 0:HC], ACT.Silu)
            act.wait_ge(cmp_logits, 1)
            AC(lc[:], lc[:], ACT.Exp, scale=SC).then_inc(cmp_exp, 1)

            def att(i):
                if i >= 16:
                    return
                T = (i // 2) % 2
                nk = (T + 1) * P
                act.wait_ge(logits_done, i + 1)
                for r in range(RG):
                    ins = AC(sg[:, i % 2, r, 0:nk], sg[:, i % 2, r, 0:nk], ACT.Exp, scale=SC,
                             bias=ast_[:, i, 1, r:r + 1], accum_out=ast_[:, i, 2, r:r + 1])
                ins.then_inc(exp_done, 1)

            for kind, i in NSA_ORDER:
                if kind == "a":
                    att(i)
                elif i % 2:
                    b = B["z"] + i // 2
                    split_to(U["z"] + i + AHEAD)
                    act.wait_ge(unit_used, g.through(b))
                    if i // 2:
                        act.wait_ge(z_used, i // 2)
                    AC(zt[:], ps[:, 0:2, :], ACT.Silu).then_inc(z_done, 1)
                else:
                    split_to(U["z"] + i + AHEAD)
            act.wait_ge(y_turned, 1)
            AC(xh[:].rearrange("p k n -> p (k n)"), ps[:, 4:8, :].rearrange("p b n -> p (b n)"), ACT.Copy)\
                .then_inc(yh_done, 1)
            split_to(U["in0"] + 1)
            for i in range(2):
                b = B["nsa_out"] + i
                evac(b, tok[:, :, i * NB:(i + 1) * NB])
                act.wait_ge(banks_free[b % 2], g.freed(b))
            for i in range(NT):
                ins = AC(ob[:, i, :], tok[:, i, :], ACT.Square, accum_out=st[:, 4 + i:5 + i])
            step(ins)
            AC(st[:, 6:8], st[:, 4:6], ACT.Sqrt, scale=1.0 / D, bias=epst[:, 0:1]).then_inc(post_root, 1)

            def ffn(nt, ub, bb, fb, high, first_extra=None, last_extra=None):
                def turn(f):
                    act.wait_ge(hidden_turned, g.at(hidden_turned, fb + f + 1))
                    src = ps[:, 4:6, :].rearrange("p t (k n) -> p k t n", k=KU) if nt == 2 else \
                        ps[:, 6 + f % 2, :].rearrange("p (k n) -> p k n", k=KU)
                    dst = high[:, f * KU:(f + 1) * KU, :]
                    if nt == 2:
                        dst = dst.rearrange("p k (t n) -> p k t n", t=NT)
                    AC(dst, src, ACT.Copy).then_inc(hidden_high, 1)

                for f in range(NFB):
                    b = bb + 2 * f
                    split_to(ub + 4 * f + 1 + AHEAD)
                    act.wait_ge(unit_used, g.through(b))
                    act.wait_ge(banks_free[(b - 1) % 2], g.freed(b - 1))
                    AC(gt[:, 0:nt, :], ps[:, pair(b):pair(b) + nt, :], ACT.Silu).then_inc(banks_free[b % 2], 1)
                    if f:
                        turn(f - 1)
                    elif first_extra:
                        first_extra()
                    split_to(ub + 4 * f + 3 + AHEAD)
                if nt == 1:
                    split_to(ub + 4 * NFB + 1 + AHEAD)
                turn(NFB - 1)
                if last_extra:
                    split_to(ub + 4 * NFB + 5 + AHEAD)
                    last_extra()
                split_to(ub + UNITS_ROUND - 1 + AHEAD)

            def mix(i):
                split_to(U[f"in{i}"] + 1)
                turned_high(3 * i + 1)
                ib, iu = B[f"in{i}"], U[f"in{i}"]
                for j in range(2):
                    split_to(iu + 2 * j + 1 + AHEAD)
                    evac(ib + j, qk[:, j])
                    act.wait_ge(qk_squares, 2 * i + j + 1)
                    AC(qk_ss[:, j], qk_ss[:, j], ACT.Sqrt, scale=1.0 / DH, bias=epst[:, 0:1])\
                        .then_inc(qk_root, 1)
                split_to(iu + 5 + AHEAD)
                evac(ib + 2, v2[:])
                split_to(iu + 7 + AHEAD)
                evac(ib + 3, flat(uT[:]), flat(both(ib + 3)))
                split_to(iu + 9 + AHEAD)
                split_to(iu + 11 + AHEAD)
                for hb in range(2):
                    n = 2 * i + hb
                    act.wait_ge(z_scores, n + 1)
                    if n:
                        act.wait_ge(sp_done, n)
                    step(AC(spa[:], ps[:, 4:8, 0:3 * P], ACT.Abs))
                    step(AC(spa[:], spa[:], ACT.Exp, scale=-1.0))
                    AC(spa[:], spa[:], ACT.Ln, bias=ones[:, 0:1]).then_inc(ln_done, 1)
                    act.wait_ge(stick_done, n + 1)
                    if n:
                        act.wait_ge(pv_done, n)
                    AC(wT[:], ps[:, 4:8, 0:3 * P], ACT.Exp).then_inc(stick_exp, 1)
                b = B[f"oT{i}"]
                act.wait_ge(pv_done, 2 * i + 2)
                AC(flat(mixT[:, 0:4, :]), flat(both(b)), ACT.Copy).then_inc(banks_free[b % 2], 1)
                act.wait_ge(banks_free[b % 2], g.freed(b))
                act.wait_ge(banks_free[(ib + 5) % 2], g.freed(ib + 5))
                AC(mixs[:], mixT[:], ACT.Square).then_inc(mix_squares, 1)
                act.wait_ge(mix_sums, i + 1)
                AC(rn[:], ps[:, 4:6, 0:S], ACT.Sqrt, scale=1.0 / NB, bias=epst[:, 0:1])\
                    .then_inc(mix_root, 1)
                act.wait_ge(mix_normed, i + 1)
                AC(xh[:], mixT[:], ACT.Copy).then_inc(mixh_done, 1)
                split_to(U[f"o{i}"] + 3 + AHEAD)
                act.wait_ge(banks_free[(B[f"o{i}"]) % 2], g.freed(B[f"o{i}"]))
                act.wait_ge(banks_free[(B[f"o{i}"] + 1) % 2], g.freed(B[f"o{i}"] + 1))
                norm(3 * i + 2)

            def ple(i):
                ub, bb = U[f"ple{i}"], B[f"ple{i}"]
                split_to(ub + 1)
                turned_high(3 * i + 3)
                act.wait_ge(p_turned, i + 1)
                AC(flat(ptTh[:]), ps[:, 4, :], ACT.Copy).then_inc(ph_done, 1)
                for j in range(2):
                    split_to(min(ub + 2 * j + 1 + AHEAD, ub + 5))
                    b = bb + j
                    evac(b, pg[:, j], func=ACT.Sigmoid)
                if i == 0:
                    split_to(ub + 6 + 1)
                else:
                    split_to(ub + 5)

            act.wait_ge(post_added, 1)
            norm(1)
            mix(0)
            split_to(U["ffn0"] + 1)
            turned_high(2)
            ffn(2, U["ffn0"], B["ffn0"], 0, hTh)
            act.wait_ge(dense_added, 1)
            norm(3)
            ple(0)
            act.wait_ge(h_half, 2)
            norm(4)
            mix(1)
            split_to(U["ffn1"] + 1)
            turned_high(5)
            act.wait_ge(router_loaded, 16)
            AC(rwh[:], rw[:], ACT.Copy).then_inc(router_high, 1)
            AC(xnh[:], tok[:], ACT.Copy).then_inc(xn_high, 1)
            act.wait_ge(logit_shift, 1)
            AC(gw[:], gw[:], ACT.Exp).then_inc(gate_exp, 1)

            def split_gathered(n):
                act.wait_ge(gathered, g.at(gathered, n + 1))
                for j in range(KD):
                    ins = AC(xgh[:, j, :], ps[:, 6 + j // 4, (j % 4) * P:(j % 4 + 1) * P], ACT.Copy,
                             scale=gains[:, 5, j:j + 1])
                ins.then_inc(gather_high, 1)

            split_gathered(0)
            act.wait_ge(rounds_known, 1)
            rounds = act.value_load(nround[0:1, 0:1], min_val=NE, max_val=2 * NE)
            with act.Fori(0, rounds) as r:
                g.r = r

                def copy_pick():
                    act.wait_ge(pick_turned, g.at(pick_turned, 1))
                    AC(pickT[:], ps[:, 6, 0:2 * P].rearrange("p (t n) -> p t n", t=NT), ACT.Copy)\
                        .then_inc(pick_copied, 1)
                ffn(1, U["ffn1"], B["ffn1"], NFB, mTh, copy_pick, lambda: split_gathered(1))
                act.wait_ge(unit_used, g.at(unit_used, U["ffn1"] + UNITS_ROUND))
                AC(yh[:], ps[:, 4:6, :].rearrange("p b n -> p (b n)"), ACT.Copy).then_inc(y_high, 1)
                assert g.split == U["ffn1"] + UNITS_ROUND + 2
            g.r = rounds
            g.split = U["ffn1"] + 2
            g.post = True
            act.wait_ge(round_done, g.at(round_done, 1))
            norm(6)
            ple(1)

        @block_.vector
        def _(dve):
            g = Prog()

            def step(ins):
                g.n += 1
                ins.then_inc(dve_step, 1)
                dve.wait_ge(dve_step, g.n)

            V = nc.vector

            def split_to(u):
                while g.split <= u:
                    v = g.split
                    n = unit_columns(v, g.post)
                    dve.wait_ge(high_done, g.at(high_done, v + 1))
                    V.tensor_tensor(wlo[:, v % SPL, 0:n], raw[:, v % RAW, 0:n],
                                    whi[:, v % SPL, 0:n].bitcast(F32), ALU.subtract)\
                        .then_inc(low_done, 1)
                    g.split += 1

            def norm(k):
                dve.wait_ge(root_done, k + 1)
                step(V.reciprocal(st[:, 8:10], st[:, 2:4]))
                for i in range(NT):
                    ins = V.tensor_scalar(tok[:, i, :], h[:, i, :], st[:, 8 + i:9 + i], None, ALU.mult)
                ins.then_inc(h_normed, 1)

            def turned_low(k):
                dve.wait_ge(xh_done, k + 1)
                for j in range(KD):
                    ins = V.scalar_tensor_tensor(out=xl[:, j, :], in0=ps[:, 4 + j // 2, (j % 2) * S:(j % 2 + 1) * S],
                                                 scalar=gains[:, k, j:j + 1], in1=xh[:, j, :].bitcast(F32),
                                                 op0=ALU.mult, op1=ALU.subtract)
                ins.then_inc(xl_done, 1)

            dve.wait_ge(tab_product, 2)
            V.tensor_copy(cbias[:].rearrange("p t h c -> p t c h"),
                          ps[:, 1, 0:NT * NC_ * NH].rearrange("p (t c h) -> p t c h", t=NT, c=NC_))\
                .then_inc(cbias_done, 1)
            dve.wait_ge(cbias_done, 1)
            norm(0)
            split_to(1)
            turned_low(0)
            split_to(U["q"] + 1)
            split_to(U["q"] + 5)
            V.memset(xw[:, XW:XT], 0.0)
            dve.wait_ge(kc_turned, 1)
            dve.wait_ge(cmp_loaded, 16 * 5)
            for kv in range(2):
                for s in range(2):
                    q = slice(s * DH, (s + 1) * DH)
                    src = ps[q, 4 + 2 * kv:6 + 2 * kv, :].rearrange("p b n -> p (b n)")
                    src = src.rearrange("p (g c m s) -> p s m g c", g=NG, m=CS // 2, s=2)
                    for half in range(2):
                        ins = V.tensor_tensor(
                            xw[q, 0:XW].rearrange("p (v m g c) -> p v m g c", v=2, m=CB // 2, g=NG)[:, kv, 8 * half:8 * half + 8],
                            src[:, s, :, :, half:half + NC_],
                            pos2[q, kv, 8 * half:8 * half + 8].unsqueeze(2).unsqueeze(3)
                            .broadcast_to([DH, 8, NG, NC_]), ALU.add)
            ins.then_inc(windows_done, 1)
            dve.wait_ge(window_high, 1)
            V.tensor_tensor(xwl[:], xw[:], xwh[:].bitcast(F32), ALU.subtract).then_inc(window_low, 1)
            split_to(U["kv_w"] + 3)
            split_to(U["cmp"] + 3 + 2)
            dve.wait_ge(hc_turned, 1)
            step(V.tensor_copy(hcT[:].rearrange("p a j n -> p (a j n)"), ps[:, 4, 0:4 * NG * NC_]))
            dve.wait_ge(rev_stored, 16)
            for half in range(2):
                for j in range(2):
                    ins = V.tensor_copy(
                        hcR[:, half, j, :].rearrange("p (g r c) -> p g r c", g=2, r=RG),
                        hcT[:, 1, j, 2 * half * NC_:(2 * half + 2) * NC_].rearrange("p (g c) -> p g c", g=2)
                        .unsqueeze(2).broadcast_to([P, 2, RG, NC_]))
            ins.then_inc(hcT_done, 1)
            dve.wait_ge(kcvc_product, 1)
            V.tensor_copy(kcT[:], ps[:, 5, 0:NG * NC_]).then_inc(kcT_done, 1)
            for half in range(2):
                ins = V.tensor_tensor(
                    vcb[:, half], ps[0:8 * NC_, 6, half * DH:(half + 1) * DH].unsqueeze(1)
                    .broadcast_to([8 * NC_, 8, DH]),
                    bdiag[0:8 * NC_, :].unsqueeze(2).broadcast_to([8 * NC_, 8, DH]), ALU.mult)
            ins.then_inc(vcb_done, 1)
            dve.wait_ge(cmp_scores, 1)
            for j in range(2):
                ins = V.tensor_tensor(
                    lc[:].rearrange("p t (i j) c -> p j t i c", j=2)[:, j],
                    ps[:, 4 + j, 0:NT * 8 * NC_].rearrange("p (t i c) -> p t i c", t=NT, i=8),
                    cbias[:].rearrange("p t (i j) c -> p j t i c", j=2)[:, j], ALU.add)
            step(ins)
            lcv = lc[:].rearrange("p t h c -> p (t h) c")
            step(V.tensor_reduce(cst[:, 0, :], lcv, AX, ALU.max))
            step(V.tensor_scalar(cst[:, 0, :], cst[:, 0, :], MASKED / 16, None, ALU.max))
            V.tensor_tensor(lcv, lcv, cst[:, 0, :].unsqueeze(2).broadcast_to([P, NT * NH, NC_]), ALU.subtract)\
                .then_inc(cmp_logits, 1)
            dve.wait_ge(cmp_exp, 1)
            step(V.tensor_reduce(cst[:, 1, :], lcv, AX, ALU.add))
            step(V.tensor_scalar(cst[:, 1, :], cst[:, 1, :], 1e-30, None, ALU.max))
            step(V.reciprocal(cst[:, 2, :], cst[:, 1, :]))
            step(V.tensor_tensor(cst[:, 2, :].rearrange("p (t h) -> p t h", t=NT),
                                   cst[:, 2, :].rearrange("p (t h) -> p t h", t=NT), gate[:, :, 0:NH], ALU.mult))
            dve.wait_ge(lc_turned, 1)
            V.tensor_copy(lcT[:], ps[0:8 * NC_, 4, :].rearrange("p (a n) -> p a n", n=P)).then_inc(lcT_done, 1)
            dve.wait_ge(cmp_out, 1)
            for half in range(2):
                for T in range(NT):
                    src = ps[:, [5, 6, 7, 2][half * 2 + T], :]
                    a0 = T * NH + half * 8
                    ins = V.tensor_tensor(
                        ob[:, T, half * NB:(half + 1) * NB].rearrange("p (h d) -> p h d", d=DH),
                        src.rearrange("p (h d) -> p h d", d=DH),
                        cst[:, 2, a0:a0 + 8].unsqueeze(2).broadcast_to([P, 8, DH]), ALU.mult)
            ins.then_inc(o_evac, 1)
            dve.wait_ge(o_evac, 1)
            dve.wait_ge(bias_loaded, 16)

            def att(i):
                if i < 16:
                    T, half = (i // 2) % 2, (i // 4) % 2
                    grp = 2 * half + i % 2
                    nk = (T + 1) * P
                    dve.wait_ge(scores_done, i + 1)
                    if i >= 2:
                        dve.wait_ge(p_turned_all, i - 1)
                    for r in range(RG):
                        hh = grp * RG + r
                        bank = 4 + 2 * (i % 2) + r % 2
                        ins = V.tensor_tensor_reduce(
                            sg[:, i % 2, r, 0:nk], ps[:, bank, (r // 2) * S:(r // 2) * S + nk],
                            bias[:, hh, S - nk:S], 1.0, MASKED, ALU.add, ALU.max, ast_[:, i, 0, r:r + 1])
                    step(ins)
                    V.tensor_scalar(ast_[:, i, 1, :], ast_[:, i, 0, :], -SC, None, ALU.mult)\
                        .then_inc(logits_done, 1)
                if 1 <= i < 17:
                    k = i - 1
                    T = (k // 2) % 2
                    dve.wait_ge(p_turned_all, k + 1)
                    if k >= 2:
                        dve.wait_ge(pv_step, k - 1)
                    src = ps[:, 4 + 2 * (k % 2):6 + 2 * (k % 2), :].rearrange(
                        "p b (r t n) -> p (b r) t n", r=2, t=NT)
                    V.tensor_copy(pT[:, k % 2, :, 0:T + 1, :], src[:, :, 0:T + 1, :]).then_inc(pT_done, 1)
                if i >= 2 and (i - 2) % 2:
                    k = i - 2
                    T, half, br = (k // 2) % 2, (k // 4) % 2, k // 8
                    dve.wait_ge(pv_step, k + 1)
                    dve.wait_ge(exp_done, k + 1)
                    for s in (1, 0):
                        ins = V.reciprocal(grow[:, T, half * 8 + 4 * (1 - s):half * 8 + 4 * (1 - s) + 4],
                                           ast_[:, k - s, 2, :])
                    step(ins)
                    gs = grow[:, T, half * 8:half * 8 + 8]
                    step(V.tensor_tensor(gs, gs, gate[:, T, (br + 1) * NH + half * 8:(br + 1) * NH + half * 8 + 8],
                                           ALU.mult))
                    V.tensor_tensor(
                        ob[:, T, half * NB:(half + 1) * NB].rearrange("p (h d) -> p h d", d=DH),
                        ps[:, 2 + (k // 2) % 2, :].rearrange("p (h d) -> p h d", d=DH),
                        gs.unsqueeze(2).broadcast_to([P, 8, DH]), ALU.mult).then_inc(o_evac, 1)

            for kind, i in NSA_ORDER:
                if kind == "a":
                    att(i)
                    continue
                split_to(U["z"] + i + AHEAD)
                if i % 2:
                    n = i // 2
                    br, half = n // 2, n % 2
                    dve.wait_ge(z_done, n + 1)
                    dve.wait_ge(o_evac, max(1, 2 * (n - 1) + 1))
                    c = slice(half * NB, (half + 1) * NB)
                    if br == 0:
                        V.tensor_tensor(y[:, :, c], zt[:], ob[:, :, c], ALU.mult).then_inc(z_used, 1)
                    else:
                        step(V.tensor_tensor(ob[:, :, c], zt[:], ob[:, :, c], ALU.mult))
                        V.tensor_tensor(y[:, :, c], y[:, :, c], ob[:, :, c], ALU.add).then_inc(z_used, 1)
                    dve.wait_ge(z_used, n + 1)
            dve.wait_ge(yh_done, 1)
            V.tensor_tensor(xl[:].rearrange("p k n -> p (k n)"), ps[:, 4:8, :].rearrange("p b n -> p (b n)"),
                            xh[:].rearrange("p k n -> p (k n)").bitcast(F32), ALU.subtract)\
                .then_inc(yl_done, 1)
            split_to(U["in0"] + 1)
            dve.wait_ge(post_root, 1)
            step(V.reciprocal(st[:, 10:12], st[:, 6:8]))
            dve.wait_ge(postg_loaded, 16)
            for i in range(NT):
                ins = V.scalar_tensor_tensor(out=tok[:, i, :], in0=tok[:, i, :], scalar=st[:, 10 + i:11 + i],
                                             in1=postg[:], op0=ALU.mult, op1=ALU.mult)
            step(ins)
            V.tensor_tensor(h[:], h[:], tok[:], ALU.add).then_inc(post_added, 1)

            def ffn(nt, ub, bb, fb, high, low, extra=None, late=None):
                def turn(f):
                    dve.wait_ge(hidden_high, g.at(hidden_high, fb + f + 1))
                    src = ps[:, 4:6, :].rearrange("p t (k n) -> p k t n", k=KU) if nt == 2 else \
                        ps[:, 6 + f % 2, :].rearrange("p (k n) -> p k n", k=KU)
                    hi, lo = high[:, f * KU:(f + 1) * KU, :], low[:, f * KU:(f + 1) * KU, :]
                    if nt == 2:
                        for T in range(NT):
                            ins = V.tensor_tensor(lo[:, :, T * P:(T + 1) * P], src[:, :, T, :],
                                                  hi[:, :, T * P:(T + 1) * P].bitcast(F32), ALU.subtract)
                    else:
                        ins = V.tensor_tensor(lo, src, hi.bitcast(F32), ALU.subtract)
                    ins.then_inc(hidden_low, 1)

                for f in range(NFB):
                    b = bb + 2 * f + 1
                    split_to(ub + 4 * f + 3 + AHEAD)
                    dve.wait_ge(unit_used, g.through(b))
                    dve.wait_ge(banks_free[(b - 1) % 2], g.freed(b - 1))
                    if fb + f:
                        dve.wait_ge(hidden_turned, g.at(hidden_turned, fb + f))
                    V.tensor_tensor(ht[:, 0:nt, :], gt[:, 0:nt, :], ps[:, pair(b):pair(b) + nt, :], ALU.mult).then_inc(banks_free[b % 2], 1)
                    if f < NFB - 1:
                        split_to(ub + 4 * (f + 1) + 1 + AHEAD)
                        turn(f)
                if nt == 1:
                    split_to(ub + 4 * NFB + 1 + AHEAD)
                turn(NFB - 1)
                if extra:
                    split_to(ub + 4 * NFB + 5 + AHEAD)
                    extra()
                split_to(ub + UNITS_ROUND - 1 + AHEAD)
                if late:
                    late()

            def mix(i):
                split_to(U[f"in{i}"] + 1)
                turned_low(3 * i + 1)
                ib, iu = B[f"in{i}"], U[f"in{i}"]
                V.memset(cu[:, :, 0:2], 0.0)
                for j in range(2):
                    split_to(iu + 2 * j + 1 + AHEAD)
                    dve.wait_ge(banks_free[(ib + j) % 2], g.freed(ib + j))
                    step(V.tensor_tensor(sq[:], qk[:, j], qk[:, j], ALU.mult))
                    V.tensor_reduce(qk_ss[:, j].rearrange("p t h -> p (t h)"),
                                    sq[:].rearrange("p t (h d) -> p (t h) d", d=DH), AX, ALU.add)\
                        .then_inc(qk_squares, 1)
                    dve.wait_ge(qk_root, 2 * i + j + 1)
                    step(V.reciprocal(qk_ss[:, j], qk_ss[:, j]))
                    v = qk[:, j].rearrange("p t (h d) -> p (t h) d", d=DH)
                    V.tensor_tensor(v, v, qk_ss[:, j].rearrange("p t h -> p (t h)").unsqueeze(2)
                                    .broadcast_to([P, NT * SH, DH]), ALU.mult).then_inc(qk_normed, 1)
                split_to(iu + 5 + AHEAD)
                dve.wait_ge(qk_turned, i + 1)
                dve.wait_ge(mix_loaded, 16 * 20)
                V.tensor_scalar(qkT[:, 0].rearrange("p k n -> p (k n)"), ps[:, 4:6, :].rearrange("p b n -> p (b n)"),
                                qkg[:, i, 0:1], SC, ALU.mult, ALU.mult)
                V.tensor_scalar(qkT[:, 1].rearrange("p k n -> p (k n)"), ps[:, 6:8, :].rearrange("p b n -> p (b n)"),
                                qkg[:, i, 1:2], None, ALU.mult).then_inc(qkT_done, 1)
                split_to(iu + 9 + AHEAD)
                b = ib + 4
                dve.wait_ge(banks_free[(ib + 3) % 2], g.freed(ib + 3))
                dve.wait_ge(unit_used, g.through(b))
                V.tensor_tensor(cu[:, :, 2:S + 2],
                                ps[:, pair(b):pair(b) + 2, :].rearrange("p b (k n) -> p (b k) n", n=S),
                                uT[:], ALU.mult).then_inc(banks_free[b % 2], 1)
                dve.wait_ge(banks_free[b % 2], g.freed(b))
                for j in range(4):
                    ins = V.tensor_scalar(cv[:, j, :], cu[:, j, 0:S], convw[:, i, j, 0:1], convw[:, i, j, 3:4],
                                          ALU.mult, ALU.add)
                step(ins)
                for k in (1, 2):
                    for j in range(4):
                        ins = V.scalar_tensor_tensor(out=cv[:, j, :], in0=cu[:, j, k:k + S],
                                                     scalar=convw[:, i, j, k:k + 1], in1=cv[:, j, :],
                                                     op0=ALU.mult, op1=ALU.add)
                    step(ins)
                split_to(iu + 11 + AHEAD)
                b = ib + 5
                dve.wait_ge(unit_used, g.through(b))
                V.tensor_tensor(mixT[:, 4:8, :],
                                ps[:, pair(b):pair(b) + 2, :].rearrange("p b (k n) -> p (b k) n", n=S),
                                cv[:], ALU.mult).then_inc(banks_free[b % 2], 1)
                for hb in range(2):
                    n = 2 * i + hb
                    dve.wait_ge(z_scores, n + 1)
                    if n:
                        dve.wait_ge(stick_done, n)
                    dve.wait_ge(ln_done, n + 1)
                    step(V.scalar_tensor_tensor(out=spb[:], in0=ps[:, 4:8, 0:3 * P], scalar=0.0, in1=spa[:],
                                                  op0=ALU.max, op1=ALU.add))
                    for c in (0, 2 * P):
                        ins = V.tensor_tensor(spb[:, :, c:c + P], spb[:, :, c:c + P],
                                              keep.unsqueeze(1).broadcast_to([P, 4, P]), ALU.mult)
                    ins.then_inc(sp_done, 1)
                dve.wait_ge(mix_root, i + 1)
                step(V.reciprocal(rn[:], rn[:]))
                for j in range(8):
                    ins = V.scalar_tensor_tensor(out=mixT[:, j, :], in0=mixT[:, j, :], scalar=ogain[:, i, j:j + 1],
                                                 in1=rn[:, j // 4, :], op0=ALU.mult, op1=ALU.mult)
                ins.then_inc(mix_normed, 1)
                dve.wait_ge(mixh_done, i + 1)
                V.tensor_tensor(xl[:], mixT[:], xh[:].bitcast(F32), ALU.subtract).then_inc(mixl_done, 1)
                for j in range(2):
                    split_to(U[f"o{i}"] + 2 * j + 1 + AHEAD)
                    b = B[f"o{i}"] + j
                    dve.wait_ge(unit_used, g.through(b))
                    c = slice(j * NB, (j + 1) * NB)
                    V.tensor_tensor(h[:, :, c], h[:, :, c], ps[:, pair(b):pair(b) + 2, :], ALU.add).then_inc(banks_free[b % 2], 1)

            def ple(i):
                ub, bb = U[f"ple{i}"], B[f"ple{i}"]
                split_to(ub + 1)
                turned_low(3 * i + 3)
                dve.wait_ge(ph_done, i + 1)
                V.tensor_tensor(ptTl[:].rearrange("p k n -> p (k n)"), ps[:, 4, :],
                                ptTh[:].rearrange("p k n -> p (k n)").bitcast(F32), ALU.subtract)\
                    .then_inc(pl_done, 1)
                for j in range(2):
                    split_to(min(ub + 2 * j + 1 + AHEAD, ub + 5))
                if i == 0:
                    split_to(ub + 7)
                else:
                    split_to(ub + 5)
                for j in range(2):
                    b = bb + 2 + j
                    dve.wait_ge(banks_free[(b - 2) % 2], g.freed(b - 2))
                    dve.wait_ge(unit_used, g.through(b))
                    if i or j:
                        dve.wait_ge(h_half, 2 * i + j)
                    V.tensor_tensor(pm[:], ps[:, pair(b):pair(b) + 2, :], pg[:, j], ALU.mult).then_inc(banks_free[b % 2], 1)
                    dve.wait_ge(banks_free[b % 2], g.freed(b))
                    c = slice(j * NB, (j + 1) * NB)
                    V.tensor_tensor(h[:, :, c], h[:, :, c], pm[:], ALU.add).then_inc(h_half, 1)
                dve.wait_ge(h_half, 2 * i + 2)

            norm(1)
            mix(0)
            norm(2)
            split_to(U["ffn0"] + 1)
            turned_low(2)

            def add_dense():
                dve.wait_ge(unit_used, g.at(unit_used, U["ple0"]))
                V.tensor_tensor(h[:], h[:], ps[:, 4:8, :].rearrange("p (t b) n -> p t (b n)", t=NT), ALU.add)\
                    .then_inc(dense_added, 1)
            ffn(2, U["ffn0"], B["ffn0"], 0, hTh, hTl, late=add_dense)
            norm(3)
            ple(0)
            norm(4)
            mix(1)
            norm(5)
            split_to(U["ffn1"] + 1)
            turned_low(5)
            dve.wait_ge(router_high, 1)
            V.tensor_tensor(rwl[:], rw[:], rwh[:].bitcast(F32), ALU.subtract).then_inc(router_low, 1)
            dve.wait_ge(xn_high, 1)
            V.tensor_tensor(xnl[:], tok[:], xnh[:].bitcast(F32), ALU.subtract).then_inc(xn_low, 1)
            dve.wait_ge(router_logits, 1)
            step(V.tensor_copy(lg[:], ps[:, 0, 0:NT * NE].rearrange("p (t e) -> p t e", t=NT)))
            other = lg[:].unsqueeze(2).broadcast_to([P, NT, NE, NE])
            own = lg[:].unsqueeze(3).broadcast_to([P, NT, NE, NE])
            for T in range(NT):
                V.tensor_tensor(cmpa[:, T], other[:, T], own[:, T], ALU.is_gt)
                ins = V.tensor_tensor(cmpb[:, T], other[:, T], own[:, T], ALU.is_equal)
            step(ins)
            for T in range(NT):
                ins = V.tensor_tensor(cmpb[:, T], cmpb[:, T], tril8.rearrange("p (a b) -> p a b", a=NE), ALU.mult)
            step(ins)
            step(V.tensor_tensor(cmpa[:], cmpa[:], cmpb[:], ALU.add))
            step(V.tensor_reduce(sel[:].rearrange("p t e -> p (t e)"),
                                   cmpa[:].rearrange("p t a b -> p (t a) b"), AX, ALU.add))
            V.tensor_scalar(sel[:], sel[:], 2.0, None, ALU.is_lt).then_inc(sel_done, 1)
            dve.wait_ge(sel_done, 1)
            step(V.tensor_reduce(st[:, 12:14], lg[:], AX, ALU.max))
            for T in range(NT):
                ins = V.tensor_scalar(gw[:, T], lg[:, T], st[:, 12 + T:13 + T], None, ALU.subtract)
            ins.then_inc(logit_shift, 1)
            dve.wait_ge(gate_exp, 1)
            step(V.tensor_tensor(gw[:], gw[:], sel[:], ALU.mult))
            step(V.tensor_reduce(st[:, 14:16], gw[:], AX, ALU.add))
            step(V.reciprocal(st[:, 16:18], st[:, 14:16]))
            for T in range(NT):
                ins = V.tensor_scalar(gw[:, T], gw[:, T], st[:, 16 + T:17 + T], None, ALU.mult)
            step(ins)
            dve.wait_ge(slots_counted, 1)
            V.tensor_scalar(slot[:, :, 0:NE], ps[:, 1, 0:NT * NE].rearrange("p (t e) -> p t e", t=NT), 1.0, None,
                            ALU.add)
            step(V.tensor_reduce(cnt[:, NE:NE + 1], ps[:, 1, NT * NE:NT * NE + NE], AX, ALU.max))
            step(V.tensor_tensor(slot[:, :, 0:NE], slot[:, :, 0:NE], sel[:], ALU.mult))
            step(V.tensor_scalar(slot[:, :, 0:NE], slot[:, :, 0:NE], 1.0, None, ALU.subtract))
            V.tensor_scalar(slot[:, :, NE:2 * NE], slot[:, :, 0:NE], float(P), None, ALU.subtract)
            V.memset(slot[:, :, 2 * NE:2 * NE + 1], -1.0)
            step(V.tensor_scalar(cnt[:, NE + 1:NE + 2], cnt[:, NE:NE + 1], float(P), float(NE), ALU.is_gt, ALU.mult))
            step(V.tensor_scalar(cnt[:, NE + 2:NE + 3], cnt[:, NE + 1:NE + 2], float(NE), None, ALU.add))
            V.tensor_copy(nround[:], cnt[0:1, NE + 2:NE + 3]).then_inc(rounds_known, 1)

            def make_pick(col, n):
                if n:
                    dve.wait_ge(pick_turned, g.at(pick_turned, n))
                for T in range(NT):
                    ins = V.tensor_scalar(pick[:, T, :], iota, slot[:, T, col], None, ALU.is_equal)
                ins.then_inc(pick_done, 1)

            def split_gathered(n):
                dve.wait_ge(gather_high, g.at(gather_high, n + 1))
                for j in range(KD):
                    ins = V.scalar_tensor_tensor(
                        out=xgl[:, j, :], in0=ps[:, 6 + j // 4, (j % 4) * P:(j % 4 + 1) * P],
                        scalar=gains[:, 5, j:j + 1], in1=xgh[:, j, :].bitcast(F32), op0=ALU.mult,
                        op1=ALU.subtract)
                ins.then_inc(gather_low, 1)

            dve.wait_ge(rounds_known, 1)
            make_pick(slice(0, 1), 0)
            V.memset(st[:, 20:21], 0.0).then_inc(round_done, 1)
            split_gathered(0)
            rounds = dve.value_load(nround[0:1, 0:1], min_val=NE, max_val=2 * NE)
            with dve.Fori(0, rounds) as r:
                g.r = r
                e = r % NE

                def next_tokens():
                    make_pick(bass.ds(r + 1, 1), 1)
                    split_gathered(1)
                ffn(1, U["ffn1"], B["ffn1"], NFB, mTh, mTl, extra=next_tokens)
                dve.wait_ge(y_high, g.at(y_high, 1))
                V.tensor_tensor(yl[:], ps[:, 4:6, :].rearrange("p b n -> p (b n)"), yh[:].bitcast(F32),
                                ALU.subtract).then_inc(y_low, 1)
                dve.wait_ge(scatter_done, g.at(scatter_done, 1))
                for T in range(NT):
                    ins = V.scalar_tensor_tensor(
                        out=h[:, T, :], in0=ps[:, (6 if T == 0 else 4):(8 if T == 0 else 6), :]
                        .rearrange("p b n -> p (b n)"),
                        scalar=gw[:, T, bass.ds(e, 1)], in1=h[:, T, :], op0=ALU.mult, op1=ALU.add)
                ins.then_inc(round_done, 1)
                dve.wait_ge(round_done, g.at(round_done, 2))
            g.r = rounds
            g.split = U["ffn1"] + 2
            g.post = True
            norm(6)
            ple(1)

        @block_.tensor
        def _(pe):
            g = Prog()
            mm = nc.tensor.matmul

            def turn(dst, src, idn=None):
                return nc.tensor.transpose(dst, src, ident if idn is None else idn)

            def split_view(u, nk, n):
                s = u % SPL
                return (whi[:, s, 0:nk * n].rearrange("p (k n) -> p k n", k=nk),
                        wlo[:, s, 0:nk * n].rearrange("p (k n) -> p k n", k=nk))

            def products(u, nk, n, hi, lo, k0, outs, first, last, only=True, final=True):
                wh, wl = split_view(u, nk, n)
                pe.wait_ge(low_done, g.at(low_done, u + 1))
                for k in range(nk):
                    for T, o in enumerate(outs):
                        a, b = hi(k0 + k, T), lo(k0 + k, T)
                        mm(o, a, wh[:, k, :], start=first and k == 0, stop=False)
                        mm(o, a, wl[:, k, :], start=False, stop=False)
                        ins = mm(o, b, wh[:, k, :], start=False, stop=last and k == nk - 1)
                ins.then_inc(unit_used, 1)
                return ins

            def tile_of(x):
                return lambda k, T: x[:, k, T * P:(T + 1) * P]

            def block(u, b, hi, lo, kt=KD, n=NB, m=P, nt=NT, fixed=None, units=None):
                bank = pair(b) if fixed is None else fixed
                outs = [ps[0:m, bank + T, 0:n] for T in range(nt)]
                start_block(b)
                ku = units or KU
                nu = -(-kt // ku)
                for i in range(nu):
                    products(u + i, min(ku, kt - i * ku), n, hi, lo, i * ku, outs, i == 0, i == nu - 1)

            def start_block(b):
                back = b - 2 if b - 2 not in z_blocks else B["z"] - (2 if (b - B["z"]) % 2 == 0 else 1)
                if back >= 0:
                    pe.wait_ge(banks_free[back % 2], g.freed(back))

            def turn_h(k, src=None):
                src = tok if src is None else src
                for j in range(KD):
                    for T in range(NT):
                        ins = turn(ps[:, 4 + j // 2, (j % 2) * S + T * P:(j % 2) * S + (T + 1) * P],
                                   src[:, T, j * P:(j + 1) * P])
                return ins

            def normed(k):
                pe.wait_ge(h_normed, k + 1)
                turn_h(k).then_inc(h_turned, 1)

            pe.wait_ge(con_loaded, 16)
            pe.wait_ge(oh_loaded, 32)
            pe.wait_ge(table_one, 1)
            mm(ps[0:NH, 0, 0:LREV], tabx[:], oh[:, 512:512 + LREV], start=True, stop=True)\
                .then_inc(tab_product, 1)
            for T in range(NT):
                for c in range(NC_):
                    i0 = 256 + P * T - CS * c - (CB - 1)
                    o = (T * NC_ + c) * NH
                    ins = mm(ps[:, 1, o:o + NH], oh[:, i0:i0 + P], tabx[:], start=True, stop=True)
            ins.then_inc(tab_product, 1)
            normed(0)
            pe.wait_ge(rev_ready, 1)
            pe.wait_ge(cbias_done, 1)
            pe.wait_ge(xl_done, 1)
            X = (tile_of(xh), tile_of(xl))
            block(U["kv_c"], B["kv_c"], *X)
            block(U["q"], B["q"], *X)
            pe.wait_ge(banks_free[(B["kv_c"]) % 2], g.freed(B["kv_c"]))
            for a in range(2 * NG):
                for T in range(NT):
                    ins = turn(ps[:, 4 + a // 2, (a % 2) * S + T * P:(a % 2) * S + (T + 1) * P],
                               kc2[:, T, a].rearrange("p s d -> p (s d)"))
            ins.then_inc(kc_turned, 1)
            block(U["q"] + 2, B["q"] + 1, *X)
            block(U["kv_s"], B["kv_s"], *X)
            pe.wait_ge(banks_free[(B["q"]) % 2], g.freed(B["q"]))
            pe.wait_ge(banks_free[(B["q"] + 1) % 2], g.freed(B["q"] + 1))
            pe.wait_ge(windows_done, 1)
            turn_h(0).then_inc(q_turned, 1)
            block(U["kv_w"], B["kv_w"], *X)
            block(U["gate"], B["gate"], *X, n=3 * NH, units=KD)
            pe.wait_ge(banks_free[(B["kv_s"]) % 2], g.freed(B["kv_s"]))
            pe.wait_ge(banks_free[(B["kv_w"]) % 2], g.freed(B["kv_w"]))
            pe.wait_ge(qT_done, 1)
            for i in range(2):
                for a in range(NG):
                    for T in range(NT):
                        ins = turn(ps[:, 4 + 2 * i + a // 2, (a % 2) * S + T * P:(a % 2) * S + (T + 1) * P],
                                   kd[:, i, T, a].rearrange("p s d -> p (s d)"))
            ins.then_inc(k_turned, 1)
            pe.wait_ge(window_low, 1)
            for kv in range(2):
                def window(x, kv=kv):
                    return lambda k, T: x[:, (kv * CB // 2 + k) * NG * NC_:(kv * CB // 2 + k) * NG * NC_ + P]
                block(U["cmp"] + 2 * kv, B["cmp"] + kv, window(xwh), window(xwl), kt=CB // 2, n=HC, nt=1, units=8)
            pe.wait_ge(banks_free[(B["cmp"]) % 2], g.freed(B["cmp"]))
            pe.wait_ge(banks_free[(B["cmp"] + 1) % 2], g.freed(B["cmp"] + 1))
            pe.wait_ge(kT_done, 1)
            for kv in range(2):
                for j in range(2):
                    o = (kv * 2 + j) * NG * NC_
                    ins = turn(ps[:, 4, o:o + NG * NC_], hc[:, kv, j * P:(j + 1) * P],
                               ident[0:NG * NC_, 0:NG * NC_])
            ins.then_inc(hc_turned, 1)
            pe.wait_ge(hcT_done, 1)
            for j in range(2):
                mm(ps[:, 5, 0:NG * NC_], w2k[:, j].rearrange("p s d -> p (s d)"), hcT[:, 0, j, :],
                   start=j == 0, stop=j == 1)
            for half in range(2):
                for j in range(2):
                    ins = mm(ps[0:8 * NC_, 6, half * DH:(half + 1) * DH], hcR[:, half, j, :], w2v[:, j, :],
                             start=j == 0, stop=j == 1)
            ins.then_inc(kcvc_product, 1)
            pe.wait_ge(kcT_done, 1)
            for T in range(NT):
                for hh in range(NH):
                    q = slice((hh % 2) * DH, (hh % 2 + 1) * DH)
                    o = (T * 8 + hh // 2) * NC_
                    ins = mm(ps[:, 4 + hh % 2, o:o + NC_], qT[q, hh // 2, T * P:(T + 1) * P],
                             kcT[q, (hh // RG) * NC_:(hh // RG + 1) * NC_], start=True, stop=True)
            ins.then_inc(cmp_scores, 1)
            pe.wait_ge(cmp_exp, 1)
            for half in range(2):
                for T in range(NT):
                    a = half * 2 + T
                    ins = turn(ps[0:8 * NC_, 4, a * P:(a + 1) * P],
                               lc[:, T, half * 8:half * 8 + 8, :].rearrange("p h c -> p (h c)"))
            ins.then_inc(lc_turned, 1)
            pe.wait_ge(lcT_done, 1)
            pe.wait_ge(vcb_done, 1)
            for a in range(4):
                ins = mm(ps[:, [5, 6, 7, 2][a], :], lcT[:, a, :], vcb[:, a // 2].rearrange("p h d -> p (h d)"),
                         start=True, stop=True)
            ins.then_inc(cmp_out, 1)

            def att(i):
                if i >= 2:
                    k = i - 2
                    T, half, br = (k // 2) % 2, (k // 4) % 2, k // 8
                    grp = 2 * half + k % 2
                    pe.wait_ge(pT_done, k + 1)
                    if k % 2 == 0:
                        pe.wait_ge(o_evac, max(1, k // 2))
                    for r in range(RG):
                        o = ps[:, 2 + (k // 2) % 2, (k % 2) * RG * DH + r * DH:(k % 2) * RG * DH + (r + 1) * DH]
                        rr = (r % 2) * 2 + r // 2
                        for kt in range(T + 1):
                            ins = mm(o, pT[:, k % 2, rr, kt, :], vs[:, br, kt, grp * DH:(grp + 1) * DH],
                                     start=kt == 0, stop=kt == T)
                    ins.then_inc(pv_step, 1)
                if i < 16:
                    T, half, br = (i // 2) % 2, (i // 4) % 2, i // 8
                    grp = 2 * half + i % 2
                    nk = (T + 1) * P
                    if i >= 2:
                        pe.wait_ge(pT_done, i - 1)
                    else:
                        pe.wait_ge(o_evac, 1)
                    for r in range(RG):
                        hh = grp * RG + r
                        q = slice((hh % 2) * DH, (hh % 2 + 1) * DH)
                        ins = mm(ps[:, 4 + 2 * (i % 2) + r % 2, (r // 2) * S:(r // 2) * S + nk],
                                 qT[q, hh // 2, T * P:(T + 1) * P], kT[q, br, grp, 0:nk], start=True, stop=True)
                    ins.then_inc(scores_done, 1)
                if 1 <= i < 17:
                    k = i - 1
                    T = (k // 2) % 2
                    pe.wait_ge(exp_done, k + 1)
                    for r in range(RG):
                        for kt in range(T + 1):
                            c = (r // 2) * S + kt * P
                            ins = turn(ps[:, 4 + 2 * (k % 2) + r % 2, c:c + P], sg[:, k % 2, r, kt * P:(kt + 1) * P])
                    ins.then_inc(p_turned_all, 1)

            zouts = [ps[:, T, :] for T in range(NT)]
            for kind, i in NSA_ORDER:
                if kind == "a":
                    att(i)
                    continue
                if i % 2 == 0:
                    if i:
                        pe.wait_ge(z_done, i // 2)
                products(U["z"] + i, KU, NB, *X, (i % 2) * KU, zouts, i % 2 == 0, i % 2 == 1)
            pe.wait_ge(z_used, 6)
            turn_h(0, y).then_inc(y_turned, 1)
            pe.wait_ge(yl_done, 1)
            pe.wait_ge(z_done, 6)
            for i in range(2):
                b = B["nsa_out"] + i
                outs = [ps[:, pair(b) + T, :] for T in range(NT)]
                for k in range(2):
                    products(U["nsa_out"] + 2 * i + k, KU, NB, *X, k * KU, outs, k == 0, k == 1)

            def ffn(nt, ub, bb, fb, x, hx, acc, first_extra=None, extra=None):
                def turn_hidden(f):
                    pe.wait_ge(banks_free[(bb + 2 * f + 1) % 2], g.freed(bb + 2 * f + 1))
                    if nt == 2:
                        if f:
                            pe.wait_ge(hidden_low, g.at(hidden_low, f))
                        for T in range(NT):
                            for k in range(KU):
                                ins = turn(ps[:, 4 + T, k * P:(k + 1) * P], ht[:, T, k * P:(k + 1) * P])
                    else:
                        if f >= 2:
                            pe.wait_ge(hidden_low, g.at(hidden_low, fb + f - 1))
                        elif f == 0:
                            pe.wait_ge(pick_copied, g.at(pick_copied, 1))
                        for k in range(KU):
                            ins = turn(ps[:, 6 + f % 2, k * P:(k + 1) * P], ht[:, 0, k * P:(k + 1) * P])
                    ins.then_inc(hidden_turned, 1)

                for f in range(NFB):
                    block(ub + 4 * f, bb + 2 * f, *x, nt=nt)
                    if f:
                        turn_hidden(f - 1)
                    elif first_extra:
                        first_extra()
                    block(ub + 4 * f + 2, bb + 2 * f + 1, *x, nt=nt)
                u = ub + 4 * NFB
                nk = FF // P
                if nt == 2:
                    turn_hidden(NFB - 1)
                    pe.wait_ge(hidden_low, g.at(hidden_low, NFB))
                for k0 in range(0, nk, KU):
                    if nt == 1:
                        if k0 == 0:
                            pe.wait_ge(hidden_low, g.at(hidden_low, fb + NFB - 1))
                        if k0 == KU:
                            turn_hidden(NFB - 1)
                        if k0 == 3 * KU and extra:
                            extra()
                        if k0 == nk - KU:
                            pe.wait_ge(hidden_low, g.at(hidden_low, fb + NFB))
                    for half in range(2):
                        products(u, KU, NB, *hx, k0, [ps[:, acc(T, half), :] for T in range(nt)], k0 == 0,
                                 k0 == nk - KU)
                        u += 1

            def mix(i):
                normed(3 * i + 1)
                pe.wait_ge(xl_done, 3 * i + 2)
                ib, iu = B[f"in{i}"], U[f"in{i}"]
                for j in range(3):
                    block(iu + 2 * j, ib + j, *X)
                pe.wait_ge(qk_normed, 2 * i + 2)
                for j in range(2):
                    for a in range(4):
                        for T in range(NT):
                            ins = turn(ps[:, 4 + 2 * j + a // 2, (a % 2) * S + T * P:(a % 2) * S + (T + 1) * P],
                                       qk[:, j, T, a * P:(a + 1) * P])
                ins.then_inc(qk_turned, 1)

                def block_T(j):
                    b = ib + j
                    start_block(b)
                    for v in range(2):
                        u = iu + 2 * j + v
                        wh, wl = split_view(u, KU, NB)
                        pe.wait_ge(low_done, g.at(low_done, u + 1))
                        for k in range(KU):
                            kk = v * KU + k
                            for c in range(4):
                                o = ps[:, pair(b) + c // 2, (c % 2) * S:(c % 2 + 1) * S]
                                w_ = slice(c * P, (c + 1) * P)
                                f = kk == 0 and c % 2 == 0
                                mm(o, wh[:, k, w_], xh[:, kk, :], start=f, stop=False, skip_group_check=True)
                                mm(o, wh[:, k, w_], xl[:, kk, :], start=False, stop=False, skip_group_check=True)
                                ins = mm(o, wl[:, k, w_], xh[:, kk, :], start=False, stop=kk == KD - 1,
                                         skip_group_check=True)
                        ins.then_inc(unit_used, 1)

                def scores(hb):
                    if hb:
                        pe.wait_ge(stick_exp, 2 * i + hb)
                    for a in range(4):
                        hh = hb * 4 + a
                        q = slice((hh % 2) * DH, (hh % 2 + 1) * DH)
                        mm(ps[:, 4 + a, 0:S], qkT[q, 1, hh // 2, 0:P], qkT[q, 0, hh // 2, :], start=True,
                           stop=False, skip_group_check=True)
                        ins = mm(ps[:, 4 + a, S:S + P], qkT[q, 1, hh // 2, P:S], qkT[q, 0, hh // 2, P:S],
                                 start=False, stop=False, skip_group_check=True)
                    ins.then_inc(z_scores, 1)

                def stick(hb):
                    pe.wait_ge(sp_done, 2 * i + hb + 1)
                    for a in range(4):
                        for o, w_, x in (((0, S), ntri, (0, S)), ((S, S + P), ntri, (S, S + P)),
                                         ((P, S), nones, (S, S + P)), ):
                            mm(ps[:, 4 + a, o[0]:o[1]], w_, spb[:, a, x[0]:x[1]], start=False, stop=False,
                               skip_group_check=True)
                        for c in (0, S):
                            ins = mm(ps[:, 4 + a, c:c + P], ident, negm, start=False, stop=c == S,
                                     skip_group_check=True)
                    ins.then_inc(stick_done, 1)

                def pv(hb):
                    b = B[f"oT{i}"]
                    if hb == 0:
                        start_block(b)
                    pe.wait_ge(stick_exp, 2 * i + hb + 1)
                    for a in range(4):
                        hh = hb * 4 + a
                        q = slice((hh % 2) * DH, (hh % 2 + 1) * DH)
                        o = ps[q, pair(b) + hh // 4, ((hh // 2) % 2) * S:((hh // 2) % 2 + 1) * S]
                        mm(o, v2[:, 0, hh * DH:(hh + 1) * DH], wT[:, a, 0:S], start=True, stop=False,
                           skip_group_check=True)
                        ins = mm(o[:, P:S], v2[:, 1, hh * DH:(hh + 1) * DH], wT[:, a, S:S + P], start=False,
                                 stop=True, skip_group_check=True)
                    ins.then_inc(pv_done, 1)

                block_T(3)
                pe.wait_ge(qkT_done, i + 1)
                scores(0)
                block_T(4)
                block_T(5)
                stick(0)
                pv(0)
                scores(1)
                stick(1)
                pv(1)
                pe.wait_ge(mix_squares, i + 1)
                for half in range(2):
                    for j in range(4):
                        ins = mm(ps[:, 4 + half, 0:S], ones, mixs[:, half * 4 + j, :], start=j == 0, stop=j == 3)
                ins.then_inc(mix_sums, 1)
                pe.wait_ge(mixl_done, i + 1)
                for j in range(2):
                    block(U[f"o{i}"] + 2 * j, B[f"o{i}"] + j, *X)

            def ple(i):
                ub, bb = U[f"ple{i}"], B[f"ple{i}"]
                normed(3 * i + 3)
                pe.wait_ge(xl_done, 3 * i + 4)
                pe.wait_ge(p_loaded, 16 * (i + 1))
                for k in range(2):
                    for T in range(NT):
                        ins = turn(ps[:, 4, k * S + T * P:k * S + (T + 1) * P], pt_in[:, T, k * P:(k + 1) * P])
                ins.then_inc(p_turned, 1)
                pe.wait_ge(pl_done, i + 1)
                for j in range(2):
                    block(ub + 2 * j, bb + j, *X)
                for j in range(2):
                    block(ub + 4 + j, bb + 2 + j, tile_of(ptTh), tile_of(ptTl), kt=2)

            mix(0)
            normed(2)
            pe.wait_ge(xl_done, 3)
            ffn(2, U["ffn0"], B["ffn0"], 0, X, (tile_of(hTh), tile_of(hTl)), lambda T, half: 4 + 2 * T + half)
            ple(0)
            mix(1)
            normed(5)
            pe.wait_ge(xl_done, 6)
            pe.wait_ge(router_low, 1)
            pe.wait_ge(banks_free[(B["o1"]) % 2], g.freed(B["o1"]))
            pe.wait_ge(banks_free[(B["o1"] + 1) % 2], g.freed(B["o1"] + 1))
            for T in range(NT):
                o = ps[:, 0, T * NE:(T + 1) * NE]
                for k in range(KD):
                    a, b = xh[:, k, T * P:(T + 1) * P], xl[:, k, T * P:(T + 1) * P]
                    mm(o, a, rwh[:, k, :], start=k == 0, stop=False)
                    mm(o, a, rwl[:, k, :], start=False, stop=False)
                    ins = mm(o, b, rwh[:, k, :], start=False, stop=k == KD - 1)
            ins.then_inc(router_logits, 1)
            pe.wait_ge(sel_done, 1)
            mm(ps[:, 1, 0:NE], stri, sel[:, 0, :], start=True, stop=True)
            mm(ps[:, 1, NE:2 * NE], stri, sel[:, 1, :], start=True, stop=False)
            mm(ps[:, 1, NE:2 * NE], ones, sel[:, 0, :], start=False, stop=True)
            mm(ps[:, 1, 2 * NE:3 * NE], ones, sel[:, 0, :], start=True, stop=False)
            mm(ps[:, 1, 2 * NE:3 * NE], ones, sel[:, 1, :], start=False, stop=True).then_inc(slots_counted, 1)

            def gather(n):
                pe.wait_ge(pick_done, g.at(pick_done, n + 1))
                if n:
                    pe.wait_ge(hidden_low, g.at(hidden_low, 2 * NFB))
                else:
                    pe.wait_ge(xl_done, 6)
                    pe.wait_ge(xn_low, 1)
                for j in range(KD):
                    o = ps[:, 6 + j // 4, (j % 4) * P:(j % 4 + 1) * P]
                    for T in range(NT):
                        mm(o, xnh[:, T, j * P:(j + 1) * P], pick[:, T, :], start=T == 0, stop=False)
                        ins = mm(o, xnl[:, T, j * P:(j + 1) * P], pick[:, T, :], start=False, stop=T == 1)
                ins.then_inc(gathered, 1)

            gather(0)
            pe.wait_ge(rounds_known, 1)
            rounds = pe.value_load(nround[0:1, 0:1], min_val=NE, max_val=2 * NE)
            G = (lambda k, T: xgh[:, k, :], lambda k, T: xgl[:, k, :])
            M = (lambda k, T: mTh[:, k, :], lambda k, T: mTl[:, k, :])
            with pe.Fori(0, rounds) as r:
                g.r = r
                pe.wait_ge(gather_low, g.at(gather_low, 1))

                def turn_pick():
                    pe.wait_ge(round_done, g.at(round_done, 1))
                    for T in range(NT):
                        ins = turn(ps[:, 6, T * P:(T + 1) * P], pick[:, T, :].bitcast(F32))
                    ins.then_inc(pick_turned, 1)
                ffn(1, U["ffn1"], B["ffn1"], NFB, G, M, lambda T, half: 4 + half, turn_pick, lambda: gather(1))
                pe.wait_ge(y_low, g.at(y_low, 1))
                pe.wait_ge(gather_low, g.at(gather_low, 2))
                for T in range(NT):
                    for half in range(2):
                        o = ps[:, (6 if T == 0 else 4) + half, :]
                        c = slice(half * NB, (half + 1) * NB)
                        mm(o, pickT[:, T, :], yh[:, c], start=True, stop=False)
                        ins = mm(o, pickT[:, T, :], yl[:, c], start=False, stop=True)
                ins.then_inc(scatter_done, 1)
            g.r = rounds
            g.post = True
            ple(1)


NSA_ORDER = [("a", 0), ("z", 0), ("a", 1), ("z", 1), ("a", 2), ("z", 2), ("a", 3), ("z", 3), ("a", 4), ("a", 5),
             ("z", 4), ("a", 6), ("z", 5), ("a", 7), ("a", 8), ("a", 9), ("z", 6), ("z", 7), ("a", 10), ("a", 11),
             ("a", 12), ("z", 8), ("a", 13), ("z", 9), ("a", 14), ("a", 15), ("z", 10), ("a", 16), ("a", 17),
             ("z", 11)]


def square_constants():
    i = np.arange(P)
    r, c = i[:, None], i[None, :]
    parts = [r == c, -1.0 * (r >= c), -np.ones((P, P)), np.where(r >= c, -1e30, 0.0), r < c, r < c,
             np.ones((P, P)), np.broadcast_to(c, (P, P))]
    e = np.arange(NE)
    tril = np.broadcast_to((e[None, :] < e[:, None]).reshape(1, 64), (P, 64))
    diag = (r // NC_ == e[None, :]) & (r < 8 * NC_)
    return np.concatenate([np.asarray(x, np.float32) for x in parts + [tril, diag]], axis=1)


def onehot_constants():
    d = np.concatenate([np.arange(512) - 256, 255 - np.arange(LREV)])
    n = np.maximum(d, 0)
    ex = NBUCK // 2
    big = ex + (np.log(np.maximum(n, 1).astype(np.float32) / ex) / np.log(MAXD / ex) * (NBUCK - ex)).astype(np.int32)
    bucket = np.where(n < ex, n, np.minimum(big, NBUCK - 1))
    out = np.zeros((NBUCK + 1, d.size), np.float32)
    out[bucket, np.arange(d.size)] = np.where(d >= 0, 1.0 / SC, 0.0)
    out[NBUCK] = np.where(d >= 0, 0.0, MASKED)
    return out


_INS = ["x", "pre_norm_gain", "post_norm_gain", "rel_bias_table", "nsa_w_in", "nsa_w_out", "nsa_cmp_k_pos",
        "nsa_cmp_k_w1", "nsa_cmp_k_w2", "nsa_cmp_v_pos", "nsa_cmp_v_w1", "nsa_cmp_v_w2", "p_2", "mix_norm_g_2",
        "w_in_2", "q_norm_g_2", "k_norm_g_2", "conv_w_2", "conv_b_2", "attn_out_g_2", "conv_out_g_2", "w_o_2",
        "ffn_norm_g_2", "dense_w1_2", "dense_w3_2", "dense_w2_2", "router_w_2", "moe_w1_2", "moe_w3_2",
        "moe_w2_2", "ple_norm_g_2", "ple_gate_w_2", "ple_proj_w_2"]


def kernel(**inputs):
    import concourse.bacc as _bacc
    from concourse.bass_utils import run_bass_kernel_spmd as _run

    nc = _bacc.Bacc("TRN2", target_bir_lowering=False, num_devices=1)
    arrays, t = {}, {}
    given = {name: np.ascontiguousarray(inputs[name]) for name in _INS}
    given["c_square"] = square_constants()
    given["c_onehot"] = onehot_constants()
    for name, a in given.items():
        arrays[f"in_{name}_dram"] = a
        t[name] = nc.dram_tensor(f"in_{name}_dram", a.shape, mybir.dt.from_np(a.dtype), kind="ExternalInput").ap()
    out = nc.dram_tensor("out_0_dram", (1, S, D), F32, kind="ExternalOutput").ap()
    build(nc, t, out)
    r = _run(nc, [arrays], core_ids=[0])
    return r.results[0]["out_0_dram"]
```

```python
from contextlib import ExitStack

import numpy as np

import concourse.bass as bass
from concourse import mybir

F32 = mybir.dt.float32
F32R = mybir.dt.float32r
I32 = mybir.dt.int32
ALU = mybir.AluOpType
ACT = mybir.ActivationFunctionType
AX = mybir.AxisListType.X

P = 128
S = 256
NT = S // P
D = 1024
KD = D // P
NB = 512
KU = 4

NH, DH, NG = 16, 64, 4
RG = NH // NG
KV0, G0, Z0 = NH * DH, NH * DH + 6 * NG * DH, NH * DH + 6 * NG * DH + 3 * NH
CB, CS = 32, 16
NC_ = (S - CB) // CS + 1
HC = 256
NBUCK, MAXD = 32, 128
SC = DH ** -0.5
MASKED = -1e30 / SC
LREV = 384

SH = 8
FF = 3584
NFB = FF // NB
NE = 8
EPS = 1e-6

RAW = 6
SPL = 3
AHEAD = SPL - 1
UNITS_ROUND = 2 * NFB * 2 + FF // (KU * P) * 2
BLOCKS_ROUND = 2 * NFB


def weight_units(w):
    def block(m, c0, n=NB, kt=KD):
        return [(m, k, min(KU, kt - k), c0, n) for k in range(0, kt, KU)]

    def ffn(w1, w3, w2):
        out = []
        for b in range(NFB):
            out += block(w1, b * NB) + block(w3, b * NB)
        for k in range(0, FF // P, KU):
            out += [(w2, k, KU, 0, NB), (w2, k, KU, NB, NB)]
        return out

    nsa = block(w["nsa_in"], KV0)
    nsa += block(w["nsa_in"], 0) + block(w["nsa_in"], NB)
    nsa += block(w["nsa_in"], KV0 + NB) + block(w["nsa_in"], KV0 + 2 * NB)
    nsa += [(w["nsa_in"], 0, KD, G0, 3 * NH)]
    nsa += [(w["cmp_k1"], 0, 8, 0, HC), (w["cmp_k1"], 8, 8, 0, HC)]
    nsa += [(w["cmp_v1"], 0, 8, 0, HC), (w["cmp_v1"], 8, 8, 0, HC)]
    for b in range(6):
        nsa += block(w["nsa_in"], Z0 + b * NB)
    nsa += block(w["nsa_out"], 0) + block(w["nsa_out"], NB)

    def mix(i):
        out = []
        for b in range(6):
            out += block(w[f"in{i}"], b * NB)
        return out + [(w[f"o{i}"], k, KU, c, NB) for k in (KU, 0) for c in (0, NB)]

    def ple(i):
        return (block(w[f"pg{i}"], 0) + block(w[f"pg{i}"], NB)
                + block(w[f"pp{i}"], 0, kt=2) + block(w[f"pp{i}"], NB, kt=2))

    before = nsa + mix(0) + ffn(w["d1"], w["d3"], w["d2"]) + ple(0) + mix(1)
    return before, ffn(w["m1"], w["m3"], w["m2"]), ple(1)


def first_unit_of():
    at, out = 0, {}
    for name, n in (("kv_c", 2), ("q", 4), ("kv_s", 2), ("kv_w", 2), ("gate", 1), ("cmp", 4), ("z", 12),
                    ("nsa_out", 4), ("in0", 12), ("o0", 4), ("ffn0", UNITS_ROUND), ("ple0", 6), ("in1", 12),
                    ("o1", 4), ("ffn1", UNITS_ROUND)):
        out[name] = at
        at += n
    out["ple1"] = out["ffn1"]
    return out


def build(nc, t, out):
    U = first_unit_of()
    B = {}
    nblk = 0
    for name, n in (("kv_c", 1), ("q", 2), ("kv_s", 1), ("kv_w", 1), ("gate", 1), ("cmp", 2), ("z", 6),
                    ("nsa_out", 2), ("in0", 6), ("o0", 4), ("ffn0", BLOCKS_ROUND), ("ple0", 4),
                    ("in1", 6), ("o1", 4), ("ffn1", BLOCKS_ROUND)):
        B[name] = nblk
        nblk += n
    z_blocks = range(B["z"], B["z"] + 6)
    B["ple1"] = B["ffn1"]
    block_end = {}
    for name, n, units in (("kv_c", 1, 2), ("q", 2, 2), ("kv_s", 1, 2), ("kv_w", 1, 2), ("gate", 1, 1),
                           ("cmp", 2, 2), ("z", 6, 2), ("nsa_out", 2, 2), ("in0", 6, 2), ("o0", 4, 1),
                           ("ffn0", BLOCKS_ROUND, 2), ("in1", 6, 2), ("o1", 4, 1), ("ffn1", BLOCKS_ROUND, 2)):
        for j in range(n):
            block_end[B[name] + j] = U[name] + (j + 1) * units
    ple_end = [2, 4, 5, 6]
    for j in range(4):
        block_end[B["ple0"] + j] = U["ple0"] + ple_end[j]

    weights = {
        "nsa_in": t["nsa_w_in"][0], "nsa_out": t["nsa_w_out"][0],
        "cmp_k1": t["nsa_cmp_k_w1"][0], "cmp_v1": t["nsa_cmp_v_w1"][0],
        "d1": t["dense_w1_2"][0], "d3": t["dense_w3_2"][0], "d2": t["dense_w2_2"][0],
        "m1": t["moe_w1_2"][0], "m3": t["moe_w3_2"][0], "m2": t["moe_w2_2"][0],
    }
    for i in range(2):
        weights |= {f"in{i}": t["w_in_2"][i], f"o{i}": t["w_o_2"][i],
                    f"pg{i}": t["ple_gate_w_2"][i], f"pp{i}": t["ple_proj_w_2"][i]}
    before, per_round, after = weight_units(weights)
    assert len(before) == U["ffn1"] and len(per_round) == UNITS_ROUND

    with ExitStack() as ctx:
        def sb(name, shape, dt=F32, scope=ctx):
            return scope.enter_context(nc.sbuf_tensor(name, shape, dt))

        raw = sb("raw", [P, RAW, KU * NB])
        whi = sb("whi", [P, SPL, KU * NB], F32R)
        wlo = sb("wlo", [P, SPL, KU * NB], F32R)
        h = sb("h", [P, NT, D])
        tok = sb("tok", [P, NT, D])
        xh = sb("xh", [P, KD, S], F32R)
        xl = sb("xl", [P, KD, S], F32R)
        con = sb("con", [P, 8 * P + 64 + 8])
        ident, ntri, nones, negm, keep, stri, ones, iota = (con[:, i * P:(i + 1) * P] for i in range(8))
        tril8 = con[:, 8 * P:8 * P + 64]
        bdiag = con[:, 8 * P + 64:8 * P + 72]
        gains = sb("gains", [P, 7, KD])
        ogain = sb("ogain", [P, 2, KD])
        qkg = sb("qkg", [P, 2, 2])
        convw = sb("convw", [P, 2, 4, 4])
        rw = sb("rw", [P, KD, NE])
        rwh = sb("rwh", [P, KD, NE], F32R)
        rwl = sb("rwl", [P, KD, NE], F32R)
        st = sb("st", [P, 64])
        epst = sb("epst", [P, 1])
        nround = sb("nround", [1, 1], I32)

        with ExitStack() as nsa:
            tabx = sb("tabx", [NBUCK + 1, NH], scope=nsa)
            with ExitStack() as a:
                kc2 = sb("kc2", [P, NT, 2 * NG, 2, DH], scope=a)
                XW = 2 * (CB // 2) * NG * NC_
                XT = XW + P - NG * NC_
                xw = sb("xw", [P, XT], scope=a)
            bias = sb("bias", [P, NH, S], scope=nsa)
            cbias = sb("cbias", [P, NT, NH, NC_], scope=nsa)
            qT = sb("qT", [P, NH // 2, S], scope=nsa)
            kT = sb("kT", [P, 2, NG, S], scope=nsa)
            vs = sb("vs", [P, 2, NT, NG * DH], scope=nsa)
            pos2 = sb("pos2", [P, 2, CB // 2], scope=nsa)
            w2k = sb("w2k", [P, 2, 2, DH], scope=nsa)
            w2v = sb("w2v", [P, 2, DH], scope=nsa)
            kcT = sb("kcT", [P, NG * NC_], scope=nsa)
            gate = sb("gate", [P, NT, 3 * NH], scope=nsa)
            cst = sb("cst", [P, 3, NT * NH], scope=nsa)
            grow = sb("grow", [P, NT, NH], scope=nsa)
            ast_ = sb("ast", [P, 16, 3, RG], scope=nsa)
            with ExitStack() as early:
                with ExitStack() as a:
                    oh = sb("oh", [NBUCK + 1, 512 + LREV], scope=a)
                    revb = sb("revb", [NH, LREV], scope=a)
                    kd = sb("kd", [P, 2, NT, NG, 2, DH], scope=a)
                    xwh = sb("xwh", [P, XT], F32R, scope=a)
                    xwl = sb("xwl", [P, XT], F32R, scope=a)
                with ExitStack() as a:
                    hc = sb("hc", [NG * NC_, 2, HC], scope=a)
                    hcT = sb("hcT", [P, 2, 2, NG * NC_], scope=a)
                    hcR = sb("hcR", [P, 2, 2, 8 * NC_], scope=a)
                    vcb = sb("vcb", [8 * NC_, 2, 8, DH], scope=a)
                    lcT = sb("lcT", [8 * NC_, 2 * NT, P], scope=a)
                    lc = sb("lc", [P, NT, NH, NC_], scope=a)
            y = tok
            with ExitStack() as late:
                ob = sb("ob", [P, NT, D], scope=late)
                zt = sb("zt", [P, NT, NB], scope=late)
                sg = sb("sg", [P, 2, RG, S], scope=late)
                pT = sb("pT", [P, 2, RG, NT, P], scope=late)
                postg = sb("postg", [P, D], scope=late)

        with ExitStack() as mx:
            qk = sb("qk", [P, 2, NT, NB], scope=mx)
            sq = sb("sq", [P, NT, NB], scope=mx)
            qk_ss = sb("qk_ss", [P, 2, NT, SH], scope=mx)
            v2 = sb("v2", [P, NT, NB], scope=mx)
            qkT = sb("qkT", [P, 2, 4, S], scope=mx)
            uT = sb("uT", [P, 4, S], scope=mx)
            cu = sb("cu", [P, 4, S + 2], scope=mx)
            cv = sb("cv", [P, 4, S], scope=mx)
            mixT = sb("mixT", [P, 8, S], scope=mx)
            mixs = sb("mixs", [P, 8, S], scope=mx)
            factor_diag, factor_cols, factor_squares = (mixs[:, j, :] for j in range(3))
            spa = sb("spa", [P, 4, 3 * P], scope=mx)
            spb = sb("spb", [P, 4, 3 * P], scope=mx)
            wT = sb("wT", [P, 4, 3 * P], scope=mx)

        with ExitStack() as ff:
            gt = sb("gt", [P, NT, NB], scope=ff)
            ht = sb("ht", [P, NT, NB], scope=ff)
            pt_in = sb("pt_in", [P, NT, 2 * P], scope=ff)
            with ExitStack() as a:
                hTh = sb("hTh", [P, FF // P, S], F32R, scope=a)
                hTl = sb("hTl", [P, FF // P, S], F32R, scope=a)
            with ExitStack() as a:
                mTh = sb("mTh", [P, FF // P, P], F32R, scope=a)
                mTl = sb("mTl", [P, FF // P, P], F32R, scope=a)
                xnh = sb("xnh", [P, NT, D], F32R, scope=a)
                xnl = sb("xnl", [P, NT, D], F32R, scope=a)
                xgh = sb("xgh", [P, KD, P], F32R, scope=a)
                xgl = sb("xgl", [P, KD, P], F32R, scope=a)
                yh = sb("yh", [P, D], F32R, scope=a)
                yl = sb("yl", [P, D], F32R, scope=a)
                pick = sb("pick", [P, NT, P], F32R, scope=a)
                pickT = sb("pickT", [P, NT, P], F32R, scope=a)
                lg = sb("lg", [P, NT, NE], scope=a)
                cmpa = sb("cmpa", [P, NT, NE, NE], scope=a)
                cmpb = sb("cmpb", [P, NT, NE, NE], scope=a)
                sel = sb("sel", [P, NT, NE], scope=a)
                gw = sb("gw", [P, NT, NE], scope=a)
                slot = sb("slot", [P, NT, 2 * NE + 1], scope=a)
                cnt = sb("cnt", [P, NE + 4], scope=a)
            with ExitStack() as a:
                ptTh = sb("ptTh", [P, 2, S], F32R, scope=a)
                ptTl = sb("ptTl", [P, 2, S], F32R, scope=a)
                pg = sb("pg", [P, 2, NT, NB], scope=a)
                pm = sb("pm", [P, NT, NB], scope=a)

        ps = ctx.enter_context(nc.psum_tensor("ps", [P, 8, NB], F32))
        bias_dram = nc.dram_tensor("bias_scratch", [NH, P, LREV], F32, kind="Internal").ap()

        per = {}

        def sem(name, each_round=0):
            per[name] = each_round
            return ctx.enter_context(nc.semaphore(name))

        unit_loaded = [sem(f"unit_loaded{s}", 16 * UNITS_ROUND // RAW) for s in range(RAW)]
        high_done, low_done, half_used = (sem(n, 2 * UNITS_ROUND) for n in ("high_done", "low_done", "half_used"))
        banks_free = [sem(f"banks_free{i}", BLOCKS_ROUND // 2) for i in range(2)]
        hidden_turned, hidden_high, hidden_low = (
            sem(n, NFB) for n in ("hidden_turned", "hidden_high", "hidden_low"))
        act_step, dve_step = sem("act_step"), sem("dve_step")
        pick_done = sem("pick_done", 1)
        pick_turned = sem("pick_turned", 1)
        pick_copied = sem("pick_copied", 1)
        gathered = sem("gathered", 1)
        gather_high = sem("gather_high", 1)
        gather_low = sem("gather_low", 1)
        y_high = sem("y_high", 1)
        y_low = sem("y_low", 1)
        scatter_done = sem("scatter_done", 1)
        round_done = sem("round_done", 1)
        rounds_known = sem("rounds_known")
        h_half = sem("h_half")
        stored = sem("stored")
        h_turned = sem("h_turned")
        gains_loaded = sem("gains_loaded")
        tab_product = sem("tab_product")
        x_loaded = sem("x_loaded")
        eps_set = sem("eps_set")
        windows_done = sem("windows_done")
        q_turned = sem("q_turned")
        k_turned = sem("k_turned")
        cmp_logits = sem("cmp_logits")
        logits_done = sem("logits_done")
        z_used = sem("z_used")
        y_turned = sem("y_turned")
        qk_squares = sem("qk_squares")
        z_scores = sem("z_scores")
        sp_done = sem("sp_done")
        stick_done = sem("stick_done")
        pv_done = sem("pv_done")
        mix_sums = sem("mix_sums")
        conv_sums_copied = sem("conv_sums_copied")
        conv_high = sem("conv_high")
        conv_low = sem("conv_low")
        pv_copied = sem("pv_copied")
        p_turned = sem("p_turned")
        router_loaded = sem("router_loaded")
        logit_shift = sem("logit_shift")
        root_done = sem("root_done")
        factor_done = sem("factor_done")
        h_ready = sem("h_ready")
        first_gain_loaded = sem("first_gain_loaded")
        factor_diag_done = sem("factor_diag_done")
        factor_spread = sem("factor_spread")
        factor_copied = sem("factor_copied")
        xh_done = sem("xh_done")
        cbias_done = sem("cbias_done")
        kc_turned = sem("kc_turned")
        cmp_loaded = sem("cmp_loaded")
        window_high = sem("window_high")
        hc_turned = sem("hc_turned")
        rev_stored = sem("rev_stored")
        kcvc_product = sem("kcvc_product")
        cmp_scores = sem("cmp_scores")
        cmp_exp = sem("cmp_exp")
        lc_turned = sem("lc_turned")
        cmp_out = sem("cmp_out")
        o_evac = sem("o_evac")
        bias_loaded = sem("bias_loaded")
        scores_done = sem("scores_done")
        p_turned_all = sem("p_turned_all")
        pv_step = sem("pv_step")
        exp_done = sem("exp_done")
        z_done = sem("z_done")
        yh_done = sem("yh_done")
        post_root = sem("post_root")
        postg_loaded = sem("postg_loaded")
        qk_root = sem("qk_root")
        qk_turned = sem("qk_turned")
        mix_loaded = sem("mix_loaded")
        ln_done = sem("ln_done")
        mix_root = sem("mix_root")
        mixh_done = sem("mixh_done")
        ph_done = sem("ph_done")
        router_high = sem("router_high")
        xn_high = sem("xn_high")
        router_logits = sem("router_logits")
        sel_done = sem("sel_done")
        gate_exp = sem("gate_exp")
        slots_counted = sem("slots_counted")
        h_normed = sem("h_normed")
        con_loaded = sem("con_loaded")
        oh_loaded = sem("oh_loaded")
        table_one = sem("table_one")
        rev_ready = sem("rev_ready")
        xl_done = sem("xl_done")
        qT_done = sem("qT_done")
        window_low = sem("window_low")
        kT_done = sem("kT_done")
        hcT_done = sem("hcT_done")
        kcT_done = sem("kcT_done")
        lcT_done = sem("lcT_done")
        vcb_done = sem("vcb_done")
        pT_done = sem("pT_done")
        yl_done = sem("yl_done")
        qk_normed = sem("qk_normed")
        stick_exp = sem("stick_exp")
        qkT_done = sem("qkT_done")
        mix_squares = sem("mix_squares")
        mixl_done = sem("mixl_done")
        p_loaded = sem("p_loaded")
        pl_done = sem("pl_done")
        router_low = sem("router_low")
        xn_low = sem("xn_low")

        class Prog:

            def __init__(self):
                self.r, self.n, self.split, self.post = None, 0, 0, False

            def at(self, semaphore, n):
                k = per[semaphore.name]
                return n if self.r is None or not k else self.r * k + n

            def through(self, b):
                end = block_end[b] if not (self.post and b >= B["ple1"]) else U["ple1"] + ple_end[b - B["ple1"]]
                return self.at(half_used, 2 * end)

            def freed(self, b):
                count = len([x for x in range(b % 2, b + 1, 2) if x not in z_blocks])
                return self.at(banks_free[b % 2], count)

        def pair(b):
            return 2 * (b % 2)

        def turned_place(k, j):
            if k == 3:
                bank = 4 + j // KU + 2 * (j % KU // 2)
            else:
                bank = 4 + j // 2
            return ps[:, bank, (j % 2) * S:(j % 2 + 1) * S]

        def pv_place(j):
            return ps[:, 4 + 2 * j:6 + 2 * j, 3 * P:4 * P]

        def mix_tile(j):
            return (j + KU) % KD

        def factor(T):
            return st[:, 8 + T:9 + T]

        def unit_columns(v, post):
            if (v >= U["ffn1"]) != post:
                return KU * NB if v >= U["o1"] else before[v][2] * before[v][4]
            _, _, nk, _, n = after[v - U["ffn1"]] if post else before[v]
            return nk * n

        ld = nc.allow_non_contiguous_dma("small gains and constants")
        ctx.enter_context(ld)
        block_ = ctx.enter_context(nc.Block())

        @block_.sync
        def _(sp):
            g = Prog()
            sp.dma_start(h[:], t["x"][0].rearrange("(t p) d -> p t d", p=P)).then_inc(x_loaded, 16)

            def load(u, unit, e=None):
                m, k0, nk, c0, n = unit
                s = u % RAW
                if u >= RAW:
                    sp.wait_ge(low_done, g.at(low_done, 2 * (u - RAW + 1)))
                if e is None:
                    src = m[k0 * P:(k0 + nk) * P, c0:c0 + n].rearrange("(k p) n -> p k n", p=P)
                else:
                    src = m[bass.ds(e, 1), k0 * P:(k0 + nk) * P, c0:c0 + n].rearrange("a (k p) n -> p (a k) n", p=P)
                sp.dma_start(raw[:, s, 0:nk * n].rearrange("p (k n) -> p k n", k=nk), src)\
                    .then_inc(unit_loaded[s], 16)

            for u, unit in enumerate(before):
                load(u, unit)
            with sp.Fori(0, NE) as r:
                g.r = r
                for j, unit in enumerate(per_round):
                    load(U["ffn1"] + j, unit, r)
            g.r = None
            sp.wait_ge(rounds_known, 1)
            rounds = sp.value_load(nround[0:1, 0:1], min_val=NE, max_val=2 * NE)
            with sp.If(rounds > NE):
                with sp.Fori(NE, 2 * NE) as r:
                    g.r = r
                    for j, unit in enumerate(per_round):
                        load(U["ffn1"] + j, unit, r - NE)
            g.r = rounds
            for j, unit in enumerate(after):
                load(U["ple1"] + j, unit)
            for j in range(2):
                sp.wait_ge(h_half, 3 + j)
                c = slice(j * NB, (j + 1) * NB)
                sp.dma_start(out[0][:, c].rearrange("(t p) d -> p t d", p=P), h[:, :, c])\
                    .then_inc(stored, 16)
            sp.wait_ge(stored, 32)

        @block_.gpsimd
        def _(pool):
            def small(semaphore, dst, src):
                pool.dma_start(dst, src).then_inc(semaphore, 16)

            small(con_loaded, con[:], t["c_square"])
            small(first_gain_loaded, gains[:, 0, :], t["pre_norm_gain"][0].rearrange("(k p) -> p k", p=P))
            small(oh_loaded, oh[:], t["c_onehot"])
            small(oh_loaded, tabx[0:NBUCK, :], t["rel_bias_table"])
            pool.memset(tabx[NBUCK:NBUCK + 1, :], 1.0).then_inc(table_one, 1)
            pool.wait_ge(table_one, 1)
            pool.memset(epst[:], EPS).then_inc(eps_set, 1)
            for i in range(2):
                for j, n in ((1, "mix_norm_g_2"), (2, "ffn_norm_g_2"), (3, "ple_norm_g_2")):
                    small(gains_loaded, gains[:, 3 * i + j, :], t[n][i].rearrange("(k p) -> p k", p=P))
            for kv, n in ((0, "nsa_cmp_k_pos"), (1, "nsa_cmp_v_pos")):
                small(cmp_loaded, pos2[:, kv, :], t[n][0].rearrange("(m s) d -> (s d) m", s=2))
            for s in range(2):
                small(cmp_loaded, w2k[:, :, s, :], t["nsa_cmp_k_w2"][0].rearrange("(j p) d -> p j d", p=P))
            small(cmp_loaded, w2v[:], t["nsa_cmp_v_w2"][0].rearrange("(j p) d -> p j d", p=P))
            for i in range(2):
                for j, n in ((0, "attn_out_g_2"), (4, "conv_out_g_2")):
                    small(mix_loaded, ogain[:, i, j:j + 4], t[n][i].rearrange("(k p) -> p k", p=P))
                for j, n in ((0, "q_norm_g_2"), (1, "k_norm_g_2")):
                    for s in range(2):
                        small(mix_loaded, qkg[s * DH:(s + 1) * DH, i, j:j + 1],
                              t[n][i:i + 1].rearrange("a d -> d a"))
                for j in range(3):
                    small(mix_loaded, convw[:, i, :, j], t["conv_w_2"][i, j].rearrange("(k p) -> p k", p=P))
                small(mix_loaded, convw[:, i, :, 3], t["conv_b_2"][i].rearrange("(k p) -> p k", p=P))
            small(router_loaded, rw[:], t["router_w_2"][0].rearrange("(k p) e -> p k e", p=P))
            pool.wait_ge(rev_ready, 1)
            pool.dma_start(bias_dram, revb[:].unsqueeze(1).broadcast_to([NH, P, LREV])).then_inc(rev_stored, 16)
            pool.wait_ge(rev_stored, 16)
            pool.wait_ge(window_low, 1)
            pool.dma_start(bias[:], bass.AP(tensor=bias_dram.tensor, offset=P - 1,
                                            ap=[[LREV - 1, P], [P * LREV, NH], [1, S]])).then_inc(bias_loaded, 16)
            pool.wait_ge(o_evac, 1)
            small(postg_loaded, postg[:], t["post_norm_gain"][0:1].broadcast_to([P, D]))
            for i in range(2):
                pool.wait_ge(mixl_done, 2 * i + 2)
                small(p_loaded, pt_in[:], t["p_2"][i, 0].rearrange("(t p) d -> p t d", p=P))

        @block_.scalar
        def _(act):
            g = Prog()

            def step(ins):
                g.n += 1
                ins.then_inc(act_step, 1)
                act.wait_ge(act_step, g.n)

            AC = nc.scalar.activation

            def split_to(u):
                while g.split <= u:
                    v = g.split
                    n = unit_columns(v, g.post)
                    act.wait_ge(unit_loaded[v % RAW], g.at(unit_loaded[v % RAW], 16 * (v // RAW + 1)))
                    for half in range(2):
                        if v >= SPL:
                            last = half if unit_columns(v - SPL, g.post) == n else 1
                            act.wait_ge(half_used, g.at(half_used, 2 * (v - SPL) + last + 1))
                        c = slice(half * n // 2, (half + 1) * n // 2)
                        AC(whi[:, v % SPL, c], raw[:, v % RAW, c], ACT.Copy).then_inc(high_done, 1)
                    g.split += 1

            def root(k):
                for i in range(NT):
                    ins = AC(tok[:, i, :], h[:, i, :], ACT.Square, accum_out=st[:, i:i + 1])
                step(ins)
                AC(st[:, 2:4], st[:, 0:2], ACT.Sqrt, scale=1.0 / D, bias=epst[:, 0:1])\
                    .then_inc(root_done, 1)

            def turned_high(k, half):
                act.wait_ge(h_turned, 2 * k + half + 1)
                for j in range(half * KU, (half + 1) * KU):
                    ins = AC(xh[:, j, :], turned_place(k, j), ACT.Copy, scale=gains[:, k, j:j + 1])
                ins.then_inc(xh_done, 1)

            def start(k, u):
                split_to(u)
                turned_high(k, 0)
                split_to(u + 1)
                turned_high(k, 1)
                root(k)

            def both(b):
                return ps[:, pair(b):pair(b) + 2, :]

            def flat(x):
                return x.rearrange("p a n -> p (a n)")

            def evac(b, dst, src=None, func=ACT.Copy):
                act.wait_ge(half_used, g.through(b))
                AC(dst, both(b) if src is None else src, func).then_inc(banks_free[b % 2], 1)

            def evac_scaled(b, k, dst, n=NB, func=ACT.Copy):
                act.wait_ge(half_used, g.through(b))
                act.wait_ge(factor_done, k + 1)
                for T in range(NT):
                    ins = AC(dst[:, T], ps[:, pair(b) + T, 0:n], func, scale=factor(T))
                ins.then_inc(banks_free[b % 2], 1)

            act.wait_ge(first_gain_loaded, 16)
            act.wait_ge(x_loaded, 16)
            act.wait_ge(eps_set, 1)
            start(0, 0)
            act.wait_ge(tab_product, 1)
            AC(revb[:], ps[0:NH, 0, 0:LREV], ACT.Copy).then_inc(rev_ready, 1)
            split_to(U["q"] + 1)
            b = B["kv_c"]
            act.wait_ge(half_used, g.through(b))
            act.wait_ge(factor_done, 1)
            for T in range(NT):
                for s in range(2):
                    ins = AC(kc2[:, T, :, s, :], ps[:, pair(b) + T, :].rearrange("p (g d) -> p g d", d=DH), ACT.Copy,
                             scale=factor(T))
            ins.then_inc(banks_free[b % 2], 1)
            for i in range(2):
                split_to(U["q"] + 2 * i + 3)
                evac_scaled(B["q"] + i, 0, tok[:, :, i * NB:(i + 1) * NB])
            act.wait_ge(windows_done, 1)
            AC(xwh[:], xw[:], ACT.Copy).then_inc(window_high, 1)
            for i in range(2):
                split_to(U["kv_s"] + 2 * i + 3)
                b = B["kv_s"] + i
                act.wait_ge(half_used, g.through(b))
                for T in range(NT):
                    for s in range(2):
                        AC(kd[:, i, T, :, s, :], ps[:, pair(b) + T, 0:NG * DH].rearrange("p (g d) -> p g d", d=DH),
                           ACT.Copy, scale=factor(T))
                    ins = AC(vs[:, i, T, :], ps[:, pair(b) + T, NG * DH:NB], ACT.Copy, scale=factor(T))
                ins.then_inc(banks_free[b % 2], 1)
                if i == 0:
                    act.wait_ge(q_turned, 1)
                    AC(flat(qT[:]), flat(ps[:, 4:8, :]), ACT.Copy).then_inc(qT_done, 1)
            split_to(U["gate"] + 2)
            b = B["gate"]
            evac_scaled(b, 0, gate, 3 * NH, ACT.Sigmoid)
            act.wait_ge(k_turned, 1)
            AC(kT[:].rearrange("p a g n -> p (a g n)"), flat(ps[:, 4:8, :]), ACT.Copy).then_inc(kT_done, 1)
            for kv in range(2):
                split_to(U["cmp"] + 2 * kv + 3)
                b = B["cmp"] + kv
                evac(b, hc[:, kv, :], ps[0:NG * NC_, pair(b), 0:HC], ACT.Silu)
            act.wait_ge(cmp_logits, 1)
            AC(lc[:], lc[:], ACT.Exp, scale=SC).then_inc(cmp_exp, 1)

            def att(i):
                if i >= 16:
                    return
                T = (i // 2) % 2
                nk = (T + 1) * P
                act.wait_ge(logits_done, i + 1)
                for r in range(RG):
                    ins = AC(sg[:, i % 2, r, 0:nk], sg[:, i % 2, r, 0:nk], ACT.Exp, scale=SC,
                             bias=ast_[:, i, 1, r:r + 1], accum_out=ast_[:, i, 2, r:r + 1])
                ins.then_inc(exp_done, 1)

            for kind, i in NSA_ORDER:
                if kind == "a":
                    att(i)
                elif i % 2:
                    b = B["z"] + i // 2
                    split_to(U["z"] + i + AHEAD)
                    act.wait_ge(half_used, g.through(b))
                    if i // 2:
                        act.wait_ge(z_used, i // 2)
                    for T in range(NT):
                        ins = AC(zt[:, T, :], ps[:, T, :], ACT.Silu, scale=factor(T))
                    ins.then_inc(z_done, 1)
                else:
                    split_to(U["z"] + i + AHEAD)
            act.wait_ge(y_turned, 1)
            AC(xh[:].rearrange("p k n -> p (k n)"), ps[:, 4:8, :].rearrange("p b n -> p (b n)"), ACT.Copy)\
                .then_inc(yh_done, 1)
            split_to(U["nsa_out"] + 3)
            for i in range(2):
                b = B["nsa_out"] + i
                split_to(U["in0"] + i)
                evac(b, tok[:, :, i * NB:(i + 1) * NB])
                act.wait_ge(banks_free[b % 2], g.freed(b))
            for i in range(NT):
                ins = AC(ob[:, i, :], tok[:, i, :], ACT.Square, accum_out=st[:, 4 + i:5 + i])
            step(ins)
            AC(st[:, 6:8], st[:, 4:6], ACT.Sqrt, scale=1.0 / D, bias=epst[:, 0:1]).then_inc(post_root, 1)

            def ffn(nt, ub, bb, fb, high, first_extra=None, last_extra=None):
                def turn(f):
                    act.wait_ge(hidden_turned, g.at(hidden_turned, fb + f + 1))
                    src = ps[:, 4:6, :].rearrange("p t (k n) -> p k t n", k=KU) if nt == 2 else \
                        ps[:, 6 + f % 2, :].rearrange("p (k n) -> p k n", k=KU)
                    dst = high[:, f * KU:(f + 1) * KU, :]
                    if nt == 2:
                        dst = dst.rearrange("p k (t n) -> p k t n", t=NT)
                    AC(dst, src, ACT.Copy).then_inc(hidden_high, 1)

                for f in range(NFB):
                    b = bb + 2 * f
                    split_to(ub + 4 * f + 1 + AHEAD)
                    act.wait_ge(half_used, g.through(b))
                    act.wait_ge(banks_free[(b - 1) % 2], g.freed(b - 1))
                    if nt == 2:
                        act.wait_ge(factor_done, 3)
                        for T in range(NT):
                            ins = AC(gt[:, T, :], ps[:, pair(b) + T, :], ACT.Silu, scale=factor(T))
                    else:
                        ins = AC(gt[:, 0, :], ps[:, pair(b), :], ACT.Silu)
                    ins.then_inc(banks_free[b % 2], 1)
                    if f:
                        turn(f - 1)
                    elif first_extra:
                        first_extra()
                    split_to(ub + 4 * f + 3 + AHEAD)
                if nt == 1:
                    split_to(ub + 4 * NFB + 1 + AHEAD)
                turn(NFB - 1)
                if last_extra:
                    split_to(ub + 4 * NFB + 5 + AHEAD)
                    last_extra()
                split_to(ub + UNITS_ROUND - 1 + (AHEAD if nt == 1 else 0))

            def mix(i):
                start(3 * i + 1, U[f"in{i}"])
                ib, iu = B[f"in{i}"], U[f"in{i}"]
                for j in range(2):
                    split_to(iu + 2 * j + 1 + AHEAD)
                    evac_scaled(ib + j, 3 * i + 1, qk[:, j])
                    if j == 0:
                        act.wait_ge(factor_spread, i + 1)
                        AC(factor_cols, ps[:, 4, 0:S], ACT.Copy).then_inc(factor_copied, 1)
                    act.wait_ge(qk_squares, 2 * i + j + 1)
                    AC(qk_ss[:, j], qk_ss[:, j], ACT.Sqrt, scale=1.0 / DH, bias=epst[:, 0:1])\
                        .then_inc(qk_root, 1)
                split_to(iu + 5 + AHEAD)
                evac_scaled(ib + 2, 3 * i + 1, v2)
                split_to(iu + 7 + AHEAD)
                evac(ib + 3, flat(uT[:]), flat(both(ib + 3)))
                ou = U[f"o{i}"]
                split_to(iu + 10)

                def log_part(hb):
                    n = 2 * i + hb
                    act.wait_ge(z_scores, n + 1)
                    if n:
                        act.wait_ge(sp_done, n)
                    step(AC(spa[:], ps[:, 4:8, 0:3 * P], ACT.Abs))
                    step(AC(spa[:], spa[:], ACT.Exp, scale=-1.0))
                    AC(spa[:], spa[:], ACT.Ln, bias=ones[:, 0:1]).then_inc(ln_done, 1)

                def stick_weights(hb):
                    n = 2 * i + hb
                    act.wait_ge(stick_done, n + 1)
                    if n:
                        act.wait_ge(pv_done, n)
                    AC(wT[:], ps[:, 4:8, 0:3 * P], ACT.Exp).then_inc(stick_exp, 1)

                log_part(0)
                split_to(ou + 1)
                stick_weights(0)
                act.wait_ge(pv_done, 2 * i + 1)
                for j in range(2):
                    ins = AC(mixT[:, j, :].rearrange("p (t n) -> p t n", t=NT), pv_place(j), ACT.Copy)
                ins.then_inc(pv_copied, 1)
                act.wait_ge(banks_free[(ib + 5) % 2], g.freed(ib + 5))
                for j in range(KU, 2 * KU):
                    ins = AC(xh[:, mix_tile(j), :], mixT[:, j, :], ACT.Copy, scale=ogain[:, i, j:j + 1])
                ins.then_inc(conv_high, 1)
                AC(mixs[:, KU:2 * KU], mixT[:, KU:2 * KU], ACT.Square).then_inc(mix_squares, 1)
                split_to(ou + 2)
                log_part(1)
                act.wait_ge(conv_sums_copied, i + 1)
                AC(st[:, 26:28], st[:, 24:26], ACT.Sqrt, scale=1.0 / NB, bias=epst[:, 0:1]).then_inc(mix_root, 1)
                act.wait_ge(pv_copied, i + 1)
                for j in range(2):
                    AC(xh[:, mix_tile(j), :], mixT[:, j, :], ACT.Copy, scale=ogain[:, i, j:j + 1])
                AC(mixs[:, 0:2], mixT[:, 0:2], ACT.Square)
                split_to(ou + 3)
                stick_weights(1)
                act.wait_ge(pv_done, 2 * i + 2)
                for j in range(2):
                    ins = AC(xh[:, mix_tile(2 + j), :].rearrange("p (t n) -> p t n", t=NT), pv_place(j), ACT.Copy,
                             scale=ogain[:, i, 2 + j:3 + j])
                ins.then_inc(mixh_done, 1)
                for j in range(2):
                    ins = AC(mixs[:, 2 + j, :].rearrange("p (t n) -> p t n", t=NT), pv_place(j), ACT.Square)
                ins.then_inc(mix_squares, 1)
                act.wait_ge(mix_sums, 2 * i + 2)
                AC(st[:, 26:28], ps[:, 7, 0:NT], ACT.Sqrt, scale=1.0 / NB, bias=epst[:, 0:1]).then_inc(mix_root, 1)

            def ple(i):
                ub, bb = U[f"ple{i}"], B[f"ple{i}"]
                start(3 * i + 3, ub)
                for j in range(2):
                    split_to(min(ub + 2 * j + 1 + AHEAD, ub + 5))
                    b = bb + j
                    evac_scaled(b, 3 * i + 3, pg[:, j], func=ACT.Sigmoid)
                    if j == 0:
                        act.wait_ge(p_turned, i + 1)
                        AC(flat(ptTh[:]), ps[:, 4, :], ACT.Copy).then_inc(ph_done, 1)
                split_to(ub + 5)

            act.wait_ge(gains_loaded, 16 * 6)
            mix(0)
            start(2, U["ffn0"])
            ffn(2, U["ffn0"], B["ffn0"], 0, hTh)
            ple(0)
            mix(1)
            act.wait_ge(router_loaded, 16)
            AC(rwh[:], rw[:], ACT.Copy).then_inc(router_high, 1)
            start(5, U["ffn1"])
            act.wait_ge(h_normed, 1)
            AC(xnh[:], tok[:], ACT.Copy).then_inc(xn_high, 1)
            act.wait_ge(logit_shift, 1)
            AC(gw[:], gw[:], ACT.Exp).then_inc(gate_exp, 1)

            def split_gathered(n):
                act.wait_ge(gathered, g.at(gathered, n + 1))
                for j in range(KD):
                    ins = AC(xgh[:, j, :], ps[:, 6 + j // 4, (j % 4) * P:(j % 4 + 1) * P], ACT.Copy,
                             scale=gains[:, 5, j:j + 1])
                ins.then_inc(gather_high, 1)

            split_gathered(0)
            act.wait_ge(rounds_known, 1)
            rounds = act.value_load(nround[0:1, 0:1], min_val=NE, max_val=2 * NE)
            with act.Fori(0, rounds) as r:
                g.r = r

                def copy_pick():
                    act.wait_ge(pick_turned, g.at(pick_turned, 1))
                    AC(pickT[:], ps[:, 6, 0:2 * P].rearrange("p (t n) -> p t n", t=NT), ACT.Copy)\
                        .then_inc(pick_copied, 1)
                ffn(1, U["ffn1"], B["ffn1"], NFB, mTh, copy_pick, lambda: split_gathered(1))
                act.wait_ge(half_used, g.at(half_used, 2 * (U["ffn1"] + UNITS_ROUND)))
                AC(yh[:], ps[:, 4:6, :].rearrange("p b n -> p (b n)"), ACT.Copy).then_inc(y_high, 1)
                assert g.split == U["ffn1"] + UNITS_ROUND + 2
            g.r = rounds
            g.split = U["ffn1"] + 2
            g.post = True
            ple(1)

        @block_.vector
        def _(dve):
            g = Prog()

            def step(ins):
                g.n += 1
                ins.then_inc(dve_step, 1)
                dve.wait_ge(dve_step, g.n)

            V = nc.vector

            def split_to(u):
                while g.split <= u:
                    v = g.split
                    n = unit_columns(v, g.post)
                    for half in range(2):
                        dve.wait_ge(high_done, g.at(high_done, 2 * v + half + 1))
                        c = slice(half * n // 2, (half + 1) * n // 2)
                        V.tensor_tensor(wlo[:, v % SPL, c], raw[:, v % RAW, c], whi[:, v % SPL, c].bitcast(F32),
                                        ALU.subtract).then_inc(low_done, 1)
                    g.split += 1

            def invert_root(k):
                dve.wait_ge(root_done, k + 1)
                V.reciprocal(st[:, 8:10], st[:, 2:4]).then_inc(factor_done, 1)

            def turned_low(k, half):
                dve.wait_ge(xh_done, 2 * k + half + 1)
                for j in range(half * KU, (half + 1) * KU):
                    ins = V.scalar_tensor_tensor(out=xl[:, j, :], in0=turned_place(k, j),
                                                 scalar=gains[:, k, j:j + 1], in1=xh[:, j, :].bitcast(F32),
                                                 op0=ALU.mult, op1=ALU.subtract)
                ins.then_inc(xl_done, 1)

            split_to(0)
            turned_low(0, 0)
            split_to(1)
            turned_low(0, 1)
            invert_root(0)
            dve.wait_ge(tab_product, 2)
            V.tensor_copy(cbias[:].rearrange("p t h c -> p t c h"),
                          ps[:, 1, 0:NT * NC_ * NH].rearrange("p (t c h) -> p t c h", t=NT, c=NC_))\
                .then_inc(cbias_done, 1)
            dve.wait_ge(cbias_done, 1)
            split_to(U["q"] + 5)
            V.memset(xw[:, XW:XT], 0.0)
            dve.wait_ge(kc_turned, 1)
            dve.wait_ge(cmp_loaded, 16 * 5)
            for kv in range(2):
                for s in range(2):
                    q = slice(s * DH, (s + 1) * DH)
                    src = ps[q, 4 + 2 * kv:6 + 2 * kv, :].rearrange("p b n -> p (b n)")
                    src = src.rearrange("p (g c m s) -> p s m g c", g=NG, m=CS // 2, s=2)
                    for half in range(2):
                        ins = V.tensor_tensor(
                            xw[q, 0:XW].rearrange("p (v m g c) -> p v m g c", v=2, m=CB // 2, g=NG)[:, kv, 8 * half:8 * half + 8],
                            src[:, s, :, :, half:half + NC_],
                            pos2[q, kv, 8 * half:8 * half + 8].unsqueeze(2).unsqueeze(3)
                            .broadcast_to([DH, 8, NG, NC_]), ALU.add)
            ins.then_inc(windows_done, 1)
            dve.wait_ge(window_high, 1)
            V.tensor_tensor(xwl[:], xw[:], xwh[:].bitcast(F32), ALU.subtract).then_inc(window_low, 1)
            split_to(U["kv_w"] + 3)
            split_to(U["cmp"] + 3 + 2)
            dve.wait_ge(hc_turned, 1)
            step(V.tensor_copy(hcT[:].rearrange("p a j n -> p (a j n)"), ps[:, 4, 0:4 * NG * NC_]))
            dve.wait_ge(rev_stored, 16)
            for half in range(2):
                for j in range(2):
                    ins = V.tensor_copy(
                        hcR[:, half, j, :].rearrange("p (g r c) -> p g r c", g=2, r=RG),
                        hcT[:, 1, j, 2 * half * NC_:(2 * half + 2) * NC_].rearrange("p (g c) -> p g c", g=2)
                        .unsqueeze(2).broadcast_to([P, 2, RG, NC_]))
            ins.then_inc(hcT_done, 1)
            dve.wait_ge(kcvc_product, 1)
            V.tensor_copy(kcT[:], ps[:, 5, 0:NG * NC_]).then_inc(kcT_done, 1)
            for half in range(2):
                ins = V.tensor_tensor(
                    vcb[:, half], ps[0:8 * NC_, 6, half * DH:(half + 1) * DH].unsqueeze(1)
                    .broadcast_to([8 * NC_, 8, DH]),
                    bdiag[0:8 * NC_, :].unsqueeze(2).broadcast_to([8 * NC_, 8, DH]), ALU.mult)
            ins.then_inc(vcb_done, 1)
            dve.wait_ge(cmp_scores, 1)
            for j in range(2):
                ins = V.tensor_tensor(
                    lc[:].rearrange("p t (i j) c -> p j t i c", j=2)[:, j],
                    ps[:, 4 + j, 0:NT * 8 * NC_].rearrange("p (t i c) -> p t i c", t=NT, i=8),
                    cbias[:].rearrange("p t (i j) c -> p j t i c", j=2)[:, j], ALU.add)
            step(ins)
            lcv = lc[:].rearrange("p t h c -> p (t h) c")
            step(V.tensor_reduce(cst[:, 0, :], lcv, AX, ALU.max))
            step(V.tensor_scalar(cst[:, 0, :], cst[:, 0, :], MASKED / 16, None, ALU.max))
            V.tensor_tensor(lcv, lcv, cst[:, 0, :].unsqueeze(2).broadcast_to([P, NT * NH, NC_]), ALU.subtract)\
                .then_inc(cmp_logits, 1)
            dve.wait_ge(cmp_exp, 1)
            step(V.tensor_reduce(cst[:, 1, :], lcv, AX, ALU.add))
            step(V.tensor_scalar(cst[:, 1, :], cst[:, 1, :], 1e-30, None, ALU.max))
            step(V.reciprocal(cst[:, 2, :], cst[:, 1, :]))
            step(V.tensor_tensor(cst[:, 2, :].rearrange("p (t h) -> p t h", t=NT),
                                   cst[:, 2, :].rearrange("p (t h) -> p t h", t=NT), gate[:, :, 0:NH], ALU.mult))
            dve.wait_ge(lc_turned, 1)
            V.tensor_copy(lcT[:], ps[0:8 * NC_, 4, :].rearrange("p (a n) -> p a n", n=P)).then_inc(lcT_done, 1)
            dve.wait_ge(cmp_out, 1)
            for half in range(2):
                for T in range(NT):
                    src = ps[:, [5, 6, 7, 2][half * 2 + T], :]
                    a0 = T * NH + half * 8
                    ins = V.tensor_tensor(
                        ob[:, T, half * NB:(half + 1) * NB].rearrange("p (h d) -> p h d", d=DH),
                        src.rearrange("p (h d) -> p h d", d=DH),
                        cst[:, 2, a0:a0 + 8].unsqueeze(2).broadcast_to([P, 8, DH]), ALU.mult)
            ins.then_inc(o_evac, 1)
            dve.wait_ge(o_evac, 1)
            dve.wait_ge(bias_loaded, 16)

            def att(i):
                if i < 16:
                    T, half = (i // 2) % 2, (i // 4) % 2
                    grp = 2 * half + i % 2
                    nk = (T + 1) * P
                    dve.wait_ge(scores_done, i + 1)
                    if i >= 2:
                        dve.wait_ge(p_turned_all, i - 1)
                    for r in range(RG):
                        hh = grp * RG + r
                        bank = 4 + 2 * (i % 2) + r % 2
                        ins = V.tensor_tensor_reduce(
                            sg[:, i % 2, r, 0:nk], ps[:, bank, (r // 2) * S:(r // 2) * S + nk],
                            bias[:, hh, S - nk:S], 1.0, MASKED, ALU.add, ALU.max, ast_[:, i, 0, r:r + 1])
                    step(ins)
                    V.tensor_scalar(ast_[:, i, 1, :], ast_[:, i, 0, :], -SC, None, ALU.mult)\
                        .then_inc(logits_done, 1)
                if 1 <= i < 17:
                    k = i - 1
                    T = (k // 2) % 2
                    dve.wait_ge(p_turned_all, k + 1)
                    if k >= 2:
                        dve.wait_ge(pv_step, k - 1)
                    src = ps[:, 4 + 2 * (k % 2):6 + 2 * (k % 2), :].rearrange(
                        "p b (r t n) -> p (b r) t n", r=2, t=NT)
                    V.tensor_copy(pT[:, k % 2, :, 0:T + 1, :], src[:, :, 0:T + 1, :]).then_inc(pT_done, 1)
                if i >= 2 and (i - 2) % 2:
                    k = i - 2
                    T, half, br = (k // 2) % 2, (k // 4) % 2, k // 8
                    dve.wait_ge(pv_step, k + 1)
                    dve.wait_ge(exp_done, k + 1)
                    for s in (1, 0):
                        ins = V.reciprocal(grow[:, T, half * 8 + 4 * (1 - s):half * 8 + 4 * (1 - s) + 4],
                                           ast_[:, k - s, 2, :])
                    step(ins)
                    gs = grow[:, T, half * 8:half * 8 + 8]
                    step(V.tensor_tensor(gs, gs, gate[:, T, (br + 1) * NH + half * 8:(br + 1) * NH + half * 8 + 8],
                                           ALU.mult))
                    V.tensor_tensor(
                        ob[:, T, half * NB:(half + 1) * NB].rearrange("p (h d) -> p h d", d=DH),
                        ps[:, 2 + (k // 2) % 2, :].rearrange("p (h d) -> p h d", d=DH),
                        gs.unsqueeze(2).broadcast_to([P, 8, DH]), ALU.mult).then_inc(o_evac, 1)

            for kind, i in NSA_ORDER:
                if kind == "a":
                    att(i)
                    continue
                split_to(U["z"] + i + AHEAD)
                if i % 2:
                    n = i // 2
                    br, half = n // 2, n % 2
                    dve.wait_ge(z_done, n + 1)
                    dve.wait_ge(o_evac, max(1, 2 * (n - 1) + 1))
                    c = slice(half * NB, (half + 1) * NB)
                    if br == 0:
                        V.tensor_tensor(y[:, :, c], zt[:], ob[:, :, c], ALU.mult).then_inc(z_used, 1)
                    else:
                        step(V.tensor_tensor(ob[:, :, c], zt[:], ob[:, :, c], ALU.mult))
                        V.tensor_tensor(y[:, :, c], y[:, :, c], ob[:, :, c], ALU.add).then_inc(z_used, 1)
                    dve.wait_ge(z_used, n + 1)
            dve.wait_ge(yh_done, 1)
            V.tensor_tensor(xl[:].rearrange("p k n -> p (k n)"), ps[:, 4:8, :].rearrange("p b n -> p (b n)"),
                            xh[:].rearrange("p k n -> p (k n)").bitcast(F32), ALU.subtract)\
                .then_inc(yl_done, 1)
            split_to(U["in0"] + 1)
            dve.wait_ge(post_root, 1)
            step(V.reciprocal(st[:, 10:12], st[:, 6:8]))
            dve.wait_ge(postg_loaded, 16)
            for half in range(2):
                c = slice(half * NB, (half + 1) * NB)
                for i in range(NT):
                    ins = V.scalar_tensor_tensor(out=tok[:, i, c], in0=tok[:, i, c], scalar=st[:, 10 + i:11 + i],
                                                 in1=postg[:, c], op0=ALU.mult, op1=ALU.mult)
                step(ins)
                V.tensor_tensor(h[:, :, c], h[:, :, c], tok[:, :, c], ALU.add).then_inc(h_ready, 1)

            def ffn(nt, ub, bb, fb, high, low, extra=None, late=None):
                def turn(f):
                    dve.wait_ge(hidden_high, g.at(hidden_high, fb + f + 1))
                    src = ps[:, 4:6, :].rearrange("p t (k n) -> p k t n", k=KU) if nt == 2 else \
                        ps[:, 6 + f % 2, :].rearrange("p (k n) -> p k n", k=KU)
                    hi, lo = high[:, f * KU:(f + 1) * KU, :], low[:, f * KU:(f + 1) * KU, :]
                    if nt == 2:
                        for T in range(NT):
                            ins = V.tensor_tensor(lo[:, :, T * P:(T + 1) * P], src[:, :, T, :],
                                                  hi[:, :, T * P:(T + 1) * P].bitcast(F32), ALU.subtract)
                    else:
                        ins = V.tensor_tensor(lo, src, hi.bitcast(F32), ALU.subtract)
                    ins.then_inc(hidden_low, 1)

                for f in range(NFB):
                    b = bb + 2 * f + 1
                    split_to(ub + 4 * f + 3 + AHEAD)
                    dve.wait_ge(half_used, g.through(b))
                    dve.wait_ge(banks_free[(b - 1) % 2], g.freed(b - 1))
                    if fb + f:
                        dve.wait_ge(hidden_turned, g.at(hidden_turned, fb + f))
                    if nt == 2:
                        for T in range(NT):
                            ins = V.scalar_tensor_tensor(out=ht[:, T, :], in0=ps[:, pair(b) + T, :], scalar=factor(T),
                                                         in1=gt[:, T, :], op0=ALU.mult, op1=ALU.mult)
                    else:
                        ins = V.tensor_tensor(ht[:, 0, :], gt[:, 0, :], ps[:, pair(b), :], ALU.mult)
                    ins.then_inc(banks_free[b % 2], 1)
                    if f < NFB - 1:
                        split_to(ub + 4 * (f + 1) + 1 + AHEAD)
                        turn(f)
                if nt == 1:
                    split_to(ub + 4 * NFB + 1 + AHEAD)
                turn(NFB - 1)
                if extra:
                    split_to(ub + 4 * NFB + 5 + AHEAD)
                    extra()
                split_to(ub + UNITS_ROUND - 1 + (AHEAD if nt == 1 else 0))
                if late:
                    late()

            def mix(i):
                split_to(U[f"in{i}"])
                turned_low(3 * i + 1, 0)
                split_to(U[f"in{i}"] + 1)
                turned_low(3 * i + 1, 1)
                split_to(U[f"in{i}"] + 2)
                invert_root(3 * i + 1)
                dve.wait_ge(factor_done, 3 * i + 2)
                for T in range(NT):
                    ins = V.tensor_scalar(factor_diag[:, T * P:(T + 1) * P], ident, factor(T), None, ALU.mult)
                ins.then_inc(factor_diag_done, 1)
                ib, iu, ou = B[f"in{i}"], U[f"in{i}"], U[f"o{i}"]
                V.memset(cu[:, :, 0:2], 0.0)
                for j in range(2):
                    split_to(iu + 2 * j + 1 + AHEAD)
                    dve.wait_ge(banks_free[(ib + j) % 2], g.freed(ib + j))
                    step(V.tensor_tensor(sq[:], qk[:, j], qk[:, j], ALU.mult))
                    V.tensor_reduce(qk_ss[:, j].rearrange("p t h -> p (t h)"),
                                    sq[:].rearrange("p t (h d) -> p (t h) d", d=DH), AX, ALU.add)\
                        .then_inc(qk_squares, 1)
                    dve.wait_ge(qk_root, 2 * i + j + 1)
                    step(V.reciprocal(qk_ss[:, j], qk_ss[:, j]))
                    v = qk[:, j].rearrange("p t (h d) -> p (t h) d", d=DH)
                    V.tensor_tensor(v, v, qk_ss[:, j].rearrange("p t h -> p (t h)").unsqueeze(2)
                                    .broadcast_to([P, NT * SH, DH]), ALU.mult).then_inc(qk_normed, 1)
                split_to(iu + 5 + AHEAD)
                dve.wait_ge(qk_turned, i + 1)
                dve.wait_ge(mix_loaded, 16 * 20)
                V.tensor_scalar(qkT[:, 0].rearrange("p k n -> p (k n)"), ps[:, 4:6, :].rearrange("p b n -> p (b n)"),
                                qkg[:, i, 0:1], SC, ALU.mult, ALU.mult)
                V.tensor_scalar(qkT[:, 1].rearrange("p k n -> p (k n)"), ps[:, 6:8, :].rearrange("p b n -> p (b n)"),
                                qkg[:, i, 1:2], None, ALU.mult).then_inc(qkT_done, 1)
                dve.wait_ge(factor_copied, i + 1)
                step(V.tensor_tensor(factor_squares, factor_cols, factor_cols, ALU.mult))
                dve.wait_ge(banks_free[(ib + 3) % 2], g.freed(ib + 3))
                step(V.tensor_tensor(uT[:], uT[:], factor_squares.unsqueeze(1).broadcast_to([P, 4, S]), ALU.mult))

                def softplus(hb):
                    n = 2 * i + hb
                    dve.wait_ge(z_scores, n + 1)
                    if n:
                        dve.wait_ge(stick_done, n)
                    dve.wait_ge(ln_done, n + 1)
                    step(V.scalar_tensor_tensor(out=spb[:], in0=ps[:, 4:8, 0:3 * P], scalar=0.0, in1=spa[:],
                                                  op0=ALU.max, op1=ALU.add))
                    for c in (0, 2 * P):
                        ins = V.tensor_tensor(spb[:, :, c:c + P], spb[:, :, c:c + P],
                                              keep.unsqueeze(1).broadcast_to([P, 4, P]), ALU.mult)
                    ins.then_inc(sp_done, 1)

                split_to(iu + 10)
                softplus(0)
                split_to(iu + 11)
                b = ib + 4
                dve.wait_ge(banks_free[(ib + 3) % 2], g.freed(ib + 3))
                dve.wait_ge(half_used, g.through(b))
                V.tensor_tensor(cu[:, :, 2:S + 2],
                                ps[:, pair(b):pair(b) + 2, :].rearrange("p b (k n) -> p (b k) n", n=S),
                                uT[:], ALU.mult).then_inc(banks_free[b % 2], 1)
                dve.wait_ge(banks_free[b % 2], g.freed(b))
                for j in range(4):
                    ins = V.tensor_scalar(cv[:, j, :], cu[:, j, 0:S], convw[:, i, j, 0:1], convw[:, i, j, 3:4],
                                          ALU.mult, ALU.add)
                step(ins)
                for k in (1, 2):
                    for j in range(4):
                        ins = V.scalar_tensor_tensor(out=cv[:, j, :], in0=cu[:, j, k:k + S],
                                                     scalar=convw[:, i, j, k:k + 1], in1=cv[:, j, :],
                                                     op0=ALU.mult, op1=ALU.add)
                    step(ins)
                step(V.tensor_tensor(cv[:], cv[:], factor_cols.unsqueeze(1).broadcast_to([P, 4, S]), ALU.mult))
                split_to(ou + 1)
                b = ib + 5
                dve.wait_ge(half_used, g.through(b))
                V.tensor_tensor(mixT[:, 4:8, :],
                                ps[:, pair(b):pair(b) + 2, :].rearrange("p b (k n) -> p (b k) n", n=S),
                                cv[:], ALU.mult).then_inc(banks_free[b % 2], 1)

                def low_part(j0, j1, src, semaphore):
                    for j in range(j0, j1):
                        m = mix_tile(j)
                        ins = V.scalar_tensor_tensor(out=xl[:, m, :].rearrange("p (t n) -> p t n", t=NT), in0=src(j),
                                                     scalar=ogain[:, i, j:j + 1],
                                                     in1=xh[:, m, :].bitcast(F32).rearrange("p (t n) -> p t n", t=NT),
                                                     op0=ALU.mult, op1=ALU.subtract)
                    ins.then_inc(semaphore, 1)

                def mixed(j):
                    return mixT[:, j, :].rearrange("p (t n) -> p t n", t=NT)

                def add_part(b):
                    j = (b - B[f"o{i}"]) % 2
                    dve.wait_ge(half_used, g.through(b))
                    for T in range(NT):
                        c = slice(j * NB, (j + 1) * NB)
                        ins = V.scalar_tensor_tensor(out=h[:, T, c], in0=ps[:, pair(b) + T, :],
                                                     scalar=st[:, 28 + T:29 + T], in1=h[:, T, c], op0=ALU.mult,
                                                     op1=ALU.add)
                    ins.then_inc(banks_free[b % 2], 1)

                dve.wait_ge(conv_high, i + 1)
                low_part(KU, 2 * KU, mixed, conv_low)
                dve.wait_ge(mix_sums, 2 * i + 1)
                V.tensor_copy(st[:, 24:26], ps[:, pair(B[f"o{i}"] + 1), 0:NT]).then_inc(conv_sums_copied, 1)
                split_to(ou + 2)
                softplus(1)
                dve.wait_ge(mix_root, 2 * i + 1)
                step(V.reciprocal(st[:, 28:30], st[:, 26:28]))
                add_part(B[f"o{i}"])
                add_part(B[f"o{i}"] + 1)
                split_to(ou + 3)
                dve.wait_ge(mixh_done, i + 1)
                low_part(0, 2, mixed, mixl_done)
                dve.wait_ge(mix_squares, 2 * i + 2)
                low_part(2, 4, lambda j: pv_place(j - 2), mixl_done)
                k, nu = 3 * i + 2, U[f"ffn{i}"]
                dve.wait_ge(mix_root, 2 * i + 2)
                dve.wait_ge(banks_free[(B[f"o{i}"]) % 2], g.freed(B[f"o{i}"]))
                dve.wait_ge(banks_free[(B[f"o{i}"] + 1) % 2], g.freed(B[f"o{i}"] + 1))
                step(V.reciprocal(st[:, 28:30], st[:, 26:28]))
                for j in range(2):
                    add_part(B[f"o{i}"] + 2 + j)
                    split_to(nu + j)
                    turned_low(k, j)

            def ple(i):
                ub, bb = U[f"ple{i}"], B[f"ple{i}"]
                split_to(ub)
                turned_low(3 * i + 3, 0)
                split_to(ub + 1)
                turned_low(3 * i + 3, 1)
                split_to(ub + 2)
                invert_root(3 * i + 3)
                split_to(ub + 3)
                dve.wait_ge(ph_done, i + 1)
                V.tensor_tensor(ptTl[:].rearrange("p k n -> p (k n)"), ps[:, 4, :],
                                ptTh[:].rearrange("p k n -> p (k n)").bitcast(F32), ALU.subtract)\
                    .then_inc(pl_done, 1)
                for j in range(2):
                    split_to(min(ub + 2 * j + 1 + AHEAD, ub + 5))
                for j in range(2):
                    b = bb + 2 + j
                    if i == 0 and j == 0:
                        split_to(ub + 6)
                    dve.wait_ge(banks_free[(b - 2) % 2], g.freed(b - 2))
                    dve.wait_ge(half_used, g.through(b))
                    if i or j:
                        dve.wait_ge(h_half, 2 * i + j)
                    V.tensor_tensor(pm[:], ps[:, pair(b):pair(b) + 2, :], pg[:, j], ALU.mult).then_inc(banks_free[b % 2], 1)
                    dve.wait_ge(banks_free[b % 2], g.freed(b))
                    c = slice(j * NB, (j + 1) * NB)
                    V.tensor_tensor(h[:, :, c], h[:, :, c], pm[:], ALU.add).then_inc(h_half, 1)
                dve.wait_ge(h_half, 2 * i + 2)

            mix(0)
            split_to(U["ffn0"] + 2)
            invert_root(2)
            dve.wait_ge(factor_done, 3)

            def add_dense():
                for j in range(2):
                    dve.wait_ge(half_used, 2 * (U["ple0"] - 1 + j))
                    c = slice(j * NB, (j + 1) * NB)
                    for T in range(NT):
                        ins = V.tensor_tensor(h[:, T, c], h[:, T, c], ps[:, 4 + 2 * T + j, :], ALU.add)
                    ins.then_inc(h_ready, 1)
                    if j == 0:
                        split_to(U["ple0"])
            ffn(2, U["ffn0"], B["ffn0"], 0, hTh, hTl, late=add_dense)
            ple(0)
            mix(1)
            invert_root(5)
            dve.wait_ge(factor_done, 6)
            for T in range(NT):
                ins = V.tensor_scalar(tok[:, T, :], h[:, T, :], factor(T), None, ALU.mult)
            ins.then_inc(h_normed, 1)
            dve.wait_ge(router_high, 1)
            V.tensor_tensor(rwl[:], rw[:], rwh[:].bitcast(F32), ALU.subtract).then_inc(router_low, 1)
            dve.wait_ge(xn_high, 1)
            V.tensor_tensor(xnl[:], tok[:], xnh[:].bitcast(F32), ALU.subtract).then_inc(xn_low, 1)
            dve.wait_ge(router_logits, 1)
            for T in range(NT):
                ins = V.tensor_scalar(lg[:, T], ps[:, 0, T * NE:(T + 1) * NE], factor(T), None, ALU.mult)
            step(ins)
            other = lg[:].unsqueeze(2).broadcast_to([P, NT, NE, NE])
            own = lg[:].unsqueeze(3).broadcast_to([P, NT, NE, NE])
            for T in range(NT):
                V.tensor_tensor(cmpa[:, T], other[:, T], own[:, T], ALU.is_gt)
                ins = V.tensor_tensor(cmpb[:, T], other[:, T], own[:, T], ALU.is_equal)
            step(ins)
            for T in range(NT):
                ins = V.tensor_tensor(cmpb[:, T], cmpb[:, T], tril8.rearrange("p (a b) -> p a b", a=NE), ALU.mult)
            step(ins)
            step(V.tensor_tensor(cmpa[:], cmpa[:], cmpb[:], ALU.add))
            step(V.tensor_reduce(sel[:].rearrange("p t e -> p (t e)"),
                                   cmpa[:].rearrange("p t a b -> p (t a) b"), AX, ALU.add))
            V.tensor_scalar(sel[:], sel[:], 2.0, None, ALU.is_lt).then_inc(sel_done, 1)
            dve.wait_ge(sel_done, 1)
            step(V.tensor_reduce(st[:, 12:14], lg[:], AX, ALU.max))
            for T in range(NT):
                ins = V.tensor_scalar(gw[:, T], lg[:, T], st[:, 12 + T:13 + T], None, ALU.subtract)
            ins.then_inc(logit_shift, 1)
            dve.wait_ge(gate_exp, 1)
            step(V.tensor_tensor(gw[:], gw[:], sel[:], ALU.mult))
            step(V.tensor_reduce(st[:, 14:16], gw[:], AX, ALU.add))
            step(V.reciprocal(st[:, 16:18], st[:, 14:16]))
            for T in range(NT):
                ins = V.tensor_scalar(gw[:, T], gw[:, T], st[:, 16 + T:17 + T], None, ALU.mult)
            step(ins)
            dve.wait_ge(slots_counted, 1)
            V.tensor_scalar(slot[:, :, 0:NE], ps[:, 1, 0:NT * NE].rearrange("p (t e) -> p t e", t=NT), 1.0, None,
                            ALU.add)
            step(V.tensor_reduce(cnt[:, NE:NE + 1], ps[:, 1, NT * NE:NT * NE + NE], AX, ALU.max))
            step(V.tensor_tensor(slot[:, :, 0:NE], slot[:, :, 0:NE], sel[:], ALU.mult))
            step(V.tensor_scalar(slot[:, :, 0:NE], slot[:, :, 0:NE], 1.0, None, ALU.subtract))
            V.tensor_scalar(slot[:, :, NE:2 * NE], slot[:, :, 0:NE], float(P), None, ALU.subtract)
            V.memset(slot[:, :, 2 * NE:2 * NE + 1], -1.0)
            step(V.tensor_scalar(cnt[:, NE + 1:NE + 2], cnt[:, NE:NE + 1], float(P), float(NE), ALU.is_gt, ALU.mult))
            step(V.tensor_scalar(cnt[:, NE + 2:NE + 3], cnt[:, NE + 1:NE + 2], float(NE), None, ALU.add))
            V.tensor_copy(nround[:], cnt[0:1, NE + 2:NE + 3]).then_inc(rounds_known, 1)

            def make_pick(col, n):
                if n:
                    dve.wait_ge(pick_turned, g.at(pick_turned, n))
                for T in range(NT):
                    ins = V.tensor_scalar(pick[:, T, :], iota, slot[:, T, col], None, ALU.is_equal)
                ins.then_inc(pick_done, 1)

            def split_gathered(n):
                dve.wait_ge(gather_high, g.at(gather_high, n + 1))
                for j in range(KD):
                    ins = V.scalar_tensor_tensor(
                        out=xgl[:, j, :], in0=ps[:, 6 + j // 4, (j % 4) * P:(j % 4 + 1) * P],
                        scalar=gains[:, 5, j:j + 1], in1=xgh[:, j, :].bitcast(F32), op0=ALU.mult,
                        op1=ALU.subtract)
                ins.then_inc(gather_low, 1)

            dve.wait_ge(rounds_known, 1)
            make_pick(slice(0, 1), 0)
            V.memset(st[:, 20:21], 0.0).then_inc(round_done, 1)
            split_gathered(0)
            rounds = dve.value_load(nround[0:1, 0:1], min_val=NE, max_val=2 * NE)
            with dve.Fori(0, rounds) as r:
                g.r = r
                e = r % NE

                def next_tokens():
                    make_pick(bass.ds(r + 1, 1), 1)
                    split_gathered(1)
                ffn(1, U["ffn1"], B["ffn1"], NFB, mTh, mTl, extra=next_tokens)
                dve.wait_ge(y_high, g.at(y_high, 1))
                V.tensor_tensor(yl[:], ps[:, 4:6, :].rearrange("p b n -> p (b n)"), yh[:].bitcast(F32),
                                ALU.subtract).then_inc(y_low, 1)
                dve.wait_ge(scatter_done, g.at(scatter_done, 1))
                for T in range(NT):
                    ins = V.scalar_tensor_tensor(
                        out=h[:, T, :], in0=ps[:, (6 if T == 0 else 4):(8 if T == 0 else 6), :]
                        .rearrange("p b n -> p (b n)"),
                        scalar=gw[:, T, bass.ds(e, 1)], in1=h[:, T, :], op0=ALU.mult, op1=ALU.add)
                ins.then_inc(round_done, 1)
                dve.wait_ge(round_done, g.at(round_done, 2))
            g.r = rounds
            g.split = U["ffn1"] + 2
            g.post = True
            ple(1)

        @block_.tensor
        def _(pe):
            g = Prog()
            mm = nc.tensor.matmul

            def turn(dst, src, idn=None):
                return nc.tensor.transpose(dst, src, ident if idn is None else idn)

            def split_view(u, nk, n):
                s = u % SPL
                return (whi[:, s, 0:nk * n].rearrange("p (k n) -> p k n", k=nk),
                        wlo[:, s, 0:nk * n].rearrange("p (k n) -> p k n", k=nk))

            def products(u, nk, n, hi, lo, k0, outs, first, last, middle=None):
                wh, wl = split_view(u, nk, n)
                for half in range(2):
                    if half and middle:
                        middle()
                    ks = range(half * nk // 2, (half + 1) * nk // 2)
                    pe.wait_ge(high_done, g.at(high_done, 2 * u + half + 1))
                    for k in ks:
                        for T, o in enumerate(outs):
                            mm(o, hi(k0 + k, T), wh[:, k, :], start=first and k == 0, stop=False)
                            mm(o, lo(k0 + k, T), wh[:, k, :], start=False, stop=False)
                    pe.wait_ge(low_done, g.at(low_done, 2 * u + half + 1))
                    for k in ks:
                        for T, o in enumerate(outs):
                            ins = mm(o, hi(k0 + k, T), wl[:, k, :], start=False, stop=last and k == nk - 1)
                    ins.then_inc(half_used, 1)

            def tile_of(x):
                return lambda k, T: x[:, k, T * P:(T + 1) * P]

            def block(u, b, hi, lo, kt=KD, n=NB, nt=NT, units=None, norm=None, between=None):
                bank = pair(b)
                outs = [ps[:, bank + T, 0:n] for T in range(nt)]
                start_block(b)
                ku = units or KU
                nu = -(-kt // ku)
                for i in range(nu):
                    if norm is not None:
                        pe.wait_ge(xl_done, 2 * norm + i + 1)
                    if i and between:
                        between()
                    products(u + i, min(ku, kt - i * ku), n, hi, lo, i * ku, outs, i == 0, i == nu - 1,
                             (lambda: turn_rows(norm, 1)) if norm and i == 0 else None)

            def start_block(b):
                back = b - 2 if b - 2 not in z_blocks else B["z"] - (2 if (b - B["z"]) % 2 == 0 else 1)
                if back >= 0:
                    pe.wait_ge(banks_free[back % 2], g.freed(back))

            def turn_all(src):
                for j in range(KD):
                    for T in range(NT):
                        ins = turn(ps[:, 4 + j // 2, (j % 2) * S + T * P:(j % 2) * S + (T + 1) * P],
                                   src[:, T, j * P:(j + 1) * P])
                return ins

            def turn_rows(k, half):
                if k == 0 and half == 0:
                    pe.wait_ge(x_loaded, 16)
                elif k == 1:
                    pe.wait_ge(h_ready, half + 1)
                elif k in (2, 5):
                    b = B[f"o{k // 3}"] + 2 + half
                    pe.wait_ge(banks_free[b % 2], g.freed(b))
                elif k == 3:
                    pe.wait_ge(h_ready, 2 + half + 1)
                elif k == 4:
                    pe.wait_ge(h_half, half + 1)
                elif k == 6 and half == 0:
                    pe.wait_ge(round_done, g.at(round_done, 1))
                for j in range(half * KU, (half + 1) * KU):
                    for T in range(NT):
                        ins = turn(turned_place(k, j)[:, T * P:(T + 1) * P], h[:, T, j * P:(j + 1) * P])
                ins.then_inc(h_turned, 1)

            pe.wait_ge(con_loaded, 16)
            turn_rows(0, 0)
            turn_rows(0, 1)
            pe.wait_ge(oh_loaded, 32)
            pe.wait_ge(table_one, 1)
            mm(ps[0:NH, 0, 0:LREV], tabx[:], oh[:, 512:512 + LREV], start=True, stop=True)\
                .then_inc(tab_product, 1)
            for T in range(NT):
                for c in range(NC_):
                    i0 = 256 + P * T - CS * c - (CB - 1)
                    o = (T * NC_ + c) * NH
                    ins = mm(ps[:, 1, o:o + NH], oh[:, i0:i0 + P], tabx[:], start=True, stop=True)
            ins.then_inc(tab_product, 1)
            X = (tile_of(xh), tile_of(xl))
            pe.wait_ge(rev_ready, 1)
            pe.wait_ge(cbias_done, 1)
            block(U["kv_c"], B["kv_c"], *X, norm=0)
            block(U["q"], B["q"], *X)
            pe.wait_ge(banks_free[(B["kv_c"]) % 2], g.freed(B["kv_c"]))
            for a in range(2 * NG):
                for T in range(NT):
                    ins = turn(ps[:, 4 + a // 2, (a % 2) * S + T * P:(a % 2) * S + (T + 1) * P],
                               kc2[:, T, a].rearrange("p s d -> p (s d)"))
            ins.then_inc(kc_turned, 1)
            block(U["q"] + 2, B["q"] + 1, *X)
            block(U["kv_s"], B["kv_s"], *X)
            pe.wait_ge(banks_free[(B["q"]) % 2], g.freed(B["q"]))
            pe.wait_ge(banks_free[(B["q"] + 1) % 2], g.freed(B["q"] + 1))
            pe.wait_ge(windows_done, 1)
            turn_all(tok).then_inc(q_turned, 1)
            block(U["kv_w"], B["kv_w"], *X)
            block(U["gate"], B["gate"], *X, n=3 * NH, units=KD)
            pe.wait_ge(banks_free[(B["kv_s"]) % 2], g.freed(B["kv_s"]))
            pe.wait_ge(banks_free[(B["kv_w"]) % 2], g.freed(B["kv_w"]))
            pe.wait_ge(qT_done, 1)
            for i in range(2):
                for a in range(NG):
                    for T in range(NT):
                        ins = turn(ps[:, 4 + 2 * i + a // 2, (a % 2) * S + T * P:(a % 2) * S + (T + 1) * P],
                                   kd[:, i, T, a].rearrange("p s d -> p (s d)"))
            ins.then_inc(k_turned, 1)
            pe.wait_ge(window_low, 1)
            for kv in range(2):
                def window(x, kv=kv):
                    return lambda k, T: x[:, (kv * CB // 2 + k) * NG * NC_:(kv * CB // 2 + k) * NG * NC_ + P]
                block(U["cmp"] + 2 * kv, B["cmp"] + kv, window(xwh), window(xwl), kt=CB // 2, n=HC, nt=1, units=8)
            pe.wait_ge(banks_free[(B["cmp"]) % 2], g.freed(B["cmp"]))
            pe.wait_ge(banks_free[(B["cmp"] + 1) % 2], g.freed(B["cmp"] + 1))
            pe.wait_ge(kT_done, 1)
            for kv in range(2):
                for j in range(2):
                    o = (kv * 2 + j) * NG * NC_
                    ins = turn(ps[:, 4, o:o + NG * NC_], hc[:, kv, j * P:(j + 1) * P],
                               ident[0:NG * NC_, 0:NG * NC_])
            ins.then_inc(hc_turned, 1)
            pe.wait_ge(hcT_done, 1)
            for j in range(2):
                mm(ps[:, 5, 0:NG * NC_], w2k[:, j].rearrange("p s d -> p (s d)"), hcT[:, 0, j, :],
                   start=j == 0, stop=j == 1)
            for half in range(2):
                for j in range(2):
                    ins = mm(ps[0:8 * NC_, 6, half * DH:(half + 1) * DH], hcR[:, half, j, :], w2v[:, j, :],
                             start=j == 0, stop=j == 1)
            ins.then_inc(kcvc_product, 1)
            pe.wait_ge(kcT_done, 1)
            for T in range(NT):
                for hh in range(NH):
                    q = slice((hh % 2) * DH, (hh % 2 + 1) * DH)
                    o = (T * 8 + hh // 2) * NC_
                    ins = mm(ps[:, 4 + hh % 2, o:o + NC_], qT[q, hh // 2, T * P:(T + 1) * P],
                             kcT[q, (hh // RG) * NC_:(hh // RG + 1) * NC_], start=True, stop=True)
            ins.then_inc(cmp_scores, 1)
            pe.wait_ge(cmp_exp, 1)
            for half in range(2):
                for T in range(NT):
                    a = half * 2 + T
                    ins = turn(ps[0:8 * NC_, 4, a * P:(a + 1) * P],
                               lc[:, T, half * 8:half * 8 + 8, :].rearrange("p h c -> p (h c)"))
            ins.then_inc(lc_turned, 1)
            pe.wait_ge(lcT_done, 1)
            pe.wait_ge(vcb_done, 1)
            for a in range(4):
                ins = mm(ps[:, [5, 6, 7, 2][a], :], lcT[:, a, :], vcb[:, a // 2].rearrange("p h d -> p (h d)"),
                         start=True, stop=True)
            ins.then_inc(cmp_out, 1)

            def att(i):
                if i >= 2:
                    k = i - 2
                    T, half, br = (k // 2) % 2, (k // 4) % 2, k // 8
                    grp = 2 * half + k % 2
                    pe.wait_ge(pT_done, k + 1)
                    if k % 2 == 0:
                        pe.wait_ge(o_evac, max(1, k // 2))
                    for r in range(RG):
                        o = ps[:, 2 + (k // 2) % 2, (k % 2) * RG * DH + r * DH:(k % 2) * RG * DH + (r + 1) * DH]
                        rr = (r % 2) * 2 + r // 2
                        for kt in range(T + 1):
                            ins = mm(o, pT[:, k % 2, rr, kt, :], vs[:, br, kt, grp * DH:(grp + 1) * DH],
                                     start=kt == 0, stop=kt == T)
                    ins.then_inc(pv_step, 1)
                if i < 16:
                    T, half, br = (i // 2) % 2, (i // 4) % 2, i // 8
                    grp = 2 * half + i % 2
                    nk = (T + 1) * P
                    if i >= 2:
                        pe.wait_ge(pT_done, i - 1)
                    else:
                        pe.wait_ge(o_evac, 1)
                    for r in range(RG):
                        hh = grp * RG + r
                        q = slice((hh % 2) * DH, (hh % 2 + 1) * DH)
                        ins = mm(ps[:, 4 + 2 * (i % 2) + r % 2, (r // 2) * S:(r // 2) * S + nk],
                                 qT[q, hh // 2, T * P:(T + 1) * P], kT[q, br, grp, 0:nk], start=True, stop=True)
                    ins.then_inc(scores_done, 1)
                if 1 <= i < 17:
                    k = i - 1
                    T = (k // 2) % 2
                    pe.wait_ge(exp_done, k + 1)
                    for r in range(RG):
                        for kt in range(T + 1):
                            c = (r // 2) * S + kt * P
                            ins = turn(ps[:, 4 + 2 * (k % 2) + r % 2, c:c + P], sg[:, k % 2, r, kt * P:(kt + 1) * P])
                    ins.then_inc(p_turned_all, 1)

            zouts = [ps[:, T, :] for T in range(NT)]
            for kind, i in NSA_ORDER:
                if kind == "a":
                    att(i)
                    continue
                if i % 2 == 0:
                    if i:
                        pe.wait_ge(z_done, i // 2)
                products(U["z"] + i, KU, NB, *X, (i % 2) * KU, zouts, i % 2 == 0, i % 2 == 1)
            pe.wait_ge(z_used, 6)
            turn_all(y).then_inc(y_turned, 1)
            pe.wait_ge(yl_done, 1)
            pe.wait_ge(z_done, 6)
            for i in range(2):
                b = B["nsa_out"] + i
                outs = [ps[:, pair(b) + T, :] for T in range(NT)]
                for k in range(2):
                    products(U["nsa_out"] + 2 * i + k, KU, NB, *X, k * KU, outs, k == 0, k == 1)

            def ffn(nt, ub, bb, fb, x, hx, acc, first_extra=None, extra=None):
                def turn_hidden(f):
                    pe.wait_ge(banks_free[(bb + 2 * f + 1) % 2], g.freed(bb + 2 * f + 1))
                    if nt == 2:
                        if f:
                            pe.wait_ge(hidden_low, g.at(hidden_low, f))
                        for T in range(NT):
                            for k in range(KU):
                                ins = turn(ps[:, 4 + T, k * P:(k + 1) * P], ht[:, T, k * P:(k + 1) * P])
                    else:
                        if f >= 2:
                            pe.wait_ge(hidden_low, g.at(hidden_low, fb + f - 1))
                        elif f == 0:
                            pe.wait_ge(pick_copied, g.at(pick_copied, 1))
                        for k in range(KU):
                            ins = turn(ps[:, 6 + f % 2, k * P:(k + 1) * P], ht[:, 0, k * P:(k + 1) * P])
                    ins.then_inc(hidden_turned, 1)

                for f in range(NFB):
                    block(ub + 4 * f, bb + 2 * f, *x, nt=nt, norm=2 if nt == 2 and f == 0 else None)
                    if f:
                        turn_hidden(f - 1)
                    elif first_extra:
                        first_extra()
                    block(ub + 4 * f + 2, bb + 2 * f + 1, *x, nt=nt)
                u = ub + 4 * NFB
                nk = FF // P
                if nt == 2:
                    turn_hidden(NFB - 1)
                    pe.wait_ge(hidden_low, g.at(hidden_low, NFB))
                for k0 in range(0, nk, KU):
                    if nt == 1:
                        if k0 == 0:
                            pe.wait_ge(hidden_low, g.at(hidden_low, fb + NFB - 1))
                        if k0 == KU:
                            turn_hidden(NFB - 1)
                        if k0 == 3 * KU and extra:
                            extra()
                        if k0 == nk - KU:
                            pe.wait_ge(hidden_low, g.at(hidden_low, fb + NFB))
                    for half in range(2):
                        last = nt == 2 and k0 == nk - KU and half == 1
                        products(u, KU, NB, *hx, k0, [ps[:, acc(T, half), :] for T in range(nt)], k0 == 0,
                                 k0 == nk - KU, (lambda: turn_rows(3, 0)) if last else None)
                        u += 1

            def mix(i):
                turn_rows(3 * i + 1, 0)
                ib, iu = B[f"in{i}"], U[f"in{i}"]
                for j in range(3):
                    block(iu + 2 * j, ib + j, *X, norm=3 * i + 1 if j == 0 else None)
                    if j == 0:
                        pe.wait_ge(factor_diag_done, i + 1)
                        mm(ps[:, 4, 0:S], ones, factor_diag, start=True, stop=True).then_inc(factor_spread, 1)
                pe.wait_ge(qk_normed, 2 * i + 2)
                pe.wait_ge(factor_copied, i + 1)
                for j in range(2):
                    for a in range(4):
                        for T in range(NT):
                            ins = turn(ps[:, 4 + 2 * j + a // 2, (a % 2) * S + T * P:(a % 2) * S + (T + 1) * P],
                                       qk[:, j, T, a * P:(a + 1) * P])
                ins.then_inc(qk_turned, 1)

                def units_T(j, v):
                    b = ib + j
                    if v == 0:
                        start_block(b)
                    u = iu + 2 * j + v
                    wh, wl = split_view(u, KU, NB)
                    for half in range(2):
                        ks = range(half * KU // 2, (half + 1) * KU // 2)
                        pe.wait_ge(high_done, g.at(high_done, 2 * u + half + 1))
                        for k in ks:
                            kk = v * KU + k
                            for c in range(4):
                                o = ps[:, pair(b) + c // 2, (c % 2) * S:(c % 2 + 1) * S]
                                w_ = wh[:, k, c * P:(c + 1) * P]
                                mm(o, w_, xh[:, kk, :], start=kk == 0 and c % 2 == 0, stop=False,
                                   skip_group_check=True)
                                mm(o, w_, xl[:, kk, :], start=False, stop=False, skip_group_check=True)
                        pe.wait_ge(low_done, g.at(low_done, 2 * u + half + 1))
                        for k in ks:
                            kk = v * KU + k
                            for c in range(4):
                                o = ps[:, pair(b) + c // 2, (c % 2) * S:(c % 2 + 1) * S]
                                ins = mm(o, wl[:, k, c * P:(c + 1) * P], xh[:, kk, :], start=False,
                                         stop=kk == KD - 1, skip_group_check=True)
                        ins.then_inc(half_used, 1)

                def scores(hb):
                    if hb:
                        pe.wait_ge(pv_copied, i + 1)
                    for a in range(4):
                        hh = hb * 4 + a
                        q = slice((hh % 2) * DH, (hh % 2 + 1) * DH)
                        mm(ps[:, 4 + a, 0:S], qkT[q, 1, hh // 2, 0:P], qkT[q, 0, hh // 2, :], start=True,
                           stop=False, skip_group_check=True)
                        ins = mm(ps[:, 4 + a, S:S + P], qkT[q, 1, hh // 2, P:S], qkT[q, 0, hh // 2, P:S],
                                 start=False, stop=False, skip_group_check=True)
                    ins.then_inc(z_scores, 1)

                def stick(hb):
                    pe.wait_ge(sp_done, 2 * i + hb + 1)
                    for a in range(4):
                        for o, w_, x in (((0, S), ntri, (0, S)), ((S, S + P), ntri, (S, S + P)),
                                         ((P, S), nones, (S, S + P)), ):
                            mm(ps[:, 4 + a, o[0]:o[1]], w_, spb[:, a, x[0]:x[1]], start=False, stop=False,
                               skip_group_check=True)
                        for c in (0, S):
                            ins = mm(ps[:, 4 + a, c:c + P], ident, negm, start=False, stop=c == S,
                                     skip_group_check=True)
                    ins.then_inc(stick_done, 1)

                def pv(hb):
                    pe.wait_ge(stick_exp, 2 * i + hb + 1)
                    for a in range(4):
                        hh = hb * 4 + a
                        q = slice((hh % 2) * DH, (hh % 2 + 1) * DH)
                        o = [ps[q, 4 + 2 * (a // 2) + T, 3 * P:4 * P] for T in range(NT)]
                        v_ = [v2[:, T, hh * DH:(hh + 1) * DH] for T in range(NT)]
                        mm(o[0], v_[0], wT[:, a, 0:P], start=True, stop=True, skip_group_check=True)
                        mm(o[1], v_[0], wT[:, a, P:S], start=True, stop=False, skip_group_check=True)
                        ins = mm(o[1], v_[1], wT[:, a, S:S + P], start=False, stop=True, skip_group_check=True)
                    ins.then_inc(pv_done, 1)

                def sums(bank, j0):
                    for T in range(NT):
                        for j in range(j0, j0 + KU):
                            ins = mm(ps[:, bank, T:T + 1], mixs[:, j, T * P:(T + 1) * P], ones[:, 0:1],
                                     start=j == j0, stop=j == j0 + KU - 1)
                    ins.then_inc(mix_sums, 1)

                def project(j):
                    b = B[f"o{i}"] + j
                    start_block(b)
                    products(U[f"o{i}"] + j, KU, NB, *X, 0 if j < 2 else KU, [ps[:, pair(b) + T, :] for T in range(NT)],
                             True, True)

                units_T(3, 0)
                units_T(3, 1)
                pe.wait_ge(qkT_done, i + 1)
                scores(0)
                units_T(4, 0)
                units_T(4, 1)
                units_T(5, 0)
                stick(0)
                units_T(5, 1)
                pv(0)
                scores(1)
                pe.wait_ge(mix_squares, 2 * i + 1)
                sums(pair(B[f"o{i}"] + 1), KU)
                pe.wait_ge(conv_low, i + 1)
                project(0)
                pe.wait_ge(conv_sums_copied, i + 1)
                project(1)
                stick(1)
                pv(1)
                pe.wait_ge(mix_squares, 2 * i + 2)
                pe.wait_ge(mixl_done, 2 * i + 2)
                sums(7, 0)
                project(2)
                turn_rows(3 * i + 2, 0)
                project(3)

            def ple(i):
                ub, bb = U[f"ple{i}"], B[f"ple{i}"]
                if i:
                    turn_rows(6, 0)
                block(ub, bb, *X, norm=3 * i + 3)
                pe.wait_ge(p_loaded, 16 * (i + 1))
                for k in range(2):
                    for T in range(NT):
                        ins = turn(ps[:, 4, k * S + T * P:k * S + (T + 1) * P], pt_in[:, T, k * P:(k + 1) * P])
                ins.then_inc(p_turned, 1)
                block(ub + 2, bb + 1, *X)
                pe.wait_ge(pl_done, i + 1)
                for j in range(2):
                    block(ub + 4 + j, bb + 2 + j, tile_of(ptTh), tile_of(ptTl), kt=2)

            mix(0)
            ffn(2, U["ffn0"], B["ffn0"], 0, X, (tile_of(hTh), tile_of(hTl)), lambda T, half: 4 + 2 * T + half)
            ple(0)
            mix(1)
            turn_rows(5, 1)
            pe.wait_ge(xl_done, 12)
            pe.wait_ge(router_low, 1)
            pe.wait_ge(banks_free[(B["o1"]) % 2], g.freed(B["o1"]))
            pe.wait_ge(banks_free[(B["o1"] + 1) % 2], g.freed(B["o1"] + 1))
            for T in range(NT):
                o = ps[:, 0, T * NE:(T + 1) * NE]
                for k in range(KD):
                    a, b = xh[:, k, T * P:(T + 1) * P], xl[:, k, T * P:(T + 1) * P]
                    mm(o, a, rwh[:, k, :], start=k == 0, stop=False)
                    mm(o, a, rwl[:, k, :], start=False, stop=False)
                    ins = mm(o, b, rwh[:, k, :], start=False, stop=k == KD - 1)
            ins.then_inc(router_logits, 1)
            pe.wait_ge(sel_done, 1)
            mm(ps[:, 1, 0:NE], stri, sel[:, 0, :], start=True, stop=True)
            mm(ps[:, 1, NE:2 * NE], stri, sel[:, 1, :], start=True, stop=False)
            mm(ps[:, 1, NE:2 * NE], ones, sel[:, 0, :], start=False, stop=True)
            mm(ps[:, 1, 2 * NE:3 * NE], ones, sel[:, 0, :], start=True, stop=False)
            mm(ps[:, 1, 2 * NE:3 * NE], ones, sel[:, 1, :], start=False, stop=True).then_inc(slots_counted, 1)

            def gather(n):
                pe.wait_ge(pick_done, g.at(pick_done, n + 1))
                if n:
                    pe.wait_ge(hidden_low, g.at(hidden_low, 2 * NFB))
                else:
                    pe.wait_ge(xn_low, 1)
                for j in range(KD):
                    o = ps[:, 6 + j // 4, (j % 4) * P:(j % 4 + 1) * P]
                    for T in range(NT):
                        mm(o, xnh[:, T, j * P:(j + 1) * P], pick[:, T, :], start=T == 0, stop=False)
                        ins = mm(o, xnl[:, T, j * P:(j + 1) * P], pick[:, T, :], start=False, stop=T == 1)
                ins.then_inc(gathered, 1)

            gather(0)
            pe.wait_ge(rounds_known, 1)
            rounds = pe.value_load(nround[0:1, 0:1], min_val=NE, max_val=2 * NE)
            G = (lambda k, T: xgh[:, k, :], lambda k, T: xgl[:, k, :])
            M = (lambda k, T: mTh[:, k, :], lambda k, T: mTl[:, k, :])
            with pe.Fori(0, rounds) as r:
                g.r = r
                pe.wait_ge(gather_low, g.at(gather_low, 1))

                def turn_pick():
                    pe.wait_ge(round_done, g.at(round_done, 1))
                    for T in range(NT):
                        ins = turn(ps[:, 6, T * P:(T + 1) * P], pick[:, T, :].bitcast(F32))
                    ins.then_inc(pick_turned, 1)
                ffn(1, U["ffn1"], B["ffn1"], NFB, G, M, lambda T, half: 4 + half, turn_pick, lambda: gather(1))
                pe.wait_ge(y_low, g.at(y_low, 1))
                pe.wait_ge(gather_low, g.at(gather_low, 2))
                for T in range(NT):
                    for half in range(2):
                        o = ps[:, (6 if T == 0 else 4) + half, :]
                        c = slice(half * NB, (half + 1) * NB)
                        mm(o, pickT[:, T, :], yh[:, c], start=True, stop=False)
                        ins = mm(o, pickT[:, T, :], yl[:, c], start=False, stop=True)
                ins.then_inc(scatter_done, 1)
            g.r = rounds
            g.post = True
            ple(1)


NSA_ORDER = [("a", 0), ("z", 0), ("a", 1), ("z", 1), ("a", 2), ("z", 2), ("a", 3), ("z", 3), ("a", 4), ("a", 5),
             ("z", 4), ("a", 6), ("z", 5), ("a", 7), ("a", 8), ("a", 9), ("z", 6), ("z", 7), ("a", 10), ("a", 11),
             ("a", 12), ("z", 8), ("a", 13), ("z", 9), ("a", 14), ("a", 15), ("z", 10), ("a", 16), ("a", 17),
             ("z", 11)]


def square_constants():
    i = np.arange(P)
    r, c = i[:, None], i[None, :]
    parts = [r == c, -1.0 * (r >= c), -np.ones((P, P)), np.where(r >= c, -1e30, 0.0), r < c, r < c,
             np.ones((P, P)), np.broadcast_to(c, (P, P))]
    e = np.arange(NE)
    tril = np.broadcast_to((e[None, :] < e[:, None]).reshape(1, 64), (P, 64))
    diag = (r // NC_ == e[None, :]) & (r < 8 * NC_)
    return np.concatenate([np.asarray(x, np.float32) for x in parts + [tril, diag]], axis=1)


def onehot_constants():
    d = np.concatenate([np.arange(512) - 256, 255 - np.arange(LREV)])
    n = np.maximum(d, 0)
    ex = NBUCK // 2
    big = ex + (np.log(np.maximum(n, 1).astype(np.float32) / ex) / np.log(MAXD / ex) * (NBUCK - ex)).astype(np.int32)
    bucket = np.where(n < ex, n, np.minimum(big, NBUCK - 1))
    out = np.zeros((NBUCK + 1, d.size), np.float32)
    out[bucket, np.arange(d.size)] = np.where(d >= 0, 1.0 / SC, 0.0)
    out[NBUCK] = np.where(d >= 0, 0.0, MASKED)
    return out


_INS = ["x", "pre_norm_gain", "post_norm_gain", "rel_bias_table", "nsa_w_in", "nsa_w_out", "nsa_cmp_k_pos",
        "nsa_cmp_k_w1", "nsa_cmp_k_w2", "nsa_cmp_v_pos", "nsa_cmp_v_w1", "nsa_cmp_v_w2", "p_2", "mix_norm_g_2",
        "w_in_2", "q_norm_g_2", "k_norm_g_2", "conv_w_2", "conv_b_2", "attn_out_g_2", "conv_out_g_2", "w_o_2",
        "ffn_norm_g_2", "dense_w1_2", "dense_w3_2", "dense_w2_2", "router_w_2", "moe_w1_2", "moe_w3_2",
        "moe_w2_2", "ple_norm_g_2", "ple_gate_w_2", "ple_proj_w_2"]


def kernel(**inputs):
    import concourse.bacc as _bacc
    from concourse.bass_utils import run_bass_kernel_spmd as _run

    nc = _bacc.Bacc("TRN2", target_bir_lowering=False, num_devices=1)
    arrays, t = {}, {}
    given = {name: np.ascontiguousarray(inputs[name]) for name in _INS}
    given["c_square"] = square_constants()
    given["c_onehot"] = onehot_constants()
    for name, a in given.items():
        arrays[f"in_{name}_dram"] = a
        t[name] = nc.dram_tensor(f"in_{name}_dram", a.shape, mybir.dt.from_np(a.dtype), kind="ExternalInput").ap()
    out = nc.dram_tensor("out_0_dram", (1, S, D), F32, kind="ExternalOutput").ap()
    build(nc, t, out)
    r = _run(nc, [arrays], core_ids=[0])
    return r.results[0]["out_0_dram"]
```

```python
from contextlib import ExitStack

import numpy as np

import concourse.bass as bass
from concourse import mybir

F32 = mybir.dt.float32
F32R = mybir.dt.float32r
I32 = mybir.dt.int32
ALU = mybir.AluOpType
ACT = mybir.ActivationFunctionType
AX = mybir.AxisListType.X

P = 128
S = 256
NT = S // P
D = 1024
KD = D // P
NB = 512
KU = 4

NH, DH, NG = 16, 64, 4
RG = NH // NG
KV0, G0, Z0 = NH * DH, NH * DH + 6 * NG * DH, NH * DH + 6 * NG * DH + 3 * NH
CB, CS = 32, 16
NC_ = (S - CB) // CS + 1
HC = 256
NBUCK, MAXD = 32, 128
SC = DH ** -0.5
MASKED = -1e30 / SC
LREV = 384

SH = 8
FF = 3584
NFB = FF // NB
NE = 8
EPS = 1e-6

RAW = 6
SPL = 3
AHEAD = SPL - 1
UNITS_ROUND = 2 * NFB * 2 + FF // (KU * P) * 2
BLOCKS_ROUND = 2 * NFB


def weight_units(w):
    def block(m, c0, n=NB, kt=KD):
        return [(m, k, min(KU, kt - k), c0, n) for k in range(0, kt, KU)]

    def ffn(w1, w3, w2):
        out = []
        for b in range(NFB):
            out += block(w1, b * NB) + block(w3, b * NB)
        for k in range(0, FF // P, KU):
            out += [(w2, k, KU, 0, NB), (w2, k, KU, NB, NB)]
        return out

    nsa = block(w["nsa_in"], KV0)
    nsa += block(w["nsa_in"], 0) + block(w["nsa_in"], NB)
    nsa += block(w["nsa_in"], KV0 + NB) + block(w["nsa_in"], KV0 + 2 * NB)
    nsa += [(w["nsa_in"], 0, KD, G0, 3 * NH)]
    nsa += [(w["cmp_k1"], 0, 8, 0, HC), (w["cmp_k1"], 8, 8, 0, HC)]
    nsa += [(w["cmp_v1"], 0, 8, 0, HC), (w["cmp_v1"], 8, 8, 0, HC)]
    for b in range(6):
        nsa += block(w["nsa_in"], Z0 + b * NB)
    nsa += block(w["nsa_out"], 0) + block(w["nsa_out"], NB)

    def mix(i):
        out = []
        for b in range(6):
            out += block(w[f"in{i}"], b * NB)
        return out + [(w[f"o{i}"], k, KU, c, NB) for k in (KU, 0) for c in (0, NB)]

    def ple(i):
        return (block(w[f"pg{i}"], 0) + block(w[f"pg{i}"], NB)
                + block(w[f"pp{i}"], 0, kt=2) + block(w[f"pp{i}"], NB, kt=2))

    before = nsa + mix(0) + ffn(w["d1"], w["d3"], w["d2"]) + ple(0) + mix(1)
    return before, ffn(w["m1"], w["m3"], w["m2"]), ple(1)


def first_unit_of():
    at, out = 0, {}
    for name, n in (("kv_c", 2), ("q", 4), ("kv_s", 2), ("kv_w", 2), ("gate", 1), ("cmp", 4), ("z", 12),
                    ("nsa_out", 4), ("in0", 12), ("o0", 4), ("ffn0", UNITS_ROUND), ("ple0", 6), ("in1", 12),
                    ("o1", 4), ("ffn1", UNITS_ROUND)):
        out[name] = at
        at += n
    out["ple1"] = out["ffn1"]
    return out


def build(nc, t, out):
    U = first_unit_of()
    B = {}
    nblk = 0
    for name, n in (("kv_c", 1), ("q", 2), ("kv_s", 1), ("kv_w", 1), ("gate", 1), ("cmp", 2), ("z", 6),
                    ("nsa_out", 2), ("in0", 6), ("o0", 4), ("ffn0", BLOCKS_ROUND), ("ple0", 4),
                    ("in1", 6), ("o1", 4), ("ffn1", BLOCKS_ROUND)):
        B[name] = nblk
        nblk += n
    z_blocks = range(B["z"], B["z"] + 6)
    B["ple1"] = B["ffn1"]
    block_end = {}
    for name, n, units in (("kv_c", 1, 2), ("q", 2, 2), ("kv_s", 1, 2), ("kv_w", 1, 2), ("gate", 1, 1),
                           ("cmp", 2, 2), ("z", 6, 2), ("nsa_out", 2, 2), ("in0", 6, 2), ("o0", 4, 1),
                           ("ffn0", BLOCKS_ROUND, 2), ("in1", 6, 2), ("o1", 4, 1), ("ffn1", BLOCKS_ROUND, 2)):
        for j in range(n):
            block_end[B[name] + j] = U[name] + (j + 1) * units
    ple_end = [2, 4, 5, 6]
    for j in range(4):
        block_end[B["ple0"] + j] = U["ple0"] + ple_end[j]

    weights = {
        "nsa_in": t["nsa_w_in"][0], "nsa_out": t["nsa_w_out"][0],
        "cmp_k1": t["nsa_cmp_k_w1"][0], "cmp_v1": t["nsa_cmp_v_w1"][0],
        "d1": t["dense_w1_2"][0], "d3": t["dense_w3_2"][0], "d2": t["dense_w2_2"][0],
        "m1": t["moe_w1_2"][0], "m3": t["moe_w3_2"][0], "m2": t["moe_w2_2"][0],
    }
    for i in range(2):
        weights |= {f"in{i}": t["w_in_2"][i], f"o{i}": t["w_o_2"][i],
                    f"pg{i}": t["ple_gate_w_2"][i], f"pp{i}": t["ple_proj_w_2"][i]}
    before, per_round, after = weight_units(weights)
    assert len(before) == U["ffn1"] and len(per_round) == UNITS_ROUND

    with ExitStack() as ctx:
        def sb(name, shape, dt=F32, scope=ctx):
            return scope.enter_context(nc.sbuf_tensor(name, shape, dt))

        raw = sb("raw", [P, RAW, KU * NB])
        whi = sb("whi", [P, SPL, KU * NB], F32R)
        wlo = sb("wlo", [P, SPL, KU * NB], F32R)
        h = sb("h", [P, NT, D])
        tok = sb("tok", [P, NT, D])
        xh = sb("xh", [P, KD, S], F32R)
        xl = sb("xl", [P, KD, S], F32R)
        con = sb("con", [P, 8 * P + 64 + 8])
        ident, ntri, nones, negm, keep, stri, ones, iota = (con[:, i * P:(i + 1) * P] for i in range(8))
        tril8 = con[:, 8 * P:8 * P + 64]
        bdiag = con[:, 8 * P + 64:8 * P + 72]
        gains = sb("gains", [P, 7, KD])
        ogain = sb("ogain", [P, 2, KD])
        qkg = sb("qkg", [P, 2, 2])
        convw = sb("convw", [P, 2, 4, 4])
        rw = sb("rw", [P, KD, NE])
        rws = sb("rws", [P, KD, 2, NE], F32R)
        st = sb("st", [P, 64])
        epst = sb("epst", [P, 1])
        nround = sb("nround", [1, 1], I32)

        with ExitStack() as nsa:
            tabx = sb("tabx", [NBUCK + 1, NH], scope=nsa)
            with ExitStack() as a:
                kc2 = sb("kc2", [P, NT, 2 * NG, 2, DH], scope=a)
                XW = 2 * (CB // 2) * NG * NC_
                XT = XW + P - NG * NC_
                xw = sb("xw", [P, XT], scope=a)
            bias = sb("bias", [P, NH, S], scope=nsa)
            cbias = sb("cbias", [P, NT, NH, NC_], scope=nsa)
            qT = sb("qT", [P, NH // 2, S], scope=nsa)
            kT = sb("kT", [P, 2, NG, S], scope=nsa)
            vs = sb("vs", [P, 2, NT, NG * DH], scope=nsa)
            pos2 = sb("pos2", [P, 2, CB // 2], scope=nsa)
            w2k = sb("w2k", [P, 2, 2, DH], scope=nsa)
            w2v = sb("w2v", [P, 2, DH], scope=nsa)
            kcT = sb("kcT", [P, NG * NC_], scope=nsa)
            gate = sb("gate", [P, NT, 3 * NH], scope=nsa)
            cst = sb("cst", [P, 3, NT * NH], scope=nsa)
            grow = sb("grow", [P, NT, NH], scope=nsa)
            ast_ = sb("ast", [P, 16, 3, RG], scope=nsa)
            with ExitStack() as early:
                with ExitStack() as a:
                    oh = sb("oh", [NBUCK + 1, 512 + LREV], scope=a)
                    revb = sb("revb", [NH, LREV], scope=a)
                    kd = sb("kd", [P, 2, NT, NG, 2, DH], scope=a)
                    xwh = sb("xwh", [P, XT], F32R, scope=a)
                    xwl = sb("xwl", [P, XT], F32R, scope=a)
                with ExitStack() as a:
                    hc = sb("hc", [NG * NC_, 2, HC], scope=a)
                    hcT = sb("hcT", [P, 2, 2, NG * NC_], scope=a)
                    hcR = sb("hcR", [P, 2, 2, 8 * NC_], scope=a)
                    vcb = sb("vcb", [8 * NC_, 2, 8, DH], scope=a)
                    lcT = sb("lcT", [8 * NC_, 2 * NT, P], scope=a)
                    lc = sb("lc", [P, NT, NH, NC_], scope=a)
            y = tok
            with ExitStack() as late:
                ob = sb("ob", [P, NT, D], scope=late)
                sg = sb("sg", [P, 2, RG, S], scope=late)
                pT = sb("pT", [P, 2, RG, NT, P], scope=late)
                zt = sb("zt", [P, NT, NB], scope=late)
                postg = sb("postg", [P, D], scope=late)

        with ExitStack() as mx:
            qk = sb("qk", [P, 2, NT, NB], scope=mx)
            sq = sb("sq", [P, NT, NB], scope=mx)
            qk_ss = sb("qk_ss", [P, 2, NT, SH], scope=mx)
            v2 = sb("v2", [P, NT, NB], scope=mx)
            qkT = sb("qkT", [P, 2, 4, S], scope=mx)
            uT = sb("uT", [P, 4, S], scope=mx)
            cu = sb("cu", [P, 4, S + 2], scope=mx)
            cv = sb("cv", [P, 4, S], scope=mx)
            mixT = sb("mixT", [P, 8, S], scope=mx)
            mixs = sb("mixs", [P, 8, S], scope=mx)
            factor_diag, factor_cols, factor_squares = (mixs[:, j, :] for j in range(3))
            spa = sb("spa", [P, 4, 3 * P], scope=mx)
            spb = sb("spb", [P, 4, 3 * P], scope=mx)
            wT = sb("wT", [P, 4, 3 * P], scope=mx)

        with ExitStack() as ff:
            gt = sb("gt", [P, NT, NB], scope=ff)
            ht = sb("ht", [P, NT, NB], scope=ff)
            pt_in = sb("pt_in", [P, NT, 2 * P], scope=ff)
            with ExitStack() as a:
                hTh = sb("hTh", [P, FF // P, S], F32R, scope=a)
                hTl = sb("hTl", [P, FF // P, S], F32R, scope=a)
            with ExitStack() as a:
                mTh = sb("mTh", [P, FF // P, P], F32R, scope=a)
                mTl = sb("mTl", [P, FF // P, P], F32R, scope=a)
                xnh = sb("xnh", [P, NT, D], F32R, scope=a)
                xnl = sb("xnl", [P, NT, D], F32R, scope=a)
                xgh = sb("xgh", [P, KD, P], F32R, scope=a)
                xgl = sb("xgl", [P, KD, P], F32R, scope=a)
                yh = sb("yh", [P, D], F32R, scope=a)
                yl = sb("yl", [P, D], F32R, scope=a)
                pick = sb("pick", [P, NT, P], F32R, scope=a)
                pickT = sb("pickT", [P, NT, P], F32R, scope=a)
                lg = sb("lg", [P, NT, NE], scope=a)
                cmpa = sb("cmpa", [P, NT, NE, NE], scope=a)
                cmpb = sb("cmpb", [P, NT, NE, NE], scope=a)
                sel = sb("sel", [P, NT, NE], scope=a)
                gw = sb("gw", [P, NT, NE], scope=a)
                slot = sb("slot", [P, NT, 2 * NE + 1], scope=a)
                cnt = sb("cnt", [P, NE + 4], scope=a)
            with ExitStack() as a:
                ptTh = sb("ptTh", [P, 2, S], F32R, scope=a)
                ptTl = sb("ptTl", [P, 2, S], F32R, scope=a)
                pg = sb("pg", [P, 2, NT, NB], scope=a)
                pm = sb("pm", [P, NT, NB], scope=a)

        ps = ctx.enter_context(nc.psum_tensor("ps", [P, 8, NB], F32))
        bias_dram = nc.dram_tensor("bias_scratch", [NH, P, LREV], F32, kind="Internal").ap()

        per = {}

        def sem(name, each_round=0):
            per[name] = each_round
            return ctx.enter_context(nc.semaphore(name))

        unit_loaded = [sem(f"unit_loaded{s}", 16 * UNITS_ROUND // RAW) for s in range(RAW)]
        high_done, low_done, half_used = (sem(n, 2 * UNITS_ROUND) for n in ("high_done", "low_done", "half_used"))
        banks_free = [sem(f"banks_free{i}", BLOCKS_ROUND // 2) for i in range(2)]
        hidden_turned, hidden_high, hidden_low = (
            sem(n, NFB) for n in ("hidden_turned", "hidden_high", "hidden_low"))
        act_step, dve_step = sem("act_step"), sem("dve_step")
        gate_made = sem("gate_made")
        hidden_made = sem("hidden_made")
        pick_done = sem("pick_done", 1)
        pick_turned = sem("pick_turned", 1)
        pick_copied = sem("pick_copied", 1)
        gathered = sem("gathered", 1)
        gather_high = sem("gather_high", 1)
        gather_low = sem("gather_low", 1)
        y_high = sem("y_high", 2)
        y_low = sem("y_low", 2)
        scatter_done = sem("scatter_done", 2)
        round_done = sem("round_done", 1)
        rounds_known = sem("rounds_known")
        h_half = sem("h_half")
        stored = sem("stored")
        h_turned = sem("h_turned")
        gains_loaded = sem("gains_loaded")
        tab_product = sem("tab_product")
        x_loaded = sem("x_loaded")
        eps_set = sem("eps_set")
        windows_done = sem("windows_done")
        q_turned = sem("q_turned")
        k_turned = sem("k_turned")
        cmp_logits = sem("cmp_logits")
        logits_done = sem("logits_done")
        z_used = sem("z_used")
        y_turned = sem("y_turned")
        qk_squares = sem("qk_squares")
        z_scores = sem("z_scores")
        sp_done = sem("sp_done")
        stick_done = sem("stick_done")
        pv_done = sem("pv_done")
        mix_sums = sem("mix_sums")
        conv_sums_copied = sem("conv_sums_copied")
        conv_high = sem("conv_high")
        conv_low = sem("conv_low")
        pv_copied = sem("pv_copied")
        p_turned = sem("p_turned")
        router_loaded = sem("router_loaded")
        logit_shift = sem("logit_shift")
        root_done = sem("root_done")
        factor_done = sem("factor_done")
        h_ready = sem("h_ready")
        first_gain_loaded = sem("first_gain_loaded")
        factor_diag_done = sem("factor_diag_done")
        factor_spread = sem("factor_spread")
        factor_copied = sem("factor_copied")
        xh_done = sem("xh_done")
        cbias_done = sem("cbias_done")
        kc_turned = sem("kc_turned")
        cmp_loaded = sem("cmp_loaded")
        window_high = sem("window_high")
        hc_turned = sem("hc_turned")
        rev_stored = sem("rev_stored")
        kcvc_product = sem("kcvc_product")
        cmp_scores = sem("cmp_scores")
        cmp_exp = sem("cmp_exp")
        lc_turned = sem("lc_turned")
        cmp_out = sem("cmp_out")
        o_evac = sem("o_evac")
        bias_loaded = sem("bias_loaded")
        scores_done = sem("scores_done")
        p_turned_all = sem("p_turned_all")
        pv_step = sem("pv_step")
        exp_done = sem("exp_done")
        z_done = sem("z_done")
        yh_done = sem("yh_done")
        post_squares = sem("post_squares")
        post_summed = sem("post_summed")
        post_root = sem("post_root")
        postg_loaded = sem("postg_loaded")
        qk_root = sem("qk_root")
        qk_turned = sem("qk_turned")
        mix_loaded = sem("mix_loaded")
        ln_done = sem("ln_done")
        mix_root = sem("mix_root")
        mixh_done = sem("mixh_done")
        ph_done = sem("ph_done")
        router_high = sem("router_high")
        xn_high = sem("xn_high")
        router_logits = sem("router_logits")
        sel_done = sem("sel_done")
        gate_exp = sem("gate_exp")
        slots_counted = sem("slots_counted")
        h_normed = sem("h_normed")
        con_loaded = sem("con_loaded")
        ident_loaded = sem("ident_loaded")
        oh_loaded = sem("oh_loaded")
        table_one = sem("table_one")
        rev_ready = sem("rev_ready")
        xl_done = sem("xl_done")
        qT_done = sem("qT_done")
        window_low = sem("window_low")
        kT_done = sem("kT_done")
        hcT_done = sem("hcT_done")
        kcT_done = sem("kcT_done")
        lcT_done = sem("lcT_done")
        vcb_done = sem("vcb_done")
        pT_done = sem("pT_done")
        yl_done = sem("yl_done")
        qk_normed = sem("qk_normed")
        stick_exp = sem("stick_exp")
        qkT_done = sem("qkT_done")
        mix_squares = sem("mix_squares")
        mixl_done = sem("mixl_done")
        p_loaded = sem("p_loaded")
        pl_done = sem("pl_done")
        router_low = sem("router_low")
        xn_low = sem("xn_low")

        class Prog:

            def __init__(self):
                self.r, self.n, self.split, self.post = None, 0, 0, False

            def at(self, semaphore, n):
                k = per[semaphore.name]
                return n if self.r is None or not k else self.r * k + n

            def through(self, b):
                end = block_end[b] if not (self.post and b >= B["ple1"]) else U["ple1"] + ple_end[b - B["ple1"]]
                return self.at(half_used, 2 * end)

            def freed(self, b):
                count = len([x for x in range(b % 2, b + 1, 2) if x not in z_blocks])
                return self.at(banks_free[b % 2], count)

        def pair(b):
            return 2 * (b % 2)

        dense_diag, dense_cols = tok[:, 0, 0:S], tok[:, 0, S:2 * S]

        def turned_place(k, j):
            if k == 3:
                bank = 4 + j // KU + 2 * (j % KU // 2)
            else:
                bank = 4 + j // 2
            return ps[:, bank, (j % 2) * S:(j % 2 + 1) * S]

        def pv_place(j):
            return ps[:, 4 + 2 * j:6 + 2 * j, 3 * P:4 * P]

        def mix_tile(j):
            return (j + KU) % KD

        def factor(T):
            return st[:, 8 + T:9 + T]

        def unit_columns(v, post):
            if (v >= U["ffn1"]) != post:
                return KU * NB if v >= U["o1"] else before[v][2] * before[v][4]
            _, _, nk, _, n = after[v - U["ffn1"]] if post else before[v]
            return nk * n

        ld = nc.allow_non_contiguous_dma("small gains and constants")
        ctx.enter_context(ld)
        block_ = ctx.enter_context(nc.Block())

        @block_.sync
        def _(sp):
            g = Prog()
            sp.dma_start(ident, t["c_square"][:, 0:P]).then_inc(ident_loaded, 16)
            sp.dma_start(gains[:, 0, :], t["pre_norm_gain"][0].rearrange("(k p) -> p k", p=P))\
                .then_inc(first_gain_loaded, 16)
            sp.dma_start(h[:], t["x"][0].rearrange("(t p) d -> p t d", p=P)).then_inc(x_loaded, 16)

            def load(u, unit, e=None):
                m, k0, nk, c0, n = unit
                s = u % RAW
                if u >= RAW:
                    sp.wait_ge(low_done, g.at(low_done, 2 * (u - RAW + 1)))
                if e is None:
                    src = m[k0 * P:(k0 + nk) * P, c0:c0 + n].rearrange("(k p) n -> p k n", p=P)
                else:
                    src = m[bass.ds(e, 1), k0 * P:(k0 + nk) * P, c0:c0 + n].rearrange("a (k p) n -> p (a k) n", p=P)
                sp.dma_start(raw[:, s, 0:nk * n].rearrange("p (k n) -> p k n", k=nk), src)\
                    .then_inc(unit_loaded[s], 16)

            for u, unit in enumerate(before):
                load(u, unit)
            with sp.Fori(0, NE) as r:
                g.r = r
                for j, unit in enumerate(per_round):
                    load(U["ffn1"] + j, unit, r)
            g.r = None
            sp.wait_ge(rounds_known, 1)
            rounds = sp.value_load(nround[0:1, 0:1], min_val=NE, max_val=2 * NE)
            with sp.If(rounds > NE):
                with sp.Fori(NE, 2 * NE) as r:
                    g.r = r
                    for j, unit in enumerate(per_round):
                        load(U["ffn1"] + j, unit, r - NE)
            g.r = rounds
            for j, unit in enumerate(after):
                load(U["ple1"] + j, unit)
            for j in range(2):
                sp.wait_ge(h_half, 3 + j)
                c = slice(j * NB, (j + 1) * NB)
                sp.dma_start(out[0][:, c].rearrange("(t p) d -> p t d", p=P), h[:, :, c])\
                    .then_inc(stored, 16)
            sp.wait_ge(stored, 32)

        @block_.gpsimd
        def _(pool):
            def small(semaphore, dst, src):
                pool.dma_start(dst, src).then_inc(semaphore, 16)

            pool.memset(epst[:], EPS).then_inc(eps_set, 1)
            small(oh_loaded, oh[:], t["c_onehot"])
            pool.wait_ge(eps_set, 1)
            small(oh_loaded, tabx[0:NBUCK, :], t["rel_bias_table"])
            pool.memset(tabx[NBUCK:NBUCK + 1, :], 1.0).then_inc(table_one, 1)
            small(con_loaded, con[:, P:], t["c_square"][:, P:])
            for i in range(2):
                for j, n in ((1, "mix_norm_g_2"), (2, "ffn_norm_g_2"), (3, "ple_norm_g_2")):
                    small(gains_loaded, gains[:, 3 * i + j, :], t[n][i].rearrange("(k p) -> p k", p=P))
            for kv, n in ((0, "nsa_cmp_k_pos"), (1, "nsa_cmp_v_pos")):
                small(cmp_loaded, pos2[:, kv, :], t[n][0].rearrange("(m s) d -> (s d) m", s=2))
            for s in range(2):
                small(cmp_loaded, w2k[:, :, s, :], t["nsa_cmp_k_w2"][0].rearrange("(j p) d -> p j d", p=P))
            small(cmp_loaded, w2v[:], t["nsa_cmp_v_w2"][0].rearrange("(j p) d -> p j d", p=P))
            for i in range(2):
                for j, n in ((0, "attn_out_g_2"), (4, "conv_out_g_2")):
                    small(mix_loaded, ogain[:, i, j:j + 4], t[n][i].rearrange("(k p) -> p k", p=P))
                for j, n in ((0, "q_norm_g_2"), (1, "k_norm_g_2")):
                    for s in range(2):
                        small(mix_loaded, qkg[s * DH:(s + 1) * DH, i, j:j + 1],
                              t[n][i:i + 1].rearrange("a d -> d a"))
                for j in range(3):
                    small(mix_loaded, convw[:, i, :, j], t["conv_w_2"][i, j].rearrange("(k p) -> p k", p=P))
                small(mix_loaded, convw[:, i, :, 3], t["conv_b_2"][i].rearrange("(k p) -> p k", p=P))
            small(router_loaded, rw[:], t["router_w_2"][0].rearrange("(k p) e -> p k e", p=P))
            pool.wait_ge(rev_ready, 1)
            pool.dma_start(bias_dram, revb[:].unsqueeze(1).broadcast_to([NH, P, LREV])).then_inc(rev_stored, 16)
            pool.wait_ge(rev_stored, 16)
            pool.wait_ge(window_low, 1)
            pool.dma_start(bias[:], bass.AP(tensor=bias_dram.tensor, offset=P - 1,
                                            ap=[[LREV - 1, P], [P * LREV, NH], [1, S]])).then_inc(bias_loaded, 16)
            pool.wait_ge(o_evac, 1)
            small(postg_loaded, postg[:], t["post_norm_gain"][0:1].broadcast_to([P, D]))
            for i in range(2):
                pool.wait_ge(mixl_done, 2 * i + 2)
                small(p_loaded, pt_in[:], t["p_2"][i, 0].rearrange("(t p) d -> p t d", p=P))

        @block_.scalar
        def _(act):
            g = Prog()

            def step(ins):
                g.n += 1
                ins.then_inc(act_step, 1)
                act.wait_ge(act_step, g.n)

            AC = nc.scalar.activation

            def split_to(u):
                while g.split <= u:
                    v = g.split
                    n = unit_columns(v, g.post)
                    act.wait_ge(unit_loaded[v % RAW], g.at(unit_loaded[v % RAW], 16 * (v // RAW + 1)))
                    for half in range(2):
                        if v >= SPL:
                            last = half if unit_columns(v - SPL, g.post) == n else 1
                            act.wait_ge(half_used, g.at(half_used, 2 * (v - SPL) + last + 1))
                        c = slice(half * n // 2, (half + 1) * n // 2)
                        AC(whi[:, v % SPL, c], raw[:, v % RAW, c], ACT.Copy).then_inc(high_done, 1)
                    g.split += 1

            def root(k):
                for i in range(NT):
                    ins = AC(tok[:, i, :], h[:, i, :], ACT.Square, accum_out=st[:, i:i + 1])
                step(ins)
                AC(st[:, 2:4], st[:, 0:2], ACT.Sqrt, scale=1.0 / D, bias=epst[:, 0:1])\
                    .then_inc(root_done, 1)

            def turned_high(k, half):
                act.wait_ge(h_turned, 2 * k + half + 1)
                for j in range(half * KU, (half + 1) * KU):
                    ins = AC(xh[:, j, :], turned_place(k, j), ACT.Copy, scale=gains[:, k, j:j + 1])
                ins.then_inc(xh_done, 1)

            def start(k, u):
                split_to(u)
                turned_high(k, 0)
                split_to(u + 1)
                turned_high(k, 1)
                root(k)

            def both(b):
                return ps[:, pair(b):pair(b) + 2, :]

            def flat(x):
                return x.rearrange("p a n -> p (a n)")

            def evac(b, dst, src=None, func=ACT.Copy):
                act.wait_ge(half_used, g.through(b))
                AC(dst, both(b) if src is None else src, func).then_inc(banks_free[b % 2], 1)

            def evac_scaled(b, k, dst, n=NB, func=ACT.Copy):
                act.wait_ge(half_used, g.through(b))
                act.wait_ge(factor_done, k + 1)
                for T in range(NT):
                    ins = AC(dst[:, T], ps[:, pair(b) + T, 0:n], func, scale=factor(T))
                ins.then_inc(banks_free[b % 2], 1)

            act.wait_ge(first_gain_loaded, 16)
            act.wait_ge(x_loaded, 16)
            act.wait_ge(eps_set, 1)
            turned_high(0, 0)
            turned_high(0, 1)
            split_to(1)
            root(0)
            split_to(U["q"])
            act.wait_ge(tab_product, 1)
            AC(revb[:], ps[0:NH, 4, 0:LREV], ACT.Copy).then_inc(rev_ready, 1)
            split_to(U["q"] + 1)
            b = B["kv_c"]
            act.wait_ge(half_used, g.through(b))
            act.wait_ge(factor_done, 1)
            for T in range(NT):
                for s in range(2):
                    ins = AC(kc2[:, T, :, s, :], ps[:, pair(b) + T, :].rearrange("p (g d) -> p g d", d=DH), ACT.Copy,
                             scale=factor(T))
            ins.then_inc(banks_free[b % 2], 1)
            for i in range(2):
                split_to(U["q"] + 2 * i + 3)
                evac_scaled(B["q"] + i, 0, tok[:, :, i * NB:(i + 1) * NB])
            act.wait_ge(windows_done, 1)
            AC(xwh[:], xw[:], ACT.Copy).then_inc(window_high, 1)
            for i in range(2):
                split_to(U["kv_s"] + 2 * i + 3)
                b = B["kv_s"] + i
                act.wait_ge(half_used, g.through(b))
                for T in range(NT):
                    for s in range(2):
                        AC(kd[:, i, T, :, s, :], ps[:, pair(b) + T, 0:NG * DH].rearrange("p (g d) -> p g d", d=DH),
                           ACT.Copy, scale=factor(T))
                    ins = AC(vs[:, i, T, :], ps[:, pair(b) + T, NG * DH:NB], ACT.Copy, scale=factor(T))
                ins.then_inc(banks_free[b % 2], 1)
                if i == 0:
                    act.wait_ge(q_turned, 1)
                    AC(flat(qT[:]), flat(ps[:, 4:8, :]), ACT.Copy).then_inc(qT_done, 1)
            split_to(U["gate"] + 2)
            b = B["gate"]
            evac_scaled(b, 0, gate, 3 * NH, ACT.Sigmoid)
            act.wait_ge(k_turned, 1)
            AC(kT[:].rearrange("p a g n -> p (a g n)"), flat(ps[:, 4:8, :]), ACT.Copy).then_inc(kT_done, 1)
            for kv in range(2):
                split_to(U["cmp"] + 2 * kv + 3)
                b = B["cmp"] + kv
                evac(b, hc[:, kv, :], ps[0:NG * NC_, pair(b), 0:HC], ACT.Silu)
            split_to(U["z"] + 2)
            act.wait_ge(cmp_logits, 1)
            AC(lc[:], lc[:], ACT.Exp, scale=SC).then_inc(cmp_exp, 1)
            split_to(U["z"] + 3)

            def z_silu(n):
                b = B["z"] + n
                act.wait_ge(half_used, g.through(b))
                if n:
                    act.wait_ge(z_used, n)
                for T in range(NT):
                    ins = AC(zt[:, T, :], ps[:, T, :], ACT.Silu, scale=factor(T))
                ins.then_inc(z_done, 1)

            z_silu(0)
            split_to(U["z"] + 5)
            z_silu(1)

            def att(i):
                if i >= 16:
                    return
                T = (i // 2) % 2
                nk = (T + 1) * P
                act.wait_ge(logits_done, i + 1)
                for r in range(RG):
                    ins = AC(sg[:, i % 2, r, 0:nk], sg[:, i % 2, r, 0:nk], ACT.Exp, scale=SC,
                             bias=ast_[:, i, 1, r:r + 1], accum_out=ast_[:, i, 2, r:r + 1])
                ins.then_inc(exp_done, 1)

            for kind, i in NSA_ORDER:
                if kind == "a":
                    att(i)
                elif kind == "s":
                    z_silu(i)
                elif kind == "z" and i % 2 == 0:
                    split_to(U["z"] + i // 2 + AHEAD)
            for half in range(2):
                act.wait_ge(y_turned, half + 1)
                AC(flat(xh[:, half * KU:(half + 1) * KU]), flat(ps[:, 4 + 2 * half:6 + 2 * half, :]), ACT.Copy)\
                    .then_inc(yh_done, 1)
            split_to(U["nsa_out"] + 3)
            for i in range(2):
                b = B["nsa_out"] + i
                c = slice(i * NB, (i + 1) * NB)
                split_to(U["in0"] + i)
                if i:
                    AC(st[:, 22:23], epst[:, 0:1], ACT.Sqrt)
                evac(b, tok[:, :, c])
                act.wait_ge(banks_free[b % 2], g.freed(b))
                for T in range(NT):
                    o = (18 if i else 4) + T
                    ins = AC(zt[:, T, :], tok[:, T, c], ACT.Square, accum_out=st[:, o:o + 1])
                ins.then_inc(post_squares, 1)
            act.wait_ge(post_summed, 1)
            AC(st[:, 6:8], st[:, 4:6], ACT.Sqrt, scale=1.0 / D, bias=epst[:, 0:1]).then_inc(post_root, 1)

            def dense():
                ub, bb = U["ffn0"], B["ffn0"]
                for f in range(NFB):
                    split_to(ub + 4 * f + 1 + AHEAD)
                    if f == 0:
                        act.wait_ge(factor_spread, 2)
                        AC(dense_cols, ps[:, 4, 0:S], ACT.Copy).then_inc(factor_copied, 1)
                    b = bb + 2 * f
                    act.wait_ge(banks_free[b % 2], g.freed(b))
                    AC(gt[:], gt[:], ACT.Silu).then_inc(gate_made, 1)
                    split_to(ub + 4 * f + 3 + AHEAD)
                    act.wait_ge(hidden_made, f + 1)
                    AC(flat(hTh[:, f * KU:(f + 1) * KU, :]), flat(ht[:]), ACT.Copy).then_inc(hidden_high, 1)
                split_to(ub + UNITS_ROUND - 1)

            def expert(first_extra, last_extra):
                ub, bb, fb = U["ffn1"], B["ffn1"], NFB

                def turn(f):
                    act.wait_ge(hidden_turned, g.at(hidden_turned, f + 1))
                    AC(mTh[:, f * KU:(f + 1) * KU, :], ps[:, 6 + f % 2, :].rearrange("p (k n) -> p k n", k=KU),
                       ACT.Copy).then_inc(hidden_high, 1)

                for f in range(NFB):
                    b = bb + 2 * f
                    split_to(ub + 4 * f + 1 + AHEAD)
                    act.wait_ge(half_used, g.through(b))
                    act.wait_ge(banks_free[(b - 1) % 2], g.freed(b - 1))
                    AC(gt[:, 0, :], ps[:, pair(b), :], ACT.Silu).then_inc(banks_free[b % 2], 1)
                    if f:
                        turn(f - 1)
                    else:
                        first_extra()
                    split_to(ub + 4 * f + 3 + AHEAD)
                split_to(ub + 4 * NFB + 1 + AHEAD)
                turn(NFB - 1)
                split_to(ub + 4 * NFB + 5 + AHEAD)
                last_extra()
                split_to(ub + UNITS_ROUND - 1 + AHEAD)

            def mix(i):
                start(3 * i + 1, U[f"in{i}"])
                ib, iu = B[f"in{i}"], U[f"in{i}"]
                for j in range(2):
                    split_to(iu + 2 * j + 1 + AHEAD)
                    evac_scaled(ib + j, 3 * i + 1, qk[:, j])
                    if j == 0:
                        act.wait_ge(factor_spread, 2 * i + 1)
                        AC(factor_cols, ps[:, 4, 0:S], ACT.Copy).then_inc(factor_copied, 1)
                    act.wait_ge(qk_squares, 2 * i + j + 1)
                    AC(qk_ss[:, j], qk_ss[:, j], ACT.Sqrt, scale=1.0 / DH, bias=epst[:, 0:1])\
                        .then_inc(qk_root, 1)
                split_to(iu + 5 + AHEAD)
                evac_scaled(ib + 2, 3 * i + 1, v2)
                split_to(iu + 7 + AHEAD)
                evac(ib + 3, flat(uT[:]), flat(both(ib + 3)))
                ou = U[f"o{i}"]
                split_to(iu + 10)

                def log_part(hb):
                    n = 2 * i + hb
                    act.wait_ge(z_scores, n + 1)
                    if n:
                        act.wait_ge(sp_done, n)
                    step(AC(spa[:], ps[:, 4:8, 0:3 * P], ACT.Abs))
                    step(AC(spa[:], spa[:], ACT.Exp, scale=-1.0))
                    AC(spa[:], spa[:], ACT.Ln, bias=ones[:, 0:1]).then_inc(ln_done, 1)

                def stick_weights(hb):
                    n = 2 * i + hb
                    act.wait_ge(stick_done, n + 1)
                    if n:
                        act.wait_ge(pv_done, n)
                    AC(wT[:], ps[:, 4:8, 0:3 * P], ACT.Exp).then_inc(stick_exp, 1)

                log_part(0)
                split_to(ou + 1)
                stick_weights(0)
                act.wait_ge(pv_done, 2 * i + 1)
                for j in range(2):
                    ins = AC(mixT[:, j, :].rearrange("p (t n) -> p t n", t=NT), pv_place(j), ACT.Copy)
                ins.then_inc(pv_copied, 1)
                act.wait_ge(banks_free[(ib + 5) % 2], g.freed(ib + 5))
                for j in range(KU, 2 * KU):
                    ins = AC(xh[:, mix_tile(j), :], mixT[:, j, :], ACT.Copy, scale=ogain[:, i, j:j + 1])
                ins.then_inc(conv_high, 1)
                AC(mixs[:, KU:2 * KU], mixT[:, KU:2 * KU], ACT.Square).then_inc(mix_squares, 1)
                split_to(ou + 2)
                log_part(1)
                act.wait_ge(conv_sums_copied, i + 1)
                AC(st[:, 26:28], st[:, 24:26], ACT.Sqrt, scale=1.0 / NB, bias=epst[:, 0:1]).then_inc(mix_root, 1)
                act.wait_ge(pv_copied, i + 1)
                for j in range(2):
                    AC(xh[:, mix_tile(j), :], mixT[:, j, :], ACT.Copy, scale=ogain[:, i, j:j + 1])
                AC(mixs[:, 0:2], mixT[:, 0:2], ACT.Square)
                split_to(ou + 3)
                stick_weights(1)
                act.wait_ge(pv_done, 2 * i + 2)
                for j in range(2):
                    ins = AC(xh[:, mix_tile(2 + j), :].rearrange("p (t n) -> p t n", t=NT), pv_place(j), ACT.Copy,
                             scale=ogain[:, i, 2 + j:3 + j])
                ins.then_inc(mixh_done, 1)
                for j in range(2):
                    ins = AC(mixs[:, 2 + j, :].rearrange("p (t n) -> p t n", t=NT), pv_place(j), ACT.Square)
                ins.then_inc(mix_squares, 1)
                act.wait_ge(mix_sums, 2 * i + 2)
                AC(st[:, 26:28], ps[:, 7, 0:NT], ACT.Sqrt, scale=1.0 / NB, bias=epst[:, 0:1]).then_inc(mix_root, 1)

            def ple(i):
                ub, bb = U[f"ple{i}"], B[f"ple{i}"]
                start(3 * i + 3, ub)
                for j in range(2):
                    split_to(min(ub + 2 * j + 1 + AHEAD, ub + 5))
                    b = bb + j
                    evac_scaled(b, 3 * i + 3, pg[:, j], func=ACT.Sigmoid)
                    if j == 0:
                        act.wait_ge(p_turned, i + 1)
                        AC(flat(ptTh[:]), ps[:, 4, :], ACT.Copy).then_inc(ph_done, 1)
                split_to(ub + 5)

            act.wait_ge(gains_loaded, 16 * 6)
            mix(0)
            start(2, U["ffn0"])
            dense()
            ple(0)
            act.wait_ge(router_loaded, 16)
            AC(rws[:, :, 0, :], rw[:], ACT.Copy).then_inc(router_high, 1)
            mix(1)
            start(5, U["ffn1"])
            act.wait_ge(h_normed, 1)
            AC(xnh[:], tok[:], ACT.Copy).then_inc(xn_high, 1)
            act.wait_ge(logit_shift, 1)
            AC(gw[:], gw[:], ACT.Exp).then_inc(gate_exp, 1)

            def split_gathered(n):
                act.wait_ge(gathered, g.at(gathered, n + 1))
                for j in range(KD):
                    ins = AC(xgh[:, j, :], ps[:, 6 + j // 4, (j % 4) * P:(j % 4 + 1) * P], ACT.Copy,
                             scale=gains[:, 5, j:j + 1])
                ins.then_inc(gather_high, 1)

            split_gathered(0)
            act.wait_ge(rounds_known, 1)
            rounds = act.value_load(nround[0:1, 0:1], min_val=NE, max_val=2 * NE)
            with act.Fori(0, rounds) as r:
                g.r = r

                def copy_pick():
                    act.wait_ge(pick_turned, g.at(pick_turned, 1))
                    AC(pickT[:], ps[:, 6, 0:2 * P].rearrange("p (t n) -> p t n", t=NT), ACT.Copy)\
                        .then_inc(pick_copied, 1)
                expert(copy_pick, lambda: split_gathered(1))
                for half in range(2):
                    act.wait_ge(half_used, g.at(half_used, 2 * (U["ffn1"] + UNITS_ROUND - 1 + half)))
                    AC(yh[:, half * NB:(half + 1) * NB], ps[:, 4 + half, :], ACT.Copy).then_inc(y_high, 1)
                assert g.split == U["ffn1"] + UNITS_ROUND + 2
            g.r = rounds
            g.split = U["ffn1"] + 2
            g.post = True
            ple(1)

        @block_.vector
        def _(dve):
            g = Prog()

            def step(ins):
                g.n += 1
                ins.then_inc(dve_step, 1)
                dve.wait_ge(dve_step, g.n)

            V = nc.vector

            def split_to(u):
                while g.split <= u:
                    v = g.split
                    n = unit_columns(v, g.post)
                    for half in range(2):
                        dve.wait_ge(high_done, g.at(high_done, 2 * v + half + 1))
                        c = slice(half * n // 2, (half + 1) * n // 2)
                        V.tensor_tensor(wlo[:, v % SPL, c], raw[:, v % RAW, c], whi[:, v % SPL, c].bitcast(F32),
                                        ALU.subtract).then_inc(low_done, 1)
                    g.split += 1

            def invert_root(k):
                dve.wait_ge(root_done, k + 1)
                V.reciprocal(st[:, 8:10], st[:, 2:4]).then_inc(factor_done, 1)

            def turned_low(k, half):
                dve.wait_ge(xh_done, 2 * k + half + 1)
                for j in range(half * KU, (half + 1) * KU):
                    ins = V.scalar_tensor_tensor(out=xl[:, j, :], in0=turned_place(k, j),
                                                 scalar=gains[:, k, j:j + 1], in1=xh[:, j, :].bitcast(F32),
                                                 op0=ALU.mult, op1=ALU.subtract)
                ins.then_inc(xl_done, 1)

            turned_low(0, 0)
            turned_low(0, 1)
            split_to(1)
            invert_root(0)
            split_to(U["q"] + 1)
            dve.wait_ge(tab_product, 2)
            V.tensor_copy(cbias[:].rearrange("p t h c -> p t c h"),
                          ps[:, 5, 0:NT * NC_ * NH].rearrange("p (t c h) -> p t c h", t=NT, c=NC_))\
                .then_inc(cbias_done, 1)
            dve.wait_ge(cbias_done, 1)
            split_to(U["q"] + 5)
            V.memset(xw[:, XW:XT], 0.0)
            dve.wait_ge(kc_turned, 1)
            dve.wait_ge(cmp_loaded, 16 * 5)
            for kv in range(2):
                for s in range(2):
                    q = slice(s * DH, (s + 1) * DH)
                    src = ps[q, 4 + 2 * kv:6 + 2 * kv, :].rearrange("p b n -> p (b n)")
                    src = src.rearrange("p (g c m s) -> p s m g c", g=NG, m=CS // 2, s=2)
                    for half in range(2):
                        ins = V.tensor_tensor(
                            xw[q, 0:XW].rearrange("p (v m g c) -> p v m g c", v=2, m=CB // 2, g=NG)
                            [:, kv, 8 * half:8 * half + 8],
                            src[:, s, :, :, half:half + NC_],
                            pos2[q, kv, 8 * half:8 * half + 8].unsqueeze(2).unsqueeze(3)
                            .broadcast_to([DH, 8, NG, NC_]), ALU.add)
            ins.then_inc(windows_done, 1)
            dve.wait_ge(window_high, 1)
            V.tensor_tensor(xwl[:], xw[:], xwh[:].bitcast(F32), ALU.subtract).then_inc(window_low, 1)
            split_to(U["kv_w"] + 3)
            split_to(U["cmp"] + 3 + 2)
            dve.wait_ge(hc_turned, 1)
            step(V.tensor_copy(hcT[:].rearrange("p a j n -> p (a j n)"), ps[:, 4, 0:4 * NG * NC_]))
            dve.wait_ge(rev_stored, 16)
            for half in range(2):
                for j in range(2):
                    ins = V.tensor_copy(
                        hcR[:, half, j, :].rearrange("p (g r c) -> p g r c", g=2, r=RG),
                        hcT[:, 1, j, 2 * half * NC_:(2 * half + 2) * NC_].rearrange("p (g c) -> p g c", g=2)
                        .unsqueeze(2).broadcast_to([P, 2, RG, NC_]))
            ins.then_inc(hcT_done, 1)
            split_to(U["z"] + 2)
            dve.wait_ge(kcvc_product, 1)
            V.tensor_copy(kcT[:], ps[:, 5, 0:NG * NC_]).then_inc(kcT_done, 1)
            for half in range(2):
                ins = V.tensor_tensor(
                    vcb[:, half], ps[0:8 * NC_, 6, half * DH:(half + 1) * DH].unsqueeze(1)
                    .broadcast_to([8 * NC_, 8, DH]),
                    bdiag[0:8 * NC_, :].unsqueeze(2).broadcast_to([8 * NC_, 8, DH]), ALU.mult)
            ins.then_inc(vcb_done, 1)
            dve.wait_ge(cmp_scores, 1)
            for j in range(2):
                ins = V.tensor_tensor(
                    lc[:].rearrange("p t (i j) c -> p j t i c", j=2)[:, j],
                    ps[:, 4 + j, 0:NT * 8 * NC_].rearrange("p (t i c) -> p t i c", t=NT, i=8),
                    cbias[:].rearrange("p t (i j) c -> p j t i c", j=2)[:, j], ALU.add)
            step(ins)
            lcv = lc[:].rearrange("p t h c -> p (t h) c")
            step(V.tensor_reduce(cst[:, 0, :], lcv, AX, ALU.max))
            step(V.tensor_scalar(cst[:, 0, :], cst[:, 0, :], MASKED / 16, None, ALU.max))
            V.tensor_tensor(lcv, lcv, cst[:, 0, :].unsqueeze(2).broadcast_to([P, NT * NH, NC_]), ALU.subtract)\
                .then_inc(cmp_logits, 1)
            split_to(U["z"] + 3)
            dve.wait_ge(cmp_exp, 1)
            step(V.tensor_reduce(cst[:, 1, :], lcv, AX, ALU.add))
            step(V.tensor_scalar(cst[:, 1, :], cst[:, 1, :], 1e-30, None, ALU.max))
            step(V.reciprocal(cst[:, 2, :], cst[:, 1, :]))
            step(V.tensor_tensor(cst[:, 2, :].rearrange("p (t h) -> p t h", t=NT),
                                   cst[:, 2, :].rearrange("p (t h) -> p t h", t=NT), gate[:, :, 0:NH], ALU.mult))
            dve.wait_ge(lc_turned, 1)
            V.tensor_copy(lcT[:], ps[0:8 * NC_, 4, :].rearrange("p (a n) -> p a n", n=P)).then_inc(lcT_done, 1)
            dve.wait_ge(cmp_out, 1)
            for half in range(2):
                for T in range(NT):
                    src = ps[:, [5, 6, 7, 2][half * 2 + T], :]
                    a0 = T * NH + half * 8
                    ins = V.tensor_tensor(
                        ob[:, T, half * NB:(half + 1) * NB].rearrange("p (h d) -> p h d", d=DH),
                        src.rearrange("p (h d) -> p h d", d=DH),
                        cst[:, 2, a0:a0 + 8].unsqueeze(2).broadcast_to([P, 8, DH]), ALU.mult)
            ins.then_inc(o_evac, 1)
            dve.wait_ge(o_evac, 1)
            split_to(U["z"] + 4)
            dve.wait_ge(bias_loaded, 16)

            def att(i):
                if i < 16:
                    T, half = (i // 2) % 2, (i // 4) % 2
                    grp = 2 * half + i % 2
                    nk = (T + 1) * P
                    dve.wait_ge(scores_done, i + 1)
                    if i >= 2:
                        dve.wait_ge(p_turned_all, i - 1)
                    for r in range(RG):
                        hh = grp * RG + r
                        bank = 4 + 2 * (i % 2) + r % 2
                        ins = V.tensor_tensor_reduce(
                            sg[:, i % 2, r, 0:nk], ps[:, bank, (r // 2) * S:(r // 2) * S + nk],
                            bias[:, hh, S - nk:S], 1.0, MASKED, ALU.add, ALU.max, ast_[:, i, 0, r:r + 1])
                    step(ins)
                    V.tensor_scalar(ast_[:, i, 1, :], ast_[:, i, 0, :], -SC, None, ALU.mult)\
                        .then_inc(logits_done, 1)
                if 1 <= i < 17:
                    k = i - 1
                    T = (k // 2) % 2
                    dve.wait_ge(p_turned_all, k + 1)
                    if k >= 2:
                        dve.wait_ge(pv_step, k - 1)
                    src = ps[:, 4 + 2 * (k % 2):6 + 2 * (k % 2), :].rearrange(
                        "p b (r t n) -> p (b r) t n", r=2, t=NT)
                    V.tensor_copy(pT[:, k % 2, :, 0:T + 1, :], src[:, :, 0:T + 1, :]).then_inc(pT_done, 1)
                if i >= 2 and (i - 2) % 2:
                    k = i - 2
                    T, half, br = (k // 2) % 2, (k // 4) % 2, k // 8
                    dve.wait_ge(pv_step, k + 1)
                    dve.wait_ge(exp_done, k + 1)
                    for s in (1, 0):
                        ins = V.reciprocal(grow[:, T, half * 8 + 4 * (1 - s):half * 8 + 4 * (1 - s) + 4],
                                           ast_[:, k - s, 2, :])
                    step(ins)
                    gs = grow[:, T, half * 8:half * 8 + 8]
                    step(V.tensor_tensor(gs, gs, gate[:, T, (br + 1) * NH + half * 8:(br + 1) * NH + half * 8 + 8],
                                           ALU.mult))
                    V.tensor_tensor(
                        ob[:, T, half * NB:(half + 1) * NB].rearrange("p (h d) -> p h d", d=DH),
                        ps[:, 2 + (k // 2) % 2, :].rearrange("p (h d) -> p h d", d=DH),
                        gs.unsqueeze(2).broadcast_to([P, 8, DH]), ALU.mult).then_inc(o_evac, 1)

            def z_product(n):
                br, half = n // 2, n % 2
                dve.wait_ge(z_done, n + 1)
                dve.wait_ge(o_evac, max(1, 2 * (n - 1) + 1))
                c = slice(half * NB, (half + 1) * NB)
                if br == 0:
                    V.tensor_tensor(y[:, :, c], zt[:], ob[:, :, c], ALU.mult).then_inc(z_used, 1)
                else:
                    step(V.tensor_tensor(ob[:, :, c], zt[:], ob[:, :, c], ALU.mult))
                    V.tensor_tensor(y[:, :, c], y[:, :, c], ob[:, :, c], ALU.add).then_inc(z_used, 1)
                dve.wait_ge(z_used, n + 1)

            z_product(0)
            split_to(U["z"] + 5)
            z_product(1)
            for kind, i in NSA_ORDER:
                if kind == "a":
                    att(i)
                elif kind == "y":
                    z_product(i)
                elif kind == "z" and i % 2 == 0:
                    split_to(U["z"] + i // 2 + AHEAD)
            for half in range(2):
                dve.wait_ge(yh_done, half + 1)
                V.tensor_tensor(xl[:, half * KU:(half + 1) * KU].rearrange("p k n -> p (k n)"),
                                ps[:, 4 + 2 * half:6 + 2 * half, :].rearrange("p b n -> p (b n)"),
                                xh[:, half * KU:(half + 1) * KU].rearrange("p k n -> p (k n)").bitcast(F32),
                                ALU.subtract).then_inc(yl_done, 1)
            split_to(U["nsa_out"] + 3)
            dve.wait_ge(postg_loaded, 16)
            for i in range(2):
                b = B["nsa_out"] + i
                c = slice(i * NB, (i + 1) * NB)
                split_to(U["in0"] + i)
                dve.wait_ge(banks_free[b % 2], g.freed(b))
                ins = V.tensor_tensor(ob[:, :, c], tok[:, :, c], postg[:, c].unsqueeze(1).broadcast_to([P, NT, NB]),
                                      ALU.mult)
            step(ins)
            dve.wait_ge(post_squares, 2)
            V.tensor_tensor(st[:, 4:6], st[:, 4:6], st[:, 18:20], ALU.add).then_inc(post_summed, 1)
            dve.wait_ge(post_root, 1)
            step(V.reciprocal(st[:, 10:12], st[:, 6:8]))
            for half in range(2):
                c = slice(half * NB, (half + 1) * NB)
                for T in range(NT):
                    ins = V.scalar_tensor_tensor(out=h[:, T, c], in0=ob[:, T, c], scalar=st[:, 10 + T:11 + T],
                                                 in1=h[:, T, c], op0=ALU.mult, op1=ALU.add)
                ins.then_inc(h_ready, 1)

            def dense():
                ub, bb = U["ffn0"], B["ffn0"]
                cols = dense_cols.unsqueeze(1).broadcast_to([P, 4, S])
                gate_, hidden = (x[:].rearrange("p t n -> p (t n)").rearrange("p (k n) -> p k n", n=S)
                                 for x in (gt, ht))

                def product(b):
                    return ps[:, pair(b):pair(b) + 2, :].rearrange("p b (k n) -> p (b k) n", n=S)

                def low(f):
                    dve.wait_ge(hidden_high, f + 1)
                    V.tensor_tensor(hTl[:, f * KU:(f + 1) * KU, :], hidden,
                                    hTh[:, f * KU:(f + 1) * KU, :].bitcast(F32), ALU.subtract).then_inc(hidden_low, 1)

                for f in range(NFB):
                    split_to(ub + 4 * f + 1 + AHEAD)
                    b = bb + 2 * f
                    if f == 0:
                        dve.wait_ge(factor_copied, 2)
                    dve.wait_ge(half_used, g.through(b))
                    V.tensor_tensor(gate_, product(b), cols, ALU.mult).then_inc(banks_free[b % 2], 1)
                    if f:
                        low(f - 1)
                    split_to(ub + 4 * f + 3 + AHEAD)
                    b += 1
                    dve.wait_ge(gate_made, f + 1)
                    dve.wait_ge(half_used, g.through(b))
                    if f:
                        dve.wait_ge(hidden_low, f)
                    V.tensor_tensor(hidden, product(b), gate_, ALU.mult).then_inc(banks_free[b % 2], 1)
                    dve.wait_ge(banks_free[b % 2], g.freed(b))
                    V.tensor_tensor(hidden, hidden, cols, ALU.mult).then_inc(hidden_made, 1)
                split_to(ub + 4 * NFB + 1 + AHEAD)
                low(NFB - 1)
                split_to(ub + UNITS_ROUND - 1)
                for j in range(2):
                    dve.wait_ge(half_used, 2 * (U["ple0"] - 1 + j))
                    c = slice(j * NB, (j + 1) * NB)
                    for T in range(NT):
                        ins = V.tensor_tensor(h[:, T, c], h[:, T, c], ps[:, 4 + 2 * T + j, :], ALU.add)
                    ins.then_inc(h_ready, 1)
                    if j == 0:
                        split_to(U["ple0"])

            def expert(extra):
                ub, bb = U["ffn1"], B["ffn1"]

                def turn(f):
                    dve.wait_ge(hidden_high, g.at(hidden_high, NFB + f + 1))
                    k = slice(f * KU, (f + 1) * KU)
                    V.tensor_tensor(mTl[:, k, :], ps[:, 6 + f % 2, :].rearrange("p (k n) -> p k n", k=KU),
                                    mTh[:, k, :].bitcast(F32), ALU.subtract).then_inc(hidden_low, 1)

                for f in range(NFB):
                    b = bb + 2 * f + 1
                    split_to(ub + 4 * f + 3 + AHEAD)
                    dve.wait_ge(half_used, g.through(b))
                    dve.wait_ge(banks_free[(b - 1) % 2], g.freed(b - 1))
                    V.tensor_tensor(ht[:, 0, :], gt[:, 0, :], ps[:, pair(b), :], ALU.mult)\
                        .then_inc(banks_free[b % 2], 1)
                    if f < NFB - 1:
                        split_to(ub + 4 * (f + 1) + 1 + AHEAD)
                        turn(f)
                split_to(ub + 4 * NFB + 1 + AHEAD)
                turn(NFB - 1)
                split_to(ub + 4 * NFB + 5 + AHEAD)
                extra()
                split_to(ub + UNITS_ROUND - 1 + AHEAD)

            def spread_factor(k, diagonal):
                dve.wait_ge(factor_done, k + 1)
                for T in range(NT):
                    ins = V.tensor_scalar(diagonal[:, T * P:(T + 1) * P], ident, factor(T), None, ALU.mult)
                ins.then_inc(factor_diag_done, 1)

            def mix(i):
                split_to(U[f"in{i}"])
                turned_low(3 * i + 1, 0)
                split_to(U[f"in{i}"] + 1)
                turned_low(3 * i + 1, 1)
                split_to(U[f"in{i}"] + 2)
                invert_root(3 * i + 1)
                spread_factor(3 * i + 1, factor_diag)
                ib, iu, ou = B[f"in{i}"], U[f"in{i}"], U[f"o{i}"]
                V.memset(cu[:, :, 0:2], 0.0)
                for j in range(2):
                    split_to(iu + 2 * j + 1 + AHEAD)
                    dve.wait_ge(banks_free[(ib + j) % 2], g.freed(ib + j))
                    step(V.tensor_tensor(sq[:], qk[:, j], qk[:, j], ALU.mult))
                    V.tensor_reduce(qk_ss[:, j].rearrange("p t h -> p (t h)"),
                                    sq[:].rearrange("p t (h d) -> p (t h) d", d=DH), AX, ALU.add)\
                        .then_inc(qk_squares, 1)
                    dve.wait_ge(qk_root, 2 * i + j + 1)
                    step(V.reciprocal(qk_ss[:, j], qk_ss[:, j]))
                    v = qk[:, j].rearrange("p t (h d) -> p (t h) d", d=DH)
                    V.tensor_tensor(v, v, qk_ss[:, j].rearrange("p t h -> p (t h)").unsqueeze(2)
                                    .broadcast_to([P, NT * SH, DH]), ALU.mult).then_inc(qk_normed, 1)
                split_to(iu + 5 + AHEAD)
                dve.wait_ge(qk_turned, i + 1)
                dve.wait_ge(mix_loaded, 16 * 20)
                V.tensor_scalar(qkT[:, 0].rearrange("p k n -> p (k n)"), ps[:, 4:6, :].rearrange("p b n -> p (b n)"),
                                qkg[:, i, 0:1], SC, ALU.mult, ALU.mult)
                V.tensor_scalar(qkT[:, 1].rearrange("p k n -> p (k n)"), ps[:, 6:8, :].rearrange("p b n -> p (b n)"),
                                qkg[:, i, 1:2], None, ALU.mult).then_inc(qkT_done, 1)
                dve.wait_ge(factor_copied, 2 * i + 1)
                step(V.tensor_tensor(factor_squares, factor_cols, factor_cols, ALU.mult))
                dve.wait_ge(banks_free[(ib + 3) % 2], g.freed(ib + 3))
                step(V.tensor_tensor(uT[:], uT[:], factor_squares.unsqueeze(1).broadcast_to([P, 4, S]), ALU.mult))

                def softplus(hb):
                    n = 2 * i + hb
                    dve.wait_ge(z_scores, n + 1)
                    if n:
                        dve.wait_ge(stick_done, n)
                    dve.wait_ge(ln_done, n + 1)
                    step(V.scalar_tensor_tensor(out=spb[:], in0=ps[:, 4:8, 0:3 * P], scalar=0.0, in1=spa[:],
                                                  op0=ALU.max, op1=ALU.add))
                    for c in (0, 2 * P):
                        ins = V.tensor_tensor(spb[:, :, c:c + P], spb[:, :, c:c + P],
                                              keep.unsqueeze(1).broadcast_to([P, 4, P]), ALU.mult)
                    ins.then_inc(sp_done, 1)

                split_to(iu + 10)
                softplus(0)
                split_to(iu + 11)
                b = ib + 4
                dve.wait_ge(banks_free[(ib + 3) % 2], g.freed(ib + 3))
                dve.wait_ge(half_used, g.through(b))
                V.tensor_tensor(cu[:, :, 2:S + 2],
                                ps[:, pair(b):pair(b) + 2, :].rearrange("p b (k n) -> p (b k) n", n=S),
                                uT[:], ALU.mult).then_inc(banks_free[b % 2], 1)
                dve.wait_ge(banks_free[b % 2], g.freed(b))
                for j in range(4):
                    ins = V.tensor_scalar(cv[:, j, :], cu[:, j, 0:S], convw[:, i, j, 0:1], convw[:, i, j, 3:4],
                                          ALU.mult, ALU.add)
                step(ins)
                for k in (1, 2):
                    for j in range(4):
                        ins = V.scalar_tensor_tensor(out=cv[:, j, :], in0=cu[:, j, k:k + S],
                                                     scalar=convw[:, i, j, k:k + 1], in1=cv[:, j, :],
                                                     op0=ALU.mult, op1=ALU.add)
                    step(ins)
                step(V.tensor_tensor(cv[:], cv[:], factor_cols.unsqueeze(1).broadcast_to([P, 4, S]), ALU.mult))
                split_to(ou + 1)
                b = ib + 5
                dve.wait_ge(half_used, g.through(b))
                V.tensor_tensor(mixT[:, 4:8, :],
                                ps[:, pair(b):pair(b) + 2, :].rearrange("p b (k n) -> p (b k) n", n=S),
                                cv[:], ALU.mult).then_inc(banks_free[b % 2], 1)

                def low_part(j0, j1, src, semaphore):
                    for j in range(j0, j1):
                        m = mix_tile(j)
                        ins = V.scalar_tensor_tensor(out=xl[:, m, :].rearrange("p (t n) -> p t n", t=NT), in0=src(j),
                                                     scalar=ogain[:, i, j:j + 1],
                                                     in1=xh[:, m, :].bitcast(F32).rearrange("p (t n) -> p t n", t=NT),
                                                     op0=ALU.mult, op1=ALU.subtract)
                    ins.then_inc(semaphore, 1)

                def mixed(j):
                    return mixT[:, j, :].rearrange("p (t n) -> p t n", t=NT)

                def add_part(b):
                    j = (b - B[f"o{i}"]) % 2
                    dve.wait_ge(half_used, g.through(b))
                    for T in range(NT):
                        c = slice(j * NB, (j + 1) * NB)
                        ins = V.scalar_tensor_tensor(out=h[:, T, c], in0=ps[:, pair(b) + T, :],
                                                     scalar=st[:, 28 + T:29 + T], in1=h[:, T, c], op0=ALU.mult,
                                                     op1=ALU.add)
                    ins.then_inc(banks_free[b % 2], 1)

                dve.wait_ge(conv_high, i + 1)
                low_part(KU, 2 * KU, mixed, conv_low)
                dve.wait_ge(mix_sums, 2 * i + 1)
                V.tensor_copy(st[:, 24:26], ps[:, pair(B[f"o{i}"] + 1), 0:NT]).then_inc(conv_sums_copied, 1)
                split_to(ou + 2)
                softplus(1)
                dve.wait_ge(mix_root, 2 * i + 1)
                step(V.reciprocal(st[:, 28:30], st[:, 26:28]))
                add_part(B[f"o{i}"])
                add_part(B[f"o{i}"] + 1)
                split_to(ou + 3)
                dve.wait_ge(mixh_done, i + 1)
                low_part(0, 2, mixed, mixl_done)
                dve.wait_ge(mix_squares, 2 * i + 2)
                low_part(2, 4, lambda j: pv_place(j - 2), mixl_done)
                k, nu = 3 * i + 2, U[f"ffn{i}"]
                dve.wait_ge(mix_root, 2 * i + 2)
                dve.wait_ge(banks_free[(B[f"o{i}"]) % 2], g.freed(B[f"o{i}"]))
                dve.wait_ge(banks_free[(B[f"o{i}"] + 1) % 2], g.freed(B[f"o{i}"] + 1))
                step(V.reciprocal(st[:, 28:30], st[:, 26:28]))
                for j in range(2):
                    add_part(B[f"o{i}"] + 2 + j)
                    split_to(nu + j)
                    turned_low(k, j)

            def ple(i):
                ub, bb = U[f"ple{i}"], B[f"ple{i}"]
                split_to(ub)
                turned_low(3 * i + 3, 0)
                split_to(ub + 1)
                turned_low(3 * i + 3, 1)
                split_to(ub + 2)
                invert_root(3 * i + 3)
                split_to(ub + 3)
                dve.wait_ge(ph_done, i + 1)
                V.tensor_tensor(ptTl[:].rearrange("p k n -> p (k n)"), ps[:, 4, :],
                                ptTh[:].rearrange("p k n -> p (k n)").bitcast(F32), ALU.subtract)\
                    .then_inc(pl_done, 1)
                for j in range(2):
                    split_to(min(ub + 2 * j + 1 + AHEAD, ub + 5))
                for j in range(2):
                    b = bb + 2 + j
                    if i == 0 and j == 0:
                        split_to(ub + 6)
                    dve.wait_ge(banks_free[(b - 2) % 2], g.freed(b - 2))
                    dve.wait_ge(half_used, g.through(b))
                    if i or j:
                        dve.wait_ge(h_half, 2 * i + j)
                    V.tensor_tensor(pm[:], ps[:, pair(b):pair(b) + 2, :], pg[:, j], ALU.mult)\
                        .then_inc(banks_free[b % 2], 1)
                    dve.wait_ge(banks_free[b % 2], g.freed(b))
                    c = slice(j * NB, (j + 1) * NB)
                    V.tensor_tensor(h[:, :, c], h[:, :, c], pm[:], ALU.add).then_inc(h_half, 1)
                dve.wait_ge(h_half, 2 * i + 2)

            mix(0)
            split_to(U["ffn0"] + 2)
            invert_root(2)
            spread_factor(2, dense_diag)
            dense()
            ple(0)
            dve.wait_ge(router_high, 1)
            V.tensor_tensor(rws[:, :, 1, :], rw[:], rws[:, :, 0, :].bitcast(F32), ALU.subtract)\
                .then_inc(router_low, 1)
            mix(1)
            invert_root(5)
            dve.wait_ge(factor_done, 6)
            for T in range(NT):
                ins = V.tensor_scalar(tok[:, T, :], h[:, T, :], factor(T), None, ALU.mult)
            ins.then_inc(h_normed, 1)
            dve.wait_ge(router_logits, 1)
            for T in range(NT):
                ins = V.tensor_scalar(lg[:, T], ps[:, 0, 2 * T * NE:(2 * T + 1) * NE], factor(T), None, ALU.mult)
            step(ins)
            for T in range(NT):
                ins = V.scalar_tensor_tensor(out=lg[:, T], in0=ps[:, 0, (2 * T + 1) * NE:(2 * T + 2) * NE],
                                             scalar=factor(T), in1=lg[:, T], op0=ALU.mult, op1=ALU.add)
            step(ins)
            other = lg[:].unsqueeze(2).broadcast_to([P, NT, NE, NE])
            own = lg[:].unsqueeze(3).broadcast_to([P, NT, NE, NE])
            for T in range(NT):
                V.tensor_tensor(cmpa[:, T], other[:, T], own[:, T], ALU.is_gt)
                ins = V.tensor_tensor(cmpb[:, T], other[:, T], own[:, T], ALU.is_equal)
            step(ins)
            for T in range(NT):
                ins = V.tensor_tensor(cmpb[:, T], cmpb[:, T], tril8.rearrange("p (a b) -> p a b", a=NE), ALU.mult)
            step(ins)
            step(V.tensor_tensor(cmpa[:], cmpa[:], cmpb[:], ALU.add))
            step(V.tensor_reduce(sel[:].rearrange("p t e -> p (t e)"),
                                   cmpa[:].rearrange("p t a b -> p (t a) b"), AX, ALU.add))
            V.tensor_scalar(sel[:], sel[:], 2.0, None, ALU.is_lt).then_inc(sel_done, 1)
            dve.wait_ge(sel_done, 1)
            step(V.tensor_reduce(st[:, 12:14], lg[:], AX, ALU.max))
            for T in range(NT):
                ins = V.tensor_scalar(gw[:, T], lg[:, T], st[:, 12 + T:13 + T], None, ALU.subtract)
            ins.then_inc(logit_shift, 1)
            dve.wait_ge(xn_high, 1)
            V.tensor_tensor(xnl[:], tok[:], xnh[:].bitcast(F32), ALU.subtract).then_inc(xn_low, 1)
            dve.wait_ge(slots_counted, 1)
            V.tensor_scalar(slot[:, :, 0:NE], ps[:, 1, 0:NT * NE].rearrange("p (t e) -> p t e", t=NT), 1.0, None,
                            ALU.add)
            step(V.tensor_reduce(cnt[:, NE:NE + 1], ps[:, 1, NT * NE:NT * NE + NE], AX, ALU.max))
            step(V.tensor_tensor(slot[:, :, 0:NE], slot[:, :, 0:NE], sel[:], ALU.mult))
            step(V.tensor_scalar(slot[:, :, 0:NE], slot[:, :, 0:NE], 1.0, None, ALU.subtract))
            V.tensor_scalar(slot[:, :, NE:2 * NE], slot[:, :, 0:NE], float(P), None, ALU.subtract)
            V.memset(slot[:, :, 2 * NE:2 * NE + 1], -1.0)
            step(V.tensor_scalar(cnt[:, NE + 1:NE + 2], cnt[:, NE:NE + 1], float(P), float(NE), ALU.is_gt, ALU.mult))
            step(V.tensor_scalar(cnt[:, NE + 2:NE + 3], cnt[:, NE + 1:NE + 2], float(NE), None, ALU.add))
            V.tensor_copy(nround[:], cnt[0:1, NE + 2:NE + 3]).then_inc(rounds_known, 1)

            def make_pick(col, n):
                if n:
                    dve.wait_ge(pick_turned, g.at(pick_turned, n))
                for T in range(NT):
                    ins = V.tensor_scalar(pick[:, T, :], iota, slot[:, T, col], None, ALU.is_equal)
                ins.then_inc(pick_done, 1)

            def split_gathered(n):
                dve.wait_ge(gather_high, g.at(gather_high, n + 1))
                for j in range(KD):
                    ins = V.scalar_tensor_tensor(
                        out=xgl[:, j, :], in0=ps[:, 6 + j // 4, (j % 4) * P:(j % 4 + 1) * P],
                        scalar=gains[:, 5, j:j + 1], in1=xgh[:, j, :].bitcast(F32), op0=ALU.mult,
                        op1=ALU.subtract)
                ins.then_inc(gather_low, 1)

            dve.wait_ge(rounds_known, 1)
            make_pick(slice(0, 1), 0)
            dve.wait_ge(gate_exp, 1)
            step(V.tensor_tensor(gw[:], gw[:], sel[:], ALU.mult))
            step(V.tensor_reduce(st[:, 14:16], gw[:], AX, ALU.add))
            step(V.reciprocal(st[:, 16:18], st[:, 14:16]))
            for T in range(NT):
                ins = V.tensor_scalar(gw[:, T], gw[:, T], st[:, 16 + T:17 + T], None, ALU.mult)
            step(ins)
            V.memset(st[:, 20:21], 0.0).then_inc(round_done, 1)
            split_gathered(0)
            rounds = dve.value_load(nround[0:1, 0:1], min_val=NE, max_val=2 * NE)
            with dve.Fori(0, rounds) as r:
                g.r = r
                e = r % NE

                def next_tokens():
                    make_pick(bass.ds(r + 1, 1), 1)
                    split_gathered(1)
                expert(next_tokens)
                for half in range(2):
                    c = slice(half * NB, (half + 1) * NB)
                    dve.wait_ge(y_high, g.at(y_high, half + 1))
                    V.tensor_tensor(yl[:, c], ps[:, 4 + half, :], yh[:, c].bitcast(F32), ALU.subtract)\
                        .then_inc(y_low, 1)
                for half in range(2):
                    c = slice(half * NB, (half + 1) * NB)
                    dve.wait_ge(scatter_done, g.at(scatter_done, half + 1))
                    for T in range(NT):
                        ins = V.scalar_tensor_tensor(out=h[:, T, c], in0=ps[:, (6 if T == 0 else 4) + half, :],
                                                     scalar=gw[:, T, bass.ds(e, 1)], in1=h[:, T, c], op0=ALU.mult,
                                                     op1=ALU.add)
                ins.then_inc(round_done, 1)
                dve.wait_ge(round_done, g.at(round_done, 2))
            g.r = rounds
            g.split = U["ffn1"] + 2
            g.post = True
            ple(1)

        @block_.tensor
        def _(pe):
            g = Prog()
            mm = nc.tensor.matmul

            def turn(dst, src, idn=None):
                return nc.tensor.transpose(dst, src, ident if idn is None else idn)

            def split_view(u, nk, n):
                s = u % SPL
                return (whi[:, s, 0:nk * n].rearrange("p (k n) -> p k n", k=nk),
                        wlo[:, s, 0:nk * n].rearrange("p (k n) -> p k n", k=nk))

            def products(u, nk, n, hi, lo, k0, outs, first, last, middle=None, halves=(0, 1)):
                wh, wl = split_view(u, nk, n)
                for half in halves:
                    if half and middle:
                        middle()
                    ks = range(half * nk // 2, (half + 1) * nk // 2)
                    pe.wait_ge(high_done, g.at(high_done, 2 * u + half + 1))
                    for k in ks:
                        for T, o in enumerate(outs):
                            mm(o, hi(k0 + k, T), wh[:, k, :], start=first and k == 0, stop=False)
                            mm(o, lo(k0 + k, T), wh[:, k, :], start=False, stop=False)
                    pe.wait_ge(low_done, g.at(low_done, 2 * u + half + 1))
                    for k in ks:
                        for T, o in enumerate(outs):
                            ins = mm(o, hi(k0 + k, T), wl[:, k, :], start=False, stop=last and k == nk - 1)
                    ins.then_inc(half_used, 1)

            def tile_of(x):
                return lambda k, T: x[:, k, T * P:(T + 1) * P]

            def block(u, b, hi, lo, kt=KD, n=NB, nt=NT, units=None, norm=None, between=None):
                bank = pair(b)
                outs = [ps[:, bank + T, 0:n] for T in range(nt)]
                start_block(b)
                ku = units or KU
                nu = -(-kt // ku)
                for i in range(nu):
                    if norm is not None:
                        pe.wait_ge(xl_done, 2 * norm + i + 1)
                    if i and between:
                        between()
                    products(u + i, min(ku, kt - i * ku), n, hi, lo, i * ku, outs, i == 0, i == nu - 1,
                             (lambda: turn_rows(norm, 1)) if norm and i == 0 else None)

            def start_block(b):
                back = b - 2 if b - 2 not in z_blocks else B["z"] - (2 if (b - B["z"]) % 2 == 0 else 1)
                if back >= 0:
                    pe.wait_ge(banks_free[back % 2], g.freed(back))

            def turn_all(src):
                for j in range(KD):
                    for T in range(NT):
                        ins = turn(ps[:, 4 + j // 2, (j % 2) * S + T * P:(j % 2) * S + (T + 1) * P],
                                   src[:, T, j * P:(j + 1) * P])
                return ins

            def turn_rows(k, half):
                if k == 0 and half == 0:
                    pe.wait_ge(x_loaded, 16)
                elif k == 1:
                    pe.wait_ge(h_ready, half + 1)
                elif k in (2, 5):
                    b = B[f"o{k // 3}"] + 2 + half
                    pe.wait_ge(banks_free[b % 2], g.freed(b))
                elif k == 3:
                    pe.wait_ge(h_ready, 2 + half + 1)
                elif k == 4:
                    pe.wait_ge(h_half, half + 1)
                elif k == 6 and half == 0:
                    pe.wait_ge(round_done, g.at(round_done, 1))
                for j in range(half * KU, (half + 1) * KU):
                    for T in range(NT):
                        ins = turn(turned_place(k, j)[:, T * P:(T + 1) * P], h[:, T, j * P:(j + 1) * P])
                ins.then_inc(h_turned, 1)

            pe.wait_ge(ident_loaded, 16)
            turn_rows(0, 0)
            turn_rows(0, 1)
            X = (tile_of(xh), tile_of(xl))
            block(U["kv_c"], B["kv_c"], *X, norm=0)
            pe.wait_ge(oh_loaded, 32)
            pe.wait_ge(table_one, 1)
            mm(ps[0:NH, 4, 0:LREV], tabx[:], oh[:, 512:512 + LREV], start=True, stop=True)\
                .then_inc(tab_product, 1)
            for T in range(NT):
                for c in range(NC_):
                    i0 = 256 + P * T - CS * c - (CB - 1)
                    o = (T * NC_ + c) * NH
                    ins = mm(ps[:, 5, o:o + NH], oh[:, i0:i0 + P], tabx[:], start=True, stop=True)
            ins.then_inc(tab_product, 1)
            block(U["q"], B["q"], *X)
            pe.wait_ge(banks_free[(B["kv_c"]) % 2], g.freed(B["kv_c"]))
            pe.wait_ge(rev_ready, 1)
            pe.wait_ge(cbias_done, 1)
            pe.wait_ge(con_loaded, 16)
            for a in range(2 * NG):
                for T in range(NT):
                    ins = turn(ps[:, 4 + a // 2, (a % 2) * S + T * P:(a % 2) * S + (T + 1) * P],
                               kc2[:, T, a].rearrange("p s d -> p (s d)"))
            ins.then_inc(kc_turned, 1)
            block(U["q"] + 2, B["q"] + 1, *X)
            block(U["kv_s"], B["kv_s"], *X)
            pe.wait_ge(banks_free[(B["q"]) % 2], g.freed(B["q"]))
            pe.wait_ge(banks_free[(B["q"] + 1) % 2], g.freed(B["q"] + 1))
            pe.wait_ge(windows_done, 1)
            turn_all(tok).then_inc(q_turned, 1)
            block(U["kv_w"], B["kv_w"], *X)
            block(U["gate"], B["gate"], *X, n=3 * NH, units=KD)
            pe.wait_ge(banks_free[(B["kv_s"]) % 2], g.freed(B["kv_s"]))
            pe.wait_ge(banks_free[(B["kv_w"]) % 2], g.freed(B["kv_w"]))
            pe.wait_ge(qT_done, 1)
            for i in range(2):
                for a in range(NG):
                    for T in range(NT):
                        ins = turn(ps[:, 4 + 2 * i + a // 2, (a % 2) * S + T * P:(a % 2) * S + (T + 1) * P],
                                   kd[:, i, T, a].rearrange("p s d -> p (s d)"))
            ins.then_inc(k_turned, 1)
            pe.wait_ge(window_low, 1)
            for kv in range(2):
                def window(x, kv=kv):
                    return lambda k, T: x[:, (kv * CB // 2 + k) * NG * NC_:(kv * CB // 2 + k) * NG * NC_ + P]
                block(U["cmp"] + 2 * kv, B["cmp"] + kv, window(xwh), window(xwl), kt=CB // 2, n=HC, nt=1, units=8)
            pe.wait_ge(banks_free[(B["cmp"]) % 2], g.freed(B["cmp"]))
            pe.wait_ge(banks_free[(B["cmp"] + 1) % 2], g.freed(B["cmp"] + 1))
            pe.wait_ge(kT_done, 1)
            for kv in range(2):
                for j in range(2):
                    o = (kv * 2 + j) * NG * NC_
                    ins = turn(ps[:, 4, o:o + NG * NC_], hc[:, kv, j * P:(j + 1) * P],
                               ident[0:NG * NC_, 0:NG * NC_])
            ins.then_inc(hc_turned, 1)

            def z_half(i):
                if i % 4 == 0 and i:
                    pe.wait_ge(z_done, i // 4)
                u = i // 2
                products(U["z"] + u, KU, NB, *X, (u % 2) * KU, [ps[:, T, :] for T in range(NT)], u % 2 == 0,
                         u % 2 == 1, halves=(i % 2,))

            z_half(0)
            pe.wait_ge(hcT_done, 1)
            for j in range(2):
                mm(ps[:, 5, 0:NG * NC_], w2k[:, j].rearrange("p s d -> p (s d)"), hcT[:, 0, j, :],
                   start=j == 0, stop=j == 1)
            for half in range(2):
                for j in range(2):
                    ins = mm(ps[0:8 * NC_, 6, half * DH:(half + 1) * DH], hcR[:, half, j, :], w2v[:, j, :],
                             start=j == 0, stop=j == 1)
            ins.then_inc(kcvc_product, 1)
            pe.wait_ge(kcT_done, 1)
            for T in range(NT):
                for hh in range(NH):
                    q = slice((hh % 2) * DH, (hh % 2 + 1) * DH)
                    o = (T * 8 + hh // 2) * NC_
                    ins = mm(ps[:, 4 + hh % 2, o:o + NC_], qT[q, hh // 2, T * P:(T + 1) * P],
                             kcT[q, (hh // RG) * NC_:(hh // RG + 1) * NC_], start=True, stop=True)
            ins.then_inc(cmp_scores, 1)
            for i in (1, 2, 3):
                z_half(i)
            pe.wait_ge(cmp_exp, 1)
            for half in range(2):
                for T in range(NT):
                    a = half * 2 + T
                    ins = turn(ps[0:8 * NC_, 4, a * P:(a + 1) * P],
                               lc[:, T, half * 8:half * 8 + 8, :].rearrange("p h c -> p (h c)"))
            ins.then_inc(lc_turned, 1)
            z_half(4)
            pe.wait_ge(lcT_done, 1)
            pe.wait_ge(vcb_done, 1)
            for a in range(4):
                ins = mm(ps[:, [5, 6, 7, 2][a], :], lcT[:, a, :], vcb[:, a // 2].rearrange("p h d -> p (h d)"),
                         start=True, stop=True)
            ins.then_inc(cmp_out, 1)
            for i in (5, 6, 7):
                z_half(i)

            def att(i):
                if i >= 2:
                    k = i - 2
                    T, half, br = (k // 2) % 2, (k // 4) % 2, k // 8
                    grp = 2 * half + k % 2
                    pe.wait_ge(pT_done, k + 1)
                    if k % 2 == 0:
                        pe.wait_ge(o_evac, max(1, k // 2))
                    for r in range(RG):
                        o = ps[:, 2 + (k // 2) % 2, (k % 2) * RG * DH + r * DH:(k % 2) * RG * DH + (r + 1) * DH]
                        rr = (r % 2) * 2 + r // 2
                        for kt in range(T + 1):
                            ins = mm(o, pT[:, k % 2, rr, kt, :], vs[:, br, kt, grp * DH:(grp + 1) * DH],
                                     start=kt == 0, stop=kt == T)
                    ins.then_inc(pv_step, 1)
                if i < 16:
                    T, half, br = (i // 2) % 2, (i // 4) % 2, i // 8
                    grp = 2 * half + i % 2
                    nk = (T + 1) * P
                    if i >= 2:
                        pe.wait_ge(pT_done, i - 1)
                    else:
                        pe.wait_ge(o_evac, 1)
                    for r in range(RG):
                        hh = grp * RG + r
                        q = slice((hh % 2) * DH, (hh % 2 + 1) * DH)
                        ins = mm(ps[:, 4 + 2 * (i % 2) + r % 2, (r // 2) * S:(r // 2) * S + nk],
                                 qT[q, hh // 2, T * P:(T + 1) * P], kT[q, br, grp, 0:nk], start=True, stop=True)
                    ins.then_inc(scores_done, 1)
                if 1 <= i < 17:
                    k = i - 1
                    T = (k // 2) % 2
                    pe.wait_ge(exp_done, k + 1)
                    for r in range(RG):
                        for kt in range(T + 1):
                            c = (r // 2) * S + kt * P
                            ins = turn(ps[:, 4 + 2 * (k % 2) + r % 2, c:c + P], sg[:, k % 2, r, kt * P:(kt + 1) * P])
                    ins.then_inc(p_turned_all, 1)

            for kind, i in NSA_ORDER:
                if kind == "a":
                    att(i)
                elif kind == "z":
                    z_half(i)
            def turn_y(half):
                pe.wait_ge(z_used, 5 + half)
                for j in range(half * KU, (half + 1) * KU):
                    for T in range(NT):
                        ins = turn(turned_place(0, j)[:, T * P:(T + 1) * P], y[:, T, j * P:(j + 1) * P])
                ins.then_inc(y_turned, 1)

            turn_y(0)
            pe.wait_ge(z_done, 6)
            for i in range(2):
                b = B["nsa_out"] + i
                outs = [ps[:, pair(b) + T, :] for T in range(NT)]
                if i == 0:
                    pe.wait_ge(o_evac, 9)
                for k in range(2):
                    if i == 0:
                        pe.wait_ge(yl_done, k + 1)
                    products(U["nsa_out"] + 2 * i + k, KU, NB, *X, k * KU, outs, k == 0, k == 1,
                             (lambda: turn_y(1)) if i == 0 and k == 0 else None)

            def unit_T(u, b, v, norm=None):
                if v == 0:
                    start_block(b)
                if norm is not None:
                    pe.wait_ge(xl_done, 2 * norm + v + 1)
                wh, wl = split_view(u, KU, NB)
                for half in range(2):
                    if norm is not None and v == 0 and half:
                        turn_rows(norm, 1)
                    ks = range(half * KU // 2, (half + 1) * KU // 2)
                    pe.wait_ge(high_done, g.at(high_done, 2 * u + half + 1))
                    for k in ks:
                        kk = v * KU + k
                        for c in range(4):
                            o = ps[:, pair(b) + c // 2, (c % 2) * S:(c % 2 + 1) * S]
                            w_ = wh[:, k, c * P:(c + 1) * P]
                            mm(o, w_, xh[:, kk, :], start=kk == 0 and c % 2 == 0, stop=False, skip_group_check=True)
                            mm(o, w_, xl[:, kk, :], start=False, stop=False, skip_group_check=True)
                    pe.wait_ge(low_done, g.at(low_done, 2 * u + half + 1))
                    for k in ks:
                        kk = v * KU + k
                        for c in range(4):
                            o = ps[:, pair(b) + c // 2, (c % 2) * S:(c % 2 + 1) * S]
                            ins = mm(o, wl[:, k, c * P:(c + 1) * P], xh[:, kk, :], start=False,
                                     stop=kk == KD - 1, skip_group_check=True)
                    ins.then_inc(half_used, 1)

            def dense():
                ub, bb = U["ffn0"], B["ffn0"]
                for b in range(2 * NFB):
                    for v in range(2):
                        unit_T(ub + 2 * b + v, bb + b, v, norm=2 if b == 0 else None)
                    if b == 0:
                        pe.wait_ge(factor_diag_done, 2)
                        mm(ps[:, 4, 0:S], ones, dense_diag, start=True, stop=True).then_inc(factor_spread, 1)
                u, nk = ub + 4 * NFB, FF // P
                pe.wait_ge(factor_copied, 2)
                for k0 in range(0, nk, KU):
                    pe.wait_ge(hidden_low, k0 // KU + 1)
                    for half in range(2):
                        last = k0 == nk - KU and half == 1
                        products(u, KU, NB, tile_of(hTh), tile_of(hTl), k0,
                                 [ps[:, 4 + 2 * T + half, :] for T in range(NT)], k0 == 0, k0 == nk - KU,
                                 (lambda: turn_rows(3, 0)) if last else None)
                        u += 1

            def expert(x, hx, first_extra, extra):
                ub, bb = U["ffn1"], B["ffn1"]

                def turn_hidden(f):
                    pe.wait_ge(banks_free[(bb + 2 * f + 1) % 2], g.freed(bb + 2 * f + 1))
                    if f >= 2:
                        pe.wait_ge(hidden_low, g.at(hidden_low, NFB + f - 1))
                    elif f == 0:
                        pe.wait_ge(pick_copied, g.at(pick_copied, 1))
                    for k in range(KU):
                        ins = turn(ps[:, 6 + f % 2, k * P:(k + 1) * P], ht[:, 0, k * P:(k + 1) * P])
                    ins.then_inc(hidden_turned, 1)

                for f in range(NFB):
                    block(ub + 4 * f, bb + 2 * f, *x, nt=1)
                    if f:
                        turn_hidden(f - 1)
                    else:
                        first_extra()
                    block(ub + 4 * f + 2, bb + 2 * f + 1, *x, nt=1)
                u, nk = ub + 4 * NFB, FF // P
                for k0 in range(0, nk, KU):
                    if k0 == 0:
                        pe.wait_ge(hidden_low, g.at(hidden_low, 2 * NFB - 1))
                    if k0 == KU:
                        turn_hidden(NFB - 1)
                    if k0 == 3 * KU:
                        extra()
                    if k0 == nk - KU:
                        pe.wait_ge(hidden_low, g.at(hidden_low, 2 * NFB))
                    for half in range(2):
                        products(u, KU, NB, *hx, k0, [ps[:, 4 + half, :]], k0 == 0, k0 == nk - KU)
                        u += 1

            def mix(i):
                turn_rows(3 * i + 1, 0)
                ib, iu = B[f"in{i}"], U[f"in{i}"]
                for j in range(3):
                    block(iu + 2 * j, ib + j, *X, norm=3 * i + 1 if j == 0 else None)
                    if j == 0:
                        pe.wait_ge(factor_diag_done, 2 * i + 1)
                        mm(ps[:, 4, 0:S], ones, factor_diag, start=True, stop=True).then_inc(factor_spread, 1)
                pe.wait_ge(qk_normed, 2 * i + 2)
                pe.wait_ge(factor_copied, 2 * i + 1)
                for j in range(2):
                    for a in range(4):
                        for T in range(NT):
                            ins = turn(ps[:, 4 + 2 * j + a // 2, (a % 2) * S + T * P:(a % 2) * S + (T + 1) * P],
                                       qk[:, j, T, a * P:(a + 1) * P])
                ins.then_inc(qk_turned, 1)

                def scores(hb):
                    if hb:
                        pe.wait_ge(pv_copied, i + 1)
                    for a in range(4):
                        hh = hb * 4 + a
                        q = slice((hh % 2) * DH, (hh % 2 + 1) * DH)
                        mm(ps[:, 4 + a, 0:S], qkT[q, 1, hh // 2, 0:P], qkT[q, 0, hh // 2, :], start=True,
                           stop=False, skip_group_check=True)
                        ins = mm(ps[:, 4 + a, S:S + P], qkT[q, 1, hh // 2, P:S], qkT[q, 0, hh // 2, P:S],
                                 start=False, stop=False, skip_group_check=True)
                    ins.then_inc(z_scores, 1)

                def stick(hb):
                    pe.wait_ge(sp_done, 2 * i + hb + 1)
                    for a in range(4):
                        for o, w_, x in (((0, S), ntri, (0, S)), ((S, S + P), ntri, (S, S + P)),
                                         ((P, S), nones, (S, S + P)), ):
                            mm(ps[:, 4 + a, o[0]:o[1]], w_, spb[:, a, x[0]:x[1]], start=False, stop=False,
                               skip_group_check=True)
                        for c in (0, S):
                            ins = mm(ps[:, 4 + a, c:c + P], ident, negm, start=False, stop=c == S,
                                     skip_group_check=True)
                    ins.then_inc(stick_done, 1)

                def pv(hb):
                    pe.wait_ge(stick_exp, 2 * i + hb + 1)
                    for a in range(4):
                        hh = hb * 4 + a
                        q = slice((hh % 2) * DH, (hh % 2 + 1) * DH)
                        o = [ps[q, 4 + 2 * (a // 2) + T, 3 * P:4 * P] for T in range(NT)]
                        v_ = [v2[:, T, hh * DH:(hh + 1) * DH] for T in range(NT)]
                        mm(o[0], v_[0], wT[:, a, 0:P], start=True, stop=True, skip_group_check=True)
                        mm(o[1], v_[0], wT[:, a, P:S], start=True, stop=False, skip_group_check=True)
                        ins = mm(o[1], v_[1], wT[:, a, S:S + P], start=False, stop=True, skip_group_check=True)
                    ins.then_inc(pv_done, 1)

                def sums(bank, j0):
                    for T in range(NT):
                        for j in range(j0, j0 + KU):
                            ins = mm(ps[:, bank, T:T + 1], mixs[:, j, T * P:(T + 1) * P], ones[:, 0:1],
                                     start=j == j0, stop=j == j0 + KU - 1)
                    ins.then_inc(mix_sums, 1)

                def project(j):
                    b = B[f"o{i}"] + j
                    start_block(b)
                    products(U[f"o{i}"] + j, KU, NB, *X, 0 if j < 2 else KU,
                             [ps[:, pair(b) + T, :] for T in range(NT)], True, True)

                unit_T(iu + 6, ib + 3, 0)
                unit_T(iu + 7, ib + 3, 1)
                pe.wait_ge(qkT_done, i + 1)
                scores(0)
                unit_T(iu + 8, ib + 4, 0)
                unit_T(iu + 9, ib + 4, 1)
                unit_T(iu + 10, ib + 5, 0)
                stick(0)
                unit_T(iu + 11, ib + 5, 1)
                pv(0)
                scores(1)
                pe.wait_ge(mix_squares, 2 * i + 1)
                sums(pair(B[f"o{i}"] + 1), KU)
                pe.wait_ge(conv_low, i + 1)
                project(0)
                pe.wait_ge(conv_sums_copied, i + 1)
                project(1)
                stick(1)
                pv(1)
                pe.wait_ge(mix_squares, 2 * i + 2)
                pe.wait_ge(mixl_done, 2 * i + 2)
                sums(7, 0)
                project(2)
                turn_rows(3 * i + 2, 0)
                project(3)

            def ple(i):
                ub, bb = U[f"ple{i}"], B[f"ple{i}"]
                if i:
                    turn_rows(6, 0)
                block(ub, bb, *X, norm=3 * i + 3)
                pe.wait_ge(p_loaded, 16 * (i + 1))
                for k in range(2):
                    for T in range(NT):
                        ins = turn(ps[:, 4, k * S + T * P:k * S + (T + 1) * P], pt_in[:, T, k * P:(k + 1) * P])
                ins.then_inc(p_turned, 1)
                block(ub + 2, bb + 1, *X)
                pe.wait_ge(pl_done, i + 1)
                for j in range(2):
                    block(ub + 4 + j, bb + 2 + j, tile_of(ptTh), tile_of(ptTl), kt=2)

            mix(0)
            dense()
            ple(0)
            mix(1)
            turn_rows(5, 1)
            pe.wait_ge(router_low, 1)
            pe.wait_ge(banks_free[(B["o1"] + 2) % 2], g.freed(B["o1"] + 2))
            pe.wait_ge(banks_free[(B["o1"] + 3) % 2], g.freed(B["o1"] + 3))
            for half in range(2):
                pe.wait_ge(xl_done, 11 + half)
                for k in range(half * KU, (half + 1) * KU):
                    for T in range(NT):
                        a, b = xh[:, k, T * P:(T + 1) * P], xl[:, k, T * P:(T + 1) * P]
                        mm(ps[:, 0, 2 * T * NE:(2 * T + 2) * NE], a, rws[:, k].rearrange("p a e -> p (a e)"),
                           start=k == 0 and T == 0, stop=False, skip_group_check=True)
                        ins = mm(ps[:, 0, 2 * T * NE:(2 * T + 1) * NE], b, rws[:, k, 0, :], start=False,
                                 stop=k == KD - 1, skip_group_check=True)
            ins.then_inc(router_logits, 1)
            pe.wait_ge(sel_done, 1)
            mm(ps[:, 1, 0:NE], stri, sel[:, 0, :], start=True, stop=True)
            mm(ps[:, 1, NE:2 * NE], stri, sel[:, 1, :], start=True, stop=False)
            mm(ps[:, 1, NE:2 * NE], ones, sel[:, 0, :], start=False, stop=True)
            mm(ps[:, 1, 2 * NE:3 * NE], ones, sel[:, 0, :], start=True, stop=False)
            mm(ps[:, 1, 2 * NE:3 * NE], ones, sel[:, 1, :], start=False, stop=True).then_inc(slots_counted, 1)

            def gather(n):
                pe.wait_ge(pick_done, g.at(pick_done, n + 1))
                if n:
                    pe.wait_ge(hidden_low, g.at(hidden_low, 2 * NFB))
                else:
                    pe.wait_ge(xn_low, 1)
                for j in range(KD):
                    o = ps[:, 6 + j // 4, (j % 4) * P:(j % 4 + 1) * P]
                    for T in range(NT):
                        mm(o, xnh[:, T, j * P:(j + 1) * P], pick[:, T, :], start=T == 0, stop=False)
                        ins = mm(o, xnl[:, T, j * P:(j + 1) * P], pick[:, T, :], start=False, stop=T == 1)
                ins.then_inc(gathered, 1)

            gather(0)
            pe.wait_ge(rounds_known, 1)
            rounds = pe.value_load(nround[0:1, 0:1], min_val=NE, max_val=2 * NE)
            G = (lambda k, T: xgh[:, k, :], lambda k, T: xgl[:, k, :])
            M = (lambda k, T: mTh[:, k, :], lambda k, T: mTl[:, k, :])
            with pe.Fori(0, rounds) as r:
                g.r = r
                pe.wait_ge(gather_low, g.at(gather_low, 1))

                def turn_pick():
                    pe.wait_ge(round_done, g.at(round_done, 1))
                    for T in range(NT):
                        ins = turn(ps[:, 6, T * P:(T + 1) * P], pick[:, T, :].bitcast(F32))
                    ins.then_inc(pick_turned, 1)
                expert(G, M, turn_pick, lambda: gather(1))
                pe.wait_ge(gather_low, g.at(gather_low, 2))
                for half in range(2):
                    pe.wait_ge(y_low, g.at(y_low, half + 1))
                    c = slice(half * NB, (half + 1) * NB)
                    for T in range(NT):
                        o = ps[:, (6 if T == 0 else 4) + half, :]
                        mm(o, pickT[:, T, :], yh[:, c], start=True, stop=False)
                        ins = mm(o, pickT[:, T, :], yl[:, c], start=False, stop=True)
                    ins.then_inc(scatter_done, 1)
            g.r = rounds
            g.post = True
            ple(1)


NSA_ORDER = []
for _slot in range(18):
    NSA_ORDER.append(("a", _slot))
    if _slot % 4 == 1 and _slot > 1:
        NSA_ORDER.append(("y", 2 + (_slot - 5) // 4))
    if _slot < 16:
        NSA_ORDER.append(("z", 8 + _slot))
        if _slot % 4 == 3:
            NSA_ORDER.append(("s", 2 + _slot // 4))


def square_constants():
    i = np.arange(P)
    r, c = i[:, None], i[None, :]
    parts = [r == c, -1.0 * (r >= c), -np.ones((P, P)), np.where(r >= c, -1e30, 0.0), r < c, r < c,
             np.ones((P, P)), np.broadcast_to(c, (P, P))]
    e = np.arange(NE)
    tril = np.broadcast_to((e[None, :] < e[:, None]).reshape(1, 64), (P, 64))
    diag = (r // NC_ == e[None, :]) & (r < 8 * NC_)
    return np.concatenate([np.asarray(x, np.float32) for x in parts + [tril, diag]], axis=1)


def onehot_constants():
    d = np.concatenate([np.arange(512) - 256, 255 - np.arange(LREV)])
    n = np.maximum(d, 0)
    ex = NBUCK // 2
    big = ex + (np.log(np.maximum(n, 1).astype(np.float32) / ex) / np.log(MAXD / ex) * (NBUCK - ex)).astype(np.int32)
    bucket = np.where(n < ex, n, np.minimum(big, NBUCK - 1))
    out = np.zeros((NBUCK + 1, d.size), np.float32)
    out[bucket, np.arange(d.size)] = np.where(d >= 0, 1.0 / SC, 0.0)
    out[NBUCK] = np.where(d >= 0, 0.0, MASKED)
    return out


_INS = ["x", "pre_norm_gain", "post_norm_gain", "rel_bias_table", "nsa_w_in", "nsa_w_out", "nsa_cmp_k_pos",
        "nsa_cmp_k_w1", "nsa_cmp_k_w2", "nsa_cmp_v_pos", "nsa_cmp_v_w1", "nsa_cmp_v_w2", "p_2", "mix_norm_g_2",
        "w_in_2", "q_norm_g_2", "k_norm_g_2", "conv_w_2", "conv_b_2", "attn_out_g_2", "conv_out_g_2", "w_o_2",
        "ffn_norm_g_2", "dense_w1_2", "dense_w3_2", "dense_w2_2", "router_w_2", "moe_w1_2", "moe_w3_2",
        "moe_w2_2", "ple_norm_g_2", "ple_gate_w_2", "ple_proj_w_2"]


def kernel(**inputs):
    import concourse.bacc as _bacc
    from concourse.bass_utils import run_bass_kernel_spmd as _run

    nc = _bacc.Bacc("TRN2", target_bir_lowering=False, num_devices=1)
    arrays, t = {}, {}
    given = {name: np.ascontiguousarray(inputs[name]) for name in _INS}
    given["c_square"] = square_constants()
    given["c_onehot"] = onehot_constants()
    for name, a in given.items():
        arrays[f"in_{name}_dram"] = a
        t[name] = nc.dram_tensor(f"in_{name}_dram", a.shape, mybir.dt.from_np(a.dtype), kind="ExternalInput").ap()
    out = nc.dram_tensor("out_0_dram", (1, S, D), F32, kind="ExternalOutput").ap()
    build(nc, t, out)
    r = _run(nc, [arrays], core_ids=[0])
    return r.results[0]["out_0_dram"]
```
